# Optimizing a Trainium2 kernel written in Bass

```python
import jax, jax.numpy as jnp
from jax import lax
import numpy as np
import math

D_MODEL = 1024
BATCH = 1
SEQ = 256
DEPTH = 2

HEAD_DIM = 64
ATT_HEADS = D_MODEL // 128
ATT_WIDTH = ATT_HEADS * HEAD_DIM
DILATED_CONFIGS = ((128, 1), (512, 4), (2048, 16))
BLOCK = 128
ROPE_THETA = 10000.0
RWKV_HEAD = 64
RWKV_HEADS = D_MODEL // 128
RWKV_WIDTH = RWKV_HEADS * RWKV_HEAD
DECAY_LORA = 64
AAA_LORA = 64
GATE_LORA = 128
RWKV_COLS = 3 * RWKV_WIDTH + DECAY_LORA + AAA_LORA + GATE_LORA
GMLP_CHUNK = 128
GMLP_GROUPS = 8
GMLP_WIDTH = D_MODEL // 2
GMLP_GROUP_DIM = GMLP_WIDTH // GMLP_GROUPS
N_BRANCH = 3
IN_COLS = 3 * ATT_WIDTH + RWKV_COLS + 2 * GMLP_WIDTH + N_BRANCH * D_MODEL
D_FF = 2816
CONV_WIDTH = 3
RMS_EPS = 1e-6
LN_EPS = 1e-5
GN_EPS = 64e-5


def rms_norm(x, g):
    xf = x.astype(jnp.float32)
    y = xf * lax.rsqrt(jnp.mean(xf * xf, axis=-1, keepdims=True) + RMS_EPS)
    return (y * g).astype(x.dtype)

def layer_norm(x, g, b, eps):
    xf = x.astype(jnp.float32)
    mu = jnp.mean(xf, axis=-1, keepdims=True)
    var = jnp.mean(jnp.square(xf - mu), axis=-1, keepdims=True)
    return (xf - mu) * lax.rsqrt(var + eps) * g + b

def modulate(h, shift, scale):
    return h * (1.0 + scale[:, None, :]) + shift[:, None, :]

def rope_tables(seq_len):
    inv = 1.0 / (ROPE_THETA ** (jnp.arange(0, HEAD_DIM, 2, dtype=jnp.float32) / HEAD_DIM))
    ang = jnp.arange(seq_len, dtype=jnp.float32)[:, None] * inv[None, :]
    return jnp.cos(ang), jnp.sin(ang)

def apply_rope(t, cos, sin):
    t1, t2 = jnp.split(t.astype(jnp.float32), 2, axis=-1)
    c = cos[None, :, None, :]
    s = sin[None, :, None, :]
    return jnp.concatenate([t1 * c - t2 * s, t2 * c + t1 * s], axis=-1)

def dilated_window_attention(q, k, v, window, dilation):
    B, S, H, Dh = q.shape
    span = window // dilation
    L = -(-S // (dilation * BLOCK)) * BLOCK
    pad = L * dilation - S
    nb = L // BLOCK

    def to_blocks(t):
        t = jnp.pad(t, ((0, 0), (0, pad), (0, 0), (0, 0)))
        t = t.reshape(B, L, dilation, H, Dh).transpose(0, 2, 3, 1, 4)
        return t.reshape(B, dilation, H, nb, BLOCK, Dh)

    def with_prev(t):
        prev = jnp.pad(t, ((0, 0), (0, 0), (0, 0), (1, 0), (0, 0), (0, 0)))[:, :, :, :-1]
        return jnp.concatenate([prev, t], axis=4)

    qb = to_blocks(q)
    kc = with_prev(to_blocks(k))
    vc = with_prev(to_blocks(v))
    s = jnp.einsum('brhnqe,brhnke->brhnqk', qb, kc).astype(jnp.float32) * (Dh ** -0.5)
    qi = jnp.arange(BLOCK)[:, None] + BLOCK
    ki = jnp.arange(2 * BLOCK)[None, :]
    dist = qi - ki
    band = (dist >= 0) & (dist <= span)
    has_prev = (jnp.arange(nb) > 0)[:, None, None] | (ki >= BLOCK)[None]
    mask = band[None] & has_prev
    s = jnp.where(mask, s, -jnp.inf)
    m = jnp.max(s, axis=-1, keepdims=True)
    p = jnp.exp(s - m)
    l = jnp.sum(p, axis=-1, keepdims=True)
    o = jnp.einsum('brhnqk,brhnke->brhnqe', p, vc.astype(jnp.float32)) / l
    lse = (m + jnp.log(l))[..., 0]

    def from_blocks(t):
        tail = t.shape[5:]
        t = t.reshape((B, dilation, H, L) + tail)
        t = jnp.moveaxis(t, 3, 1)
        return t.reshape((B, L * dilation, H) + tail)[:, :S]

    return from_blocks(o), from_blocks(lse)

def dilated_mixture_attention(q, k, v):
    outs, lses = [], []
    for window, dilation in DILATED_CONFIGS:
        o, lse = dilated_window_attention(q, k, v, window, dilation)
        outs.append(o)
        lses.append(lse)
    wts = jax.nn.softmax(jnp.stack(lses, axis=0), axis=0)
    return jnp.sum(wts[..., None] * jnp.stack(outs, axis=0), axis=0)

def token_shift(t):
    return jnp.pad(t, ((0, 0), (1, 0), (0, 0)))[:, :-1]

def wkv7_scan(r, decay, k, v, a, b):
    B, S, H, N = r.shape
    seq = tuple(jnp.moveaxis(t, 1, 0) for t in (r, decay, k, v, a, b))

    def step(state, inp):
        r_t, w_t, k_t, v_t, a_t, b_t = inp
        sa = jnp.einsum('bhij,bhj->bhi', state, a_t)
        state = (state * w_t[:, :, None, :] + sa[..., None] * b_t[:, :, None, :]
                 + v_t[..., None] * k_t[:, :, None, :])
        return state, jnp.einsum('bhij,bhj->bhi', state, r_t)

    _, y = lax.scan(step, jnp.zeros((B, H, N, N), jnp.float32), seq)
    return jnp.moveaxis(y, 0, 1)

def rwkv7_time_mix(p_rwkv, mu, w0, w_up, a0, a_up, g_up, k_k, k_a, r_k, gn_w, gn_b):
    B, S, _ = p_rwkv.shape
    z = p_rwkv.astype(jnp.float32)
    z = z + (token_shift(z) - z) * mu
    o1 = RWKV_WIDTH
    o2 = 2 * RWKV_WIDTH
    o3 = 3 * RWKV_WIDTH
    o4 = o3 + DECAY_LORA
    o5 = o4 + AAA_LORA
    r, k, v = z[..., :o1], z[..., o1:o2], z[..., o2:o3]
    xw, xa, xg = z[..., o3:o4], z[..., o4:o5], z[..., o5:]
    w = -jax.nn.softplus(-(w0 + jnp.tanh(xw) @ w_up)) - 0.5
    a = jax.nn.sigmoid(a0 + xa @ a_up)
    g = jax.nn.sigmoid(xg) @ g_up
    hs = lambda t: t.reshape(B, S, RWKV_HEADS, RWKV_HEAD)
    kk = hs(k * k_k)
    kk = kk / jnp.maximum(jnp.sqrt(jnp.sum(kk * kk, axis=-1, keepdims=True)), 1e-12)
    k = k * (1.0 + (a - 1.0) * k_a)
    r4, k4, v4, a4 = hs(r), hs(k), hs(v), hs(a)
    decay = jnp.exp(-jnp.exp(hs(w)))
    y = wkv7_scan(r4, decay, k4, v4, -kk, kk * a4)
    mu_y = jnp.mean(y, axis=-1, keepdims=True)
    var_y = jnp.mean(jnp.square(y - mu_y), axis=-1, keepdims=True)
    y = (y - mu_y) * lax.rsqrt(var_y + GN_EPS) * gn_w.reshape(RWKV_HEADS, RWKV_HEAD) \
        + gn_b.reshape(RWKV_HEADS, RWKV_HEAD)
    y = y + jnp.sum(r4 * k4 * r_k, axis=-1, keepdims=True) * v4
    return y.reshape(B, S, RWKV_WIDTH) * g

def chunked_spatial_gating(p_uv, ln_g, ln_b, w_s, b_s):
    B, S, _ = p_uv.shape
    z = jax.nn.gelu(p_uv.astype(jnp.float32))
    u, v = z[..., :GMLP_WIDTH], z[..., GMLP_WIDTH:]
    v = layer_norm(v, ln_g, ln_b, LN_EPS)
    nc = S // GMLP_CHUNK
    vg = v.reshape(B, nc, GMLP_CHUNK, GMLP_GROUPS, GMLP_GROUP_DIM)
    causal = jnp.tril(jnp.ones((GMLP_CHUNK, GMLP_CHUNK), dtype=bool))
    ws = jnp.where(causal[None], w_s, 0.0)
    s = jnp.einsum('gij,bcjgd->bcigd', ws, vg) + b_s.T[None, None, :, :, None]
    return u * s.reshape(B, S, GMLP_WIDTH)

def conv_gated_ffn(h, w_up, conv_w, conv_b, w_down):
    S = h.shape[1]
    up = h @ w_up
    a, g = up[..., :D_FF], up[..., D_FF:]
    ap = jnp.pad(a, ((0, 0), (CONV_WIDTH - 1, 0), (0, 0)))
    a = conv_b + sum(conv_w[j] * ap[:, j:j + S] for j in range(CONV_WIDTH))
    return (jax.nn.gelu(a) * g) @ w_down

def first_inputs(seed: int = 0) -> dict:
    key = jax.random.key(seed)
    ks = jax.random.split(key, 32)
    nrm = lambda k, shape, scale: jax.random.normal(k, shape, jnp.float32) * scale
    L = DEPTH
    return {
        'x': nrm(ks[0], (BATCH, SEQ, D_MODEL), 1.0),
        'c': nrm(ks[1], (BATCH, D_MODEL), 1.0),
        'w_ada': nrm(ks[2], (L, D_MODEL, 6 * D_MODEL), 0.5 * D_MODEL ** -0.5),
        'b_ada': nrm(ks[3], (L, 6 * D_MODEL), 0.02),
        'norm_mix': 1.0 + nrm(ks[4], (L, D_MODEL), 0.05),
        'w_in': nrm(ks[5], (L, D_MODEL, IN_COLS), D_MODEL ** -0.5),
        'rwkv_mu': jax.random.uniform(ks[6], (L, RWKV_COLS), jnp.float32),
        'rwkv_w0': jax.random.uniform(ks[7], (L, RWKV_WIDTH), jnp.float32, minval=-5.0, maxval=-1.0),
        'rwkv_w_up': nrm(ks[8], (L, DECAY_LORA, RWKV_WIDTH), 0.5 * DECAY_LORA ** -0.5),
        'rwkv_a0': nrm(ks[9], (L, RWKV_WIDTH), 0.1),
        'rwkv_a_up': nrm(ks[10], (L, AAA_LORA, RWKV_WIDTH), AAA_LORA ** -0.5),
        'rwkv_g_up': nrm(ks[11], (L, GATE_LORA, RWKV_WIDTH), GATE_LORA ** -0.5),
        'rwkv_k_k': 0.85 + nrm(ks[12], (L, RWKV_WIDTH), 0.05),
        'rwkv_k_a': 1.0 + nrm(ks[13], (L, RWKV_WIDTH), 0.05),
        'rwkv_r_k': nrm(ks[14], (L, RWKV_HEADS, RWKV_HEAD), 0.1),
        'rwkv_gn_w': 1.0 + nrm(ks[15], (L, RWKV_WIDTH), 0.05),
        'rwkv_gn_b': nrm(ks[16], (L, RWKV_WIDTH), 0.02),
        'gmlp_ln_g': 1.0 + nrm(ks[17], (L, GMLP_WIDTH), 0.05),
        'gmlp_ln_b': nrm(ks[18], (L, GMLP_WIDTH), 0.02),
        'gmlp_w_s': nrm(ks[19], (L, GMLP_GROUPS, GMLP_CHUNK, GMLP_CHUNK), 0.5 * GMLP_CHUNK ** -0.5),
        'gmlp_b_s': 1.0 + nrm(ks[20], (L, GMLP_GROUPS, GMLP_CHUNK), 0.05),
        'w_branch': nrm(ks[21], (L, N_BRANCH, ATT_WIDTH, D_MODEL), ATT_WIDTH ** -0.5),
        'w_out': nrm(ks[22], (L, D_MODEL, D_MODEL), D_MODEL ** -0.5),
        'norm_ffn': 1.0 + nrm(ks[23], (L, D_MODEL), 0.05),
        'ffn_w_up': nrm(ks[24], (L, D_MODEL, 2 * D_FF), D_MODEL ** -0.5),
        'ffn_conv_w': nrm(ks[25], (L, CONV_WIDTH, D_FF), CONV_WIDTH ** -0.5),
        'ffn_conv_b': nrm(ks[26], (L, D_FF), 0.02),
        'ffn_w_down': nrm(ks[27], (L, D_FF, D_MODEL), D_FF ** -0.5),
        'norm_final': 1.0 + nrm(ks[28], (D_MODEL,), 0.05),
    }

def first_block(x, c, w_ada, b_ada, norm_mix, w_in, rwkv_mu, rwkv_w0, rwkv_w_up, rwkv_a0,
              rwkv_a_up, rwkv_g_up, rwkv_k_k, rwkv_k_a, rwkv_r_k, rwkv_gn_w, rwkv_gn_b,
              gmlp_ln_g, gmlp_ln_b, gmlp_w_s, gmlp_b_s, w_branch, w_out, norm_ffn,
              ffn_w_up, ffn_conv_w, ffn_conv_b, ffn_w_down, norm_final):
    B, S, D = x.shape
    cos, sin = rope_tables(S)
    c_act = jax.nn.silu(c)
    i0 = 3 * ATT_WIDTH
    i1 = i0 + RWKV_COLS
    i2 = i1 + 2 * GMLP_WIDTH
    for l in range(DEPTH):
        mod = c_act @ w_ada[l] + b_ada[l]
        sh1, sc1, gt1, sh2, sc2, gt2 = jnp.split(mod, 6, axis=-1)

        h = modulate(rms_norm(x, norm_mix[l]), sh1, sc1)
        p = h @ w_in[l]
        qkv = p[..., :i0].reshape(B, S, 3, ATT_HEADS, HEAD_DIM)
        q = apply_rope(qkv[:, :, 0], cos, sin)
        k = apply_rope(qkv[:, :, 1], cos, sin)
        y_att = dilated_mixture_attention(q, k, qkv[:, :, 2]).reshape(B, S, ATT_WIDTH)
        y_rwkv = rwkv7_time_mix(p[..., i0:i1], rwkv_mu[l], rwkv_w0[l], rwkv_w_up[l], rwkv_a0[l],
                                rwkv_a_up[l], rwkv_g_up[l], rwkv_k_k[l], rwkv_k_a[l], rwkv_r_k[l],
                                rwkv_gn_w[l], rwkv_gn_b[l])
        y_gmlp = chunked_spatial_gating(p[..., i1:i2], gmlp_ln_g[l], gmlp_ln_b[l], gmlp_w_s[l], gmlp_b_s[l])
        ys = jnp.stack([y_att, y_rwkv, y_gmlp], axis=2).astype(x.dtype)
        gates = jax.nn.sigmoid(p[..., i2:].reshape(B, S, N_BRANCH, D))
        branch = jnp.einsum('bsnw,nwd->bsnd', ys, w_branch[l])
        merged = jnp.sum(gates * branch, axis=2)
        x = x + gt1[:, None, :] * (merged @ w_out[l])

        h = modulate(rms_norm(x, norm_ffn[l]), sh2, sc2)
        x = x + gt2[:, None, :] * conv_gated_ffn(h, ffn_w_up[l], ffn_conv_w[l], ffn_conv_b[l], ffn_w_down[l])
    return rms_norm(x, norm_final)


NSA_HEADS = 8
NSA_GROUPS = 2
NSA_HPG = NSA_HEADS // NSA_GROUPS
NSA_DH = 64
CMP_BLOCK = 32
CMP_STRIDE = 16
CMP_HIDDEN = 256
SEL_BLOCK = 64
SEL_TOPN = 16
WINDOW = 512
Q_BLOCK = 64
GLA_HEADS = 4
GLA_DK = 128
GLA_DV = 256
GLA_RANK = 16
GLA_TAU = 16.0
GLA_CHUNK = 64
REL_BUCKETS = 32
REL_MAX_DIST = 1024
EPS = 1e-6
NEG = -1e30

W_IN_SPLITS = (
    NSA_HEADS * NSA_DH,
    6 * NSA_GROUPS * NSA_DH,
    3 * NSA_HEADS,
    GLA_HEADS * GLA_DK,
    GLA_HEADS * GLA_DK,
    GLA_HEADS * GLA_DV,
    GLA_RANK,
    GLA_HEADS * GLA_DV,
    2 * D_MODEL,
)
D_IN = sum(W_IN_SPLITS)


def rmsnorm(x, g):
    xf = x.astype(jnp.float32)
    y = xf * lax.rsqrt(jnp.mean(xf * xf, axis=-1, keepdims=True) + EPS)
    return (y * g.astype(jnp.float32)).astype(x.dtype)

def swiglu(x, w_gate, w_up, w_down):
    return (jax.nn.silu(x @ w_gate) * (x @ w_up)) @ w_down

def rel_bucket(dist):
    n = jnp.maximum(dist, 0)
    exact = REL_BUCKETS // 2
    nf = jnp.maximum(n, 1).astype(jnp.float32)
    log_b = exact + (jnp.log(nf / exact) / math.log(REL_MAX_DIST / exact)
                     * (REL_BUCKETS - exact)).astype(jnp.int32)
    return jnp.where(n < exact, n, jnp.minimum(log_b, REL_BUCKETS - 1))

def masked_softmax(logits, mask):
    p = jax.nn.softmax(jnp.where(mask, logits, NEG), axis=-1)
    return jnp.where(mask, p, 0.0)

def nsa_compress(k, pos, w1, w2):
    B, S, G, dh = k.shape
    nc = (S - CMP_BLOCK) // CMP_STRIDE + 1
    idx = jnp.arange(nc)[:, None] * CMP_STRIDE + jnp.arange(CMP_BLOCK)[None, :]
    blocks = k[:, idx] + pos[None, None, :, None, :]
    blocks = blocks.transpose(0, 1, 3, 2, 4).reshape(B, nc, G, CMP_BLOCK * dh)
    return jax.nn.silu(blocks @ w1) @ w2

def nsa_attention(q, k_cmp, v_cmp, k_slc, v_slc, k_win, v_win, gates, rel_table):
    B, S, H, dh = q.shape
    G, HPG = NSA_GROUPS, NSA_HPG
    nqb = S // Q_BLOCK
    ns = S // SEL_BLOCK
    nc = k_cmp.shape[1]
    n_sel = min(SEL_TOPN, ns)
    kw_len = WINDOW + Q_BLOCK

    c_start = jnp.arange(nc) * CMP_STRIDE
    cmp_end = c_start + CMP_BLOCK - 1
    sb_start = jnp.arange(ns) * SEL_BLOCK
    overlap = ((c_start[:, None] < sb_start[None, :] + SEL_BLOCK)
               & (c_start[:, None] + CMP_BLOCK > sb_start[None, :])).astype(jnp.float32)
    js = jnp.arange(ns)
    table_g = rel_table.reshape(REL_BUCKETS, G, HPG).transpose(1, 0, 2)

    kb = k_slc.reshape(B, ns, SEL_BLOCK, G, dh).transpose(0, 3, 1, 2, 4)
    vb = v_slc.reshape(B, ns, SEL_BLOCK, G, dh).transpose(0, 3, 1, 2, 4)
    pad = ((0, 0), (WINDOW, 0), (0, 0), (0, 0))
    kw = jnp.pad(k_win, pad)
    vw = jnp.pad(v_win, pad)

    def to_blocks(a):
        return a.reshape(B, nqb, Q_BLOCK, *a.shape[2:]).swapaxes(0, 1)

    qs = to_blocks(q * (dh ** -0.5))
    gs = to_blocks(gates)
    bi = jnp.arange(B)[:, None, None, None]
    gi = jnp.arange(G)[None, :, None, None]

    def block_fn(args):
        c, qc, gc = args
        t = c * Q_BLOCK + jnp.arange(Q_BLOCK)
        qg = qc.reshape(B, Q_BLOCK, G, HPG, dh)

        lc = jnp.einsum('bqghd,bcgd->bghqc', qg, k_cmp).astype(jnp.float32)
        bias_c = rel_table[rel_bucket(t[:, None] - cmp_end[None, :])]
        lc = lc + bias_c.reshape(Q_BLOCK, nc, G, HPG).transpose(2, 3, 0, 1)
        p_cmp = masked_softmax(lc, cmp_end[None, :] <= t[:, None])
        o_cmp = jnp.einsum('bghqc,bcgd->bqghd', p_cmp.astype(v_cmp.dtype), v_cmp)

        imp = jnp.einsum('bghqc,cs->bgqs', p_cmp, overlap)
        jcur = t // SEL_BLOCK
        forced = (js[None, :] == 0) | (js[None, :] == jcur[:, None]) | (js[None, :] == jcur[:, None] - 1)
        valid = js[None, :] <= jcur[:, None]
        score = jnp.where(forced, 1e6, jnp.where(valid, imp, -1e6))
        _, sel = lax.top_k(score, n_sel)
        ks = kb[bi, gi, sel]
        vs = vb[bi, gi, sel]
        s_pos = sel[..., None] * SEL_BLOCK + jnp.arange(SEL_BLOCK)
        ls = jnp.einsum('bqghd,bgqnrd->bghqnr', qg, ks).astype(jnp.float32)
        bias_s = table_g[gi[..., None], rel_bucket(t[:, None, None] - s_pos)]
        ls = ls + bias_s.transpose(0, 1, 5, 2, 3, 4)
        ksel = n_sel * SEL_BLOCK
        ls = ls.reshape(B, G, HPG, Q_BLOCK, ksel)
        ms = (s_pos <= t[:, None, None]).reshape(B, G, Q_BLOCK, ksel)[:, :, None]
        p_s = masked_softmax(ls, ms)
        o_slc = jnp.einsum('bghqk,bgqkd->bqghd', p_s.astype(vs.dtype),
                           vs.reshape(B, G, Q_BLOCK, ksel, dh))

        kwc = lax.dynamic_slice_in_dim(kw, c * Q_BLOCK, kw_len, axis=1)
        vwc = lax.dynamic_slice_in_dim(vw, c * Q_BLOCK, kw_len, axis=1)
        s_w = c * Q_BLOCK - WINDOW + jnp.arange(kw_len)
        dist = t[:, None] - s_w[None, :]
        mw = (s_w[None, :] >= 0) & (dist >= 0) & (dist < WINDOW)
        lw = jnp.einsum('bqghd,bkgd->bghqk', qg, kwc).astype(jnp.float32)
        lw = lw + rel_table[rel_bucket(dist)].reshape(Q_BLOCK, kw_len, G, HPG).transpose(2, 3, 0, 1)
        p_w = masked_softmax(lw, mw)
        o_win = jnp.einsum('bghqk,bkgd->bqghd', p_w.astype(vwc.dtype), vwc)

        o = jnp.stack([o_cmp, o_slc, o_win], axis=-1)
        g = gc.reshape(B, Q_BLOCK, G, HPG, 3)[..., None, :]
        return jnp.sum(o * g, axis=-1).reshape(B, Q_BLOCK, H * dh).astype(q.dtype)

    out = lax.map(block_fn, (jnp.arange(nqb), qs, gs))
    return out.swapaxes(0, 1).reshape(B, S, H * dh)

def gla_attention(q, k, v, log_a):
    B, S, Hb, dk = q.shape
    dv = v.shape[-1]
    C = GLA_CHUNK
    n = S // C

    def chunks(a):
        return a.reshape(B, n, C, *a.shape[2:])

    qc, kc, vc, la = chunks(q * (dk ** -0.5)), chunks(k), chunks(v), chunks(log_a)
    b = jnp.cumsum(la.astype(jnp.float32), axis=2)
    b_last = b[:, :, -1:]
    q_dec = qc * jnp.exp(b)
    k_intra = kc * jnp.exp(-b)
    k_state = kc * jnp.exp(b_last - b)
    causal = jnp.tril(jnp.ones((C, C), dtype=bool))
    A = jnp.where(causal, jnp.einsum('bnihd,bnjhd->bnhij', q_dec, k_intra), 0.0)
    o_intra = jnp.einsum('bnhij,bnjhv->bnihv', A, vc.astype(jnp.float32))
    decay_chunk = jnp.exp(b_last[:, :, 0])

    def step(state, inp):
        qd, ksd, vcc, dch = inp
        o = jnp.einsum('bihd,bhdv->bihv', qd, state)
        state = dch[..., None] * state + jnp.einsum('bjhd,bjhv->bhdv', ksd, vcc.astype(jnp.float32))
        return state, o

    s0 = jnp.zeros((B, Hb, dk, dv), jnp.float32)
    _, o_inter = lax.scan(step, s0, (q_dec.swapaxes(0, 1), k_state.swapaxes(0, 1),
                                     vc.swapaxes(0, 1), decay_chunk.swapaxes(0, 1)))
    o = o_intra + o_inter.swapaxes(0, 1)
    return o.reshape(B, S, Hb, dv).astype(v.dtype)

def second_inputs(seed: int = 0) -> dict:
    key = jax.random.key(seed)
    ks = jax.random.split(key, 32)
    f32 = jnp.float32
    L, D = DEPTH, D_MODEL

    def w(k, shape, fan_in):
        return jax.random.normal(k, shape, f32) * fan_in ** -0.5

    def gain(k, shape):
        return 1.0 + 0.05 * jax.random.normal(k, shape, f32)

    return {
        "x": jax.random.normal(ks[0], (BATCH, SEQ, D), f32),
        "rel_table": 0.2 * jax.random.normal(ks[1], (REL_BUCKETS, NSA_HEADS), f32),
        "ffn1_norm": gain(ks[2], (L, D)),
        "ffn1_w_gate": w(ks[3], (L, D, D_FF), D),
        "ffn1_w_up": w(ks[4], (L, D, D_FF), D),
        "ffn1_w_down": w(ks[5], (L, D_FF, D), D_FF),
        "mix_norm": gain(ks[6], (L, D)),
        "w_in": w(ks[7], (L, D, D_IN), D),
        "cmp_pos_k": 0.5 * jax.random.normal(ks[8], (L, CMP_BLOCK, NSA_DH), f32),
        "cmp_pos_v": 0.5 * jax.random.normal(ks[9], (L, CMP_BLOCK, NSA_DH), f32),
        "cmp_k_w1": w(ks[10], (L, CMP_BLOCK * NSA_DH, CMP_HIDDEN), CMP_BLOCK * NSA_DH),
        "cmp_k_w2": w(ks[11], (L, CMP_HIDDEN, NSA_DH), CMP_HIDDEN),
        "cmp_v_w1": w(ks[12], (L, CMP_BLOCK * NSA_DH, CMP_HIDDEN), CMP_BLOCK * NSA_DH),
        "cmp_v_w2": w(ks[13], (L, CMP_HIDDEN, NSA_DH), CMP_HIDDEN),
        "gla_a_w2": w(ks[14], (L, GLA_RANK, GLA_HEADS * GLA_DK), GLA_RANK),
        "gla_a_b": 0.1 * jax.random.normal(ks[15], (L, GLA_HEADS * GLA_DK), f32),
        "gla_out_norm": gain(ks[16], (L, GLA_HEADS * GLA_DV)),
        "w_branch_nsa": w(ks[17], (L, NSA_HEADS * NSA_DH, D), NSA_HEADS * NSA_DH),
        "w_branch_gla": w(ks[18], (L, GLA_HEADS * GLA_DV, D), GLA_HEADS * GLA_DV),
        "w_out": w(ks[19], (L, D, D), D),
        "ffn2_norm": gain(ks[20], (L, D)),
        "ffn2_w_gate": w(ks[21], (L, D, D_FF), D),
        "ffn2_w_up": w(ks[22], (L, D, D_FF), D),
        "ffn2_w_down": w(ks[23], (L, D_FF, D), D_FF),
        "final_norm": gain(ks[24], (D,)),
    }

def second_block(x, rel_table, ffn1_norm, ffn1_w_gate, ffn1_w_up, ffn1_w_down, mix_norm, w_in,
              cmp_pos_k, cmp_pos_v, cmp_k_w1, cmp_k_w2, cmp_v_w1, cmp_v_w2, gla_a_w2, gla_a_b,
              gla_out_norm, w_branch_nsa, w_branch_gla, w_out, ffn2_norm, ffn2_w_gate, ffn2_w_up,
              ffn2_w_down, final_norm):
    B, S, D = x.shape
    offsets = np.cumsum(W_IN_SPLITS)[:-1].tolist()
    for l in range(DEPTH):
        x = x + 0.5 * swiglu(rmsnorm(x, ffn1_norm[l]), ffn1_w_gate[l], ffn1_w_up[l], ffn1_w_down[l])

        h = rmsnorm(x, mix_norm[l])
        proj = h @ w_in[l]
        q_a, kv_a, g_a, q_b, k_b, v_b, a_lr, r_b, g_merge = jnp.split(proj, offsets, axis=-1)

        q_a = q_a.reshape(B, S, NSA_HEADS, NSA_DH)
        kv_a = kv_a.reshape(B, S, 6, NSA_GROUPS, NSA_DH)
        k_cmp = nsa_compress(kv_a[:, :, 0], cmp_pos_k[l], cmp_k_w1[l], cmp_k_w2[l])
        v_cmp = nsa_compress(kv_a[:, :, 1], cmp_pos_v[l], cmp_v_w1[l], cmp_v_w2[l])
        gates_a = jax.nn.sigmoid(g_a).reshape(B, S, NSA_HEADS, 3)
        o_a = nsa_attention(q_a, k_cmp, v_cmp, kv_a[:, :, 2], kv_a[:, :, 3],
                            kv_a[:, :, 4], kv_a[:, :, 5], gates_a, rel_table)

        log_a = jax.nn.log_sigmoid((a_lr @ gla_a_w2[l] + gla_a_b[l]).astype(jnp.float32)) / GLA_TAU
        o_b = gla_attention(q_b.reshape(B, S, GLA_HEADS, GLA_DK),
                            k_b.reshape(B, S, GLA_HEADS, GLA_DK),
                            v_b.reshape(B, S, GLA_HEADS, GLA_DV),
                            log_a.reshape(B, S, GLA_HEADS, GLA_DK))
        o_b = rmsnorm(o_b, gla_out_norm[l].reshape(GLA_HEADS, GLA_DV))
        o_b = o_b.reshape(B, S, GLA_HEADS * GLA_DV) * jax.nn.silu(r_b)

        gm = jax.nn.sigmoid(g_merge).reshape(B, S, 2, D)
        y = gm[:, :, 0] * (o_a @ w_branch_nsa[l]) + gm[:, :, 1] * (o_b @ w_branch_gla[l])
        x = x + y @ w_out[l]

        x = x + 0.5 * swiglu(rmsnorm(x, ffn2_norm[l]), ffn2_w_gate[l], ffn2_w_up[l], ffn2_w_down[l])
    return rmsnorm(x, final_norm)


def setup_inputs(seed=0):
    out = dict(first_inputs(seed))
    for name, value in second_inputs(seed + 1).items():
        if name != "x":
            out[name + "_2"] = value
    return out


def reference(
    x, c, w_ada, b_ada, norm_mix, w_in, rwkv_mu, rwkv_w0, rwkv_w_up, rwkv_a0, rwkv_a_up,
    rwkv_g_up, rwkv_k_k, rwkv_k_a, rwkv_r_k, rwkv_gn_w, rwkv_gn_b, gmlp_ln_g, gmlp_ln_b,
    gmlp_w_s, gmlp_b_s, w_branch, w_out, norm_ffn, ffn_w_up, ffn_conv_w, ffn_conv_b, ffn_w_down,
    norm_final, rel_table_2, ffn1_norm_2, ffn1_w_gate_2, ffn1_w_up_2, ffn1_w_down_2, mix_norm_2,
    w_in_2, cmp_pos_k_2, cmp_pos_v_2, cmp_k_w1_2, cmp_k_w2_2, cmp_v_w1_2, cmp_v_w2_2,
    gla_a_w2_2, gla_a_b_2, gla_out_norm_2, w_branch_nsa_2, w_branch_gla_2, w_out_2, ffn2_norm_2,
    ffn2_w_gate_2, ffn2_w_up_2, ffn2_w_down_2, final_norm_2,
):
    x = first_block(
        x, c, w_ada, b_ada, norm_mix, w_in, rwkv_mu, rwkv_w0, rwkv_w_up, rwkv_a0, rwkv_a_up,
        rwkv_g_up, rwkv_k_k, rwkv_k_a, rwkv_r_k, rwkv_gn_w, rwkv_gn_b, gmlp_ln_g, gmlp_ln_b,
        gmlp_w_s, gmlp_b_s, w_branch, w_out, norm_ffn, ffn_w_up, ffn_conv_w, ffn_conv_b,
        ffn_w_down, norm_final,
    )
    return second_block(
        x, rel_table_2, ffn1_norm_2, ffn1_w_gate_2, ffn1_w_up_2, ffn1_w_down_2, mix_norm_2,
        w_in_2, cmp_pos_k_2, cmp_pos_v_2, cmp_k_w1_2, cmp_k_w2_2, cmp_v_w1_2, cmp_v_w2_2,
        gla_a_w2_2, gla_a_b_2, gla_out_norm_2, w_branch_nsa_2, w_branch_gla_2, w_out_2,
        ffn2_norm_2, ffn2_w_gate_2, ffn2_w_up_2, ffn2_w_down_2, final_norm_2,
    )


_drawn_inputs = setup_inputs


def setup_inputs(seed=0):
    import zlib

    import numpy as np

    out = dict(_drawn_inputs(seed))
    spreads = {}
    factors = {'rwkv_w_up': 5.965,
     'rwkv_a0': 7.378,
     'rwkv_k_k': 4.948,
     'rwkv_k_a': 3.848,
     'rwkv_gn_w': 6.13,
     'rwkv_gn_b': 8.0,
     'gmlp_ln_g': 8.0,
     'gmlp_ln_b': 44.264,
     'gmlp_b_s': 4.614,
     'ffn_conv_b': 6.586,
     'cmp_pos_k_2': 4.334,
     'gla_a_b_2': 2.988}
    for name, (base, spread) in spreads.items():
        noise = np.random.default_rng([zlib.crc32(name.encode()), seed]).standard_normal(out[name].shape)
        drawn = base * np.exp(spread * noise) if base else spread * noise
        out[name] = __import__('jax').numpy.asarray(drawn.astype(out[name].dtype))
    for name, factor in factors.items():
        out[name] = (out[name] * factor).astype(out[name].dtype)
    return out
```

```python
from contextlib import ExitStack, contextmanager

import numpy as np

import concourse.bass as bass
from concourse import mybir

ALU = mybir.AluOpType
ACT = mybir.ActivationFunctionType
AX = mybir.AxisListType
F32 = mybir.dt.float32

P = 128
TOK = 256
NT = TOK // P
D = 1024
KD = D // P
DEPTH = 2
HEADS = 8
DH = 64
WIDTH = HEADS * DH
NB = WIDTH // P
D_FF = 2816
NF = D_FF // P
RWKV_COLS = 3 * WIDTH + 64 + 64 + 128
NZ = RWKV_COLS // P
CHUNK = 64
NCH = TOK // CHUNK
ATT0, RWKV0 = 0, 3 * WIDTH
UV0 = RWKV0 + RWKV_COLS
GATE0 = UV0 + 2 * WIDTH
DECAY = float(np.exp(-0.5))
RMS_EPS, LN_EPS, GN_EPS = 1e-6, 1e-5, 64e-5
NEG = -1e30
SLOTS = 4
SLOT = 2048
NC = 15
S_KV, S_GA, S_QB = 512, 1280, 1304
S_KB, S_VB, S_AL, S_RB, S_GM = 1816, 2328, 3352, 3368, 4392
GH, GV = 4, 256
NG = GH * GV // P


CONSTS = ["ident", "blockones", "ones", "strict_up", "incl_up", "strict_lo"] + [f"level{i}" for i in range(6)] + ["lower0", "upper"]


def shape_constants():
    i = np.arange(P)
    r, c = i[:, None], i[None, :]
    same = (r // CHUNK) == (c // CHUNK)
    m = {"ident": r == c, "blockones": (r // DH) == (c // DH), "ones": np.ones((P, P), bool),
         "strict_up": same & (r < c), "incl_up": same & (r <= c), "strict_lo": same & (r > c)}
    for k in range(6):
        b = 2 << k
        m[f"level{k}"] = ((r // b) == (c // b)) & (r % b < b // 2) & (c % b >= b // 2)
    m["lower0"] = m["level0"].T
    m["upper"] = r <= c
    square = np.concatenate([m[n] for n in CONSTS], axis=1).astype(np.float32)
    t, s = np.arange(TOK)[:, None], np.arange(TOK)[None, :]
    count = ((t >= s) & (t - s <= 128)).astype(np.float32)
    for d in (4, 16):
        count += (t >= s) & ((t - s) % d == 0)
    blocked = np.where(count > 0, 0, NEG).astype(np.float32)
    ends = 16 * np.arange(NC)[None, :] + 31
    seen = (ends <= t).astype(np.float32)
    inv = 1.0 / (np.float32(10000.0) ** (np.arange(0, DH, 2, dtype=np.float32) / np.float32(DH)))
    ang = np.arange(TOK, dtype=np.float32)[:, None] * inv[None, :].astype(np.float32)
    rows = np.concatenate([count, blocked, np.cos(ang), np.sin(ang), seen], axis=1).astype(np.float32)
    tiles = rows.reshape(NT, P, -1).transpose(1, 0, 2)
    dist = np.arange(TOK)
    logb = 16 + (np.log(np.maximum(dist, 1).astype(np.float32) / np.float32(16)) / np.float32(np.log(64.0))
                 * np.float32(16)).astype(np.int32)
    bucket = np.where(dist < 16, dist, np.minimum(logb, 31))
    onehot = (np.arange(32)[:, None] == bucket[None, ::-1]).astype(np.float32)
    return {"c_square": square, "c_rows": np.ascontiguousarray(tiles), "c_onehot": onehot}


class Signal:

    def __init__(self, sem):
        self.sem, self.base = sem, 0

    def at(self, n):
        return self.base + n


class Steps(Signal):

    def __init__(self, sem):
        super().__init__(sem)
        self.moving = 0

    def did(self, ins):
        ins.then_inc(self.sem, 1)
        self.base += 1
        return ins

    def settle(self, eng):
        eng.wait_ge(self.sem, self.moving + self.base)


@contextmanager
def counted(steps, it, per):
    if steps is None:
        yield
        return
    start = steps.base
    steps.moving = it * per
    yield
    assert steps.base - start == per, (steps.base - start, per)
    steps.moving = 0


def repeat(eng, n, unroll, step, peel=0, steps=None, per=0):
    for i in range(min(peel, n)):
        step(i, i)
    turns = (n - peel) // unroll
    done = peel
    if turns >= 2:
        with eng.Fori(0, turns) as it:
            with counted(steps, it, per * unroll):
                for j in range(unroll):
                    step(it * unroll + (peel + j), peel + j)
        if steps is not None:
            steps.base += per * unroll * (turns - 1)
        done = peel + turns * unroll
    for i in range(done, n):
        step(i, i)


class Program:

    def __init__(self, nc, ctx):
        self.nc, self.ctx, self.flags = nc, ctx, {}
        self.chunk = self.group = self.phase = 0
        self.pe_steps = Steps(self.sem("pe_steps"))
        self.act_steps = Steps(self.sem("act_steps"))
        self.dve_steps = Steps(self.sem("dve_steps"))
        self.pool_steps = Steps(self.sem("pool_steps"))
        self.slot_landed = [Signal(self.sem(f"slot_landed{i}")) for i in range(SLOTS)]

    chunks = 96

    def sem(self, name):
        return self.ctx.enter_context(self.nc.semaphore(name))

    def sb(self, name, shape):
        return self.ctx.enter_context(self.nc.sbuf_tensor(name, shape, F32))

    def flag(self, name):
        if name not in self.flags:
            self.flags[name] = Signal(self.sem(name))
        return self.flags[name]

    def all_flags(self):
        return [self.pe_steps, self.act_steps, self.dve_steps, self.pool_steps] + self.slot_landed + list(self.flags.values())

    def end_layer(self):
        nc = self.nc
        engines = [nc.sync, nc.tensor, nc.scalar, nc.vector, nc.gpsimd]
        for n, s in enumerate(self.all_flags()):
            engines[n % 5].sem_clear(s.sem)
            s.base = 0
        self.chunk = self.group = self.phase = 0
        nc.all_engine_barrier()


def phase_end(block, k):
    k.phase += 1
    arrived = k.flag("phase_arrived")

    def meet(eng):
        eng.drain().then_inc(arrived.sem, 1)
        eng.wait_ge(arrived.sem, 4 * k.phase)

    @block.tensor
    def _(pe):
        meet(pe)

    @block.scalar
    def _(act):
        meet(act)

    @block.vector
    def _(dve):
        meet(dve)

    @block.gpsimd
    def _(pool):
        meet(pool)


def stream(block, k, weights, n):
    used = k.flag("slot_used")

    @block.sync
    def _(sp):
        def one(i, j):
            if not isinstance(i, int) or i >= SLOTS:
                sp.wait_ge(used.sem, i + (1 - SLOTS))
            source = weights[bass.ds(i, 1)].rearrange("a p n -> (a p) n")
            sp.dma_start(k.slots[j % SLOTS][:], source).then_inc(k.slot_landed[j % SLOTS].sem, 16)
        repeat(sp, n, SLOTS, one, peel=SLOTS)


def slot_wait(pe, first, i, j, k):
    slot = (first + j) % SLOTS
    if isinstance(i, int):
        pe.wait_ge(k.slot_landed[slot].sem, 16 * ((first + i) // SLOTS + 1))
    else:
        turn = i - j
        pe.wait_ge(k.slot_landed[slot].sem, turn * (16 // SLOTS) + 16 * ((first + j) // SLOTS + 1))
    return k.slots[slot]


def bank_wait(eng, k, i, evac):
    for name in ("act_evac", "dve_evac"):
        s = k.flag(name)
        if name in evac:
            v = s.base + i - 1
            if not isinstance(i, int) or v > 0:
                eng.wait_ge(s.sem, v)
        elif isinstance(i, int) and i == 0 and s.base > 0:
            eng.wait_ge(s.sem, s.base)


def product(block, k, kind, width, groups, ktiles=KD, moving=None, stationary=None,
            act=None, dve=None, dve_per=0, unroll=2, row=None):
    per = ktiles // 4 if kind == "token" else 1
    first, group0 = k.chunk, k.group
    used = k.flag("slot_used")
    evac = [n for n, f in (("act_evac", act), ("dve_evac", dve)) if f]
    nk = 4 if kind == "token" else 8
    view = lambda s: s[:, 0:nk * width].rearrange("p (k n) -> p k n", k=nk)
    peel = 2 if group0 == 0 else 0

    @block.tensor
    def _(pe):
        def step(i, j):
            ps = k.pair[(group0 + j) % 2]
            bank_wait(pe, k, i, evac)
            for h in range(per):
                slot = view(slot_wait(pe, first, i * per + h, j * per + h, k))
                if kind == "token":
                    tiles = (1,) if row is not None else range(NT)
                    for kt in range(4):
                        for t in tiles:
                            last = kt == 3 and h == per - 1
                            ins = nc_matmul(k, ps[:, t, 0:width], stationary(4 * h + kt, t, i), slot[:, kt, :],
                                            start=(kt == 0 and h == 0), stop=last and row is None)
                    if row is not None and h == per - 1:
                        ins = nc_matmul(k, ps[:, 1, 0:width], k.c("ones")[0:1, :], row(i), start=False, stop=True)
                else:
                    for b in range(width // P):
                        for kt in range(8):
                            ins = nc_matmul(k, ps[:, 0, b * TOK:(b + 1) * TOK], slot[:, kt, b * P:(b + 1) * P],
                                            moving(kt), start=(kt == 0), stop=(kt == 7))
                ins.then_inc(used.sem, 1)
        repeat(pe, groups, unroll, step, peel=peel)

    for name, fn, dec, per_steps, st in (("act_evac", act, block.scalar, 0, None),
                                         ("dve_evac", dve, block.vector, dve_per, k.dve_steps)):
        if fn is None:
            continue
        s = k.flag(name)

        def program(eng, fn=fn, s=s, per_steps=per_steps, st=st):
            def step(i, j):
                eng.wait_ge(used.sem, i * per + (first + per))
                fn(i, j, k.pair[(group0 + j) % 2]).then_inc(s.sem, 1)
            repeat(eng, groups, unroll, step, peel=peel, steps=st, per=per_steps)
        dec(program)
        s.base += groups
    k.chunk += per * groups
    k.group += groups


def nc_matmul(k, out, lhsT, rhs, start, stop):
    return k.nc.tensor.matmul(out, lhsT, rhs, start=start, stop=stop)


def gated(block, k, conv=None):
    first, group0, n = k.chunk, k.group, NF // 2
    used = k.flag("slot_used")
    dve_evac = k.flag("dve_evac")
    convolved, activated = k.flag("convolved"), k.flag("activated")
    view = lambda s: s[:, :].rearrange("p (k n) -> p k n", k=8)
    nc = k.nc

    @block.tensor
    def _(pe):
        def step(i, j):
            ps = k.pair[(group0 + j) % 2]
            bank_wait(pe, k, i, ["dve_evac"])
            for h in range(2):
                slot = view(slot_wait(pe, first, i * 2 + h, j * 2 + h, k))
                for b in range(2):
                    for kt in range(8):
                        ins = nc_matmul(k, ps[:, h, b * TOK:(b + 1) * TOK], slot[:, kt, b * P:(b + 1) * P],
                                        k.hT[:, kt, :], start=(kt == 0), stop=(kt == 7))
                ins.then_inc(used.sem, 1)
        repeat(pe, n, 2, step, peel=0 if dve_evac.base > 0 else 2)

    @block.scalar
    def _(act):
        def step(i, j):
            y = k.ffn_act[:, j % 2, :]
            if conv:
                act.wait_ge(convolved.sem, i + convolved.at(1))
                nc.scalar.activation(y, k.ffn_conv[:, j % 2, :], ACT.Gelu_apprx_tanh).then_inc(activated.sem, 1)
            else:
                act.wait_ge(used.sem, i * 2 + (first + 1))
                if not isinstance(i, int) or i >= 2:
                    act.wait_ge(dve_evac.sem, i + dve_evac.at(-1))
                nc.scalar.activation(y, k.pair[(group0 + j) % 2][:, 0, :], ACT.Silu).then_inc(activated.sem, 1)
        repeat(act, n, 2, step, peel=0 if conv else 2)

    @block.vector
    def _(dve):
        def step(i, j):
            ps = k.pair[(group0 + j) % 2]
            if conv:
                cw, cb = conv
                dve.wait_ge(used.sem, i * 2 + (first + 1))
                y = k.ffn_conv[:, j % 2, :].rearrange("p (b t) -> p b t", b=2)
                a = ps[:, 0, :].rearrange("p (b t) -> p b t", b=2)
                for b in range(2):
                    w = lambda tap: cw[:, tap, bass.ds(i * 2 + b, 1)]
                    k.dve_steps.did(nc.vector.tensor_scalar(y[:, b, :], a[:, b, :], w(2), cb[:, bass.ds(i * 2 + b, 1)],
                                                            ALU.mult, ALU.add))
                for s in (1, 2):
                    k.dve_steps.settle(dve)
                    for b in range(2):
                        w = cw[:, 2 - s, bass.ds(i * 2 + b, 1)]
                        ins = nc.vector.scalar_tensor_tensor(y[:, b, s:TOK], a[:, b, 0:TOK - s], w, y[:, b, s:TOK],
                                                             ALU.mult, ALU.add)
                        if s == 1:
                            k.dve_steps.did(ins)
                ins.then_inc(convolved.sem, 1)
            dve.wait_ge(used.sem, i * 2 + (first + 2))
            dve.wait_ge(activated.sem, i + activated.at(1))
            out = k.hidden[:, bass.ds(i * 2, 2), :]
            nc.vector.tensor_tensor(out, k.ffn_act[:, j % 2, :].rearrange("p (b t) -> p b t", b=2),
                                    ps[:, 1, :].rearrange("p (b t) -> p b t", b=2), ALU.mult).then_inc(dve_evac.sem, 1)
        repeat(dve, n, 2, step, steps=k.dve_steps, per=4 if conv else 0)
    for s in (dve_evac, activated) + ((convolved,) if conv else ()):
        s.base += n
    k.chunk += 2 * n
    k.group += n


def down(block, k, add):
    first, group0, n = k.chunk, k.group, NF // 2
    used = k.flag("slot_used")
    act_evac, dve_evac = k.flag("act_evac"), k.flag("dve_evac")
    view = lambda s: s[:, :].rearrange("p (k n) -> p k n", k=2)

    @block.tensor
    def _(pe):
        for s in (act_evac, dve_evac):
            if s.base > 0:
                pe.wait_ge(s.sem, s.base)
        for c in range(n):
            slot = view(slot_wait(pe, first, c, c, k))
            for kk in range(2):
                for t in range(NT):
                    for half in range(2):
                        ins = nc_matmul(k, k.pair[half][:, t, :], k.hidden[:, 2 * c + kk, t * P:(t + 1) * P],
                                        slot[:, kk, half * 512:(half + 1) * 512],
                                        start=(c == 0 and kk == 0), stop=(c == n - 1 and kk == 1))
            ins.then_inc(used.sem, 1)

    @block.vector
    def _(dve):
        dve.wait_ge(used.sem, first + n)
        for half in range(2):
            ins = add(dve, half, k.pair[half])
            ins.then_inc(dve_evac.sem, 1)
    dve_evac.base += 2
    k.chunk += n
    k.group += 2


def turn(block, k, src, dst, ntiles):
    turned = k.flag("turned")
    nc = k.nc
    batches = [(t, b) for t in range(NT) for b in range(ntiles // 4)]

    @block.tensor
    def _(pe):
        for n, (t, b) in enumerate(batches):
            if n >= 4:
                pe.wait_ge(k.flag(f"turn_read{n % 2}").sem, k.flag(f"turn_read{n % 2}").at((n - 4) // 2 + 1))
            for i in range(4):
                c = (4 * b + i) * P
                ins = nc.tensor.transpose(k.bank[4 + n % 4][:, i * P:(i + 1) * P], src[:, t, c:c + P], k.c("ident"))
            ins.then_inc(turned.sem, 1)

    def out(eng_op, eng, parity):
        for n, (t, b) in enumerate(batches):
            if n % 2 == parity:
                eng.wait_ge(turned.sem, turned.at(n + 1))
                eng_op(dst[:, 4 * b:4 * b + 4, t * P:(t + 1) * P],
                       k.bank[4 + n % 4][:, :].rearrange("p (b t) -> p b t", b=4)).then_inc(
                           k.flag(f"turn_read{parity}").sem, 1)

    @block.scalar
    def _(act):
        out(nc.scalar.copy, act, 0)

    @block.vector
    def _(dve):
        out(nc.vector.tensor_copy, dve, 1)
    turned.base += len(batches)
    k.flag("turn_read0").base += (len(batches) + 1) // 2
    k.flag("turn_read1").base += len(batches) // 2


def rms_norm(block, k, gain, shift=None, eps=RMS_EPS):
    nc = k.nc
    squared, meaned, rooted = k.flag("squared"), k.flag("meaned"), k.flag("rooted")
    @block.scalar
    def _(act):
        for t in range(NT):
            ins = nc.scalar.activation(k.xn[:, t, :], k.x[:, t, :], ACT.Square, accum_out=k.stat[:, t:t + 1])
        ins.then_inc(squared.sem, 1)
        act.wait_ge(meaned.sem, meaned.at(1))
        nc.scalar.activation(k.stat[:, 4:6], k.stat[:, 2:4], ACT.Sqrt).then_inc(rooted.sem, 1)

    @block.vector
    def _(dve):
        dve.wait_ge(squared.sem, squared.at(1))
        nc.vector.tensor_scalar(k.stat[:, 2:4], k.stat[:, 0:2], 1.0 / D, eps, ALU.mult, ALU.add).then_inc(meaned.sem, 1)
        dve.wait_ge(rooted.sem, rooted.at(1))
        k.dve_steps.did(nc.vector.reciprocal(k.stat[:, 6:8], k.stat[:, 4:6]))
        k.dve_steps.settle(dve)
        for t in range(NT):
            k.dve_steps.did(nc.vector.scalar_tensor_tensor(k.xn[:, t, :], k.x[:, t, :], k.stat[:, 6 + t:7 + t], gain,
                                                           ALU.mult, ALU.mult))
        if shift is not None:
            k.dve_steps.settle(dve)
            for t in range(NT):
                k.dve_steps.did(nc.vector.tensor_tensor(k.xn[:, t, :], k.xn[:, t, :], shift, ALU.add))
    for s in (squared, meaned, rooted):
        s.base += 1
    phase_end(block, k)


class Arena:

    def __init__(self, tile, size):
        self.tile, self.size, self.at = tile, size, 0

    def take(self, *shape):
        n = int(np.prod(shape))
        assert self.at + n <= self.size, (self.at, n, self.size)
        v = self.tile[:, self.at:self.at + n]
        self.at += n
        if len(shape) == 1:
            return v
        names = "abcd"[:len(shape)]
        return v.rearrange("p (" + " ".join(names) + ") -> p " + " ".join(names),
                           **{c: m for c, m in zip(names, shape)})


def attention(block, k, qkv, yT):
    nc = k.nc
    a = k.arena
    mark = a.at
    rot = a.take(NT, 2 * WIDTH)
    qkT = a.take(2 * NB, TOK)
    S = a.take(HEADS, NT, TOK)
    part = a.take(NT, 2, 16, 32)
    PT = S
    PT = a.take(HEADS, 384)
    mx, tot, rec = k.mx, k.tot, k.rec
    scored, took, maxed, powered = (k.flag(n) for n in ("scored", "score_read", "maxed", "powered"))
    scaled = [k.flag("scaled_act"), k.flag("scaled_dve")]
    pturned, pread = k.flag("probs_turned"), [k.flag("probs_read_act"), k.flag("probs_read_dve")]
    mixed, yread, rec_ready = k.flag("mixed"), k.flag("mixed_read"), k.flag("recip_ready")
    units = [(h, t) for h in range(HEADS) for t in range(NT)]

    def rotate(op, steps, eng, t):
        src = qkv[:, t, 0:2 * WIDTH].rearrange("p (h x d) -> p x h d", h=16, x=2)
        dst = rot[:, t, :].rearrange("p (h x d) -> p x h d", h=16, x=2)
        cos = k.cos[:, t, :].unsqueeze(1).to_broadcast([P, 16, 32])
        sin = k.sin[:, t, :].unsqueeze(1).to_broadcast([P, 16, 32])
        for x, second in ((0, ALU.subtract), (1, ALU.add)):
            steps.did(op(part[:, t, 0], src[:, x], cos, ALU.mult))
            steps.did(op(part[:, t, 1], src[:, 1 - x], sin, ALU.mult))
            steps.settle(eng)
            steps.did(op(dst[:, x], part[:, t, 0], part[:, t, 1], second))
            steps.settle(eng)

    @block.vector
    def _(dve):
        rotate(nc.vector.tensor_tensor, k.dve_steps, dve, 0)

    @block.gpsimd
    def _(pool):
        rotate(nc.gpsimd.tensor_tensor, k.pool_steps, pool, 1)
    phase_end(block, k)
    turn(block, k, rot, qkT, 2 * NB)
    phase_end(block, k)

    def mix(pe, h):
        pe.wait_ge(pread[h % 2].sem, pread[h % 2].at(h // 2 + 1))
        b = h // 2
        if h % 2 == 0 and b >= 2:
            pe.wait_ge(yread.sem, yread.at(b - 1))
        o = k.bank[4 + b % 2][64 * (h % 2):64 * (h % 2) + 64, 0:TOK]
        v = lambda s: qkv[:, s, 2 * WIDTH + h * DH:2 * WIDTH + (h + 1) * DH]
        nc_matmul(k, o, v(0), PT[:, h, 0:TOK], True, False)
        nc_matmul(k, o[:, P:TOK], v(1), PT[:, h, TOK:384], False, True).then_inc(mixed.sem, 1)

    def out(act, b):
        act.wait_ge(mixed.sem, mixed.at(2 * b + 2))
        nc.scalar.copy(yT[:, b, :], k.bank[4 + b % 2][:, 0:TOK]).then_inc(yread.sem, 1)
    @block.tensor
    def _(pe):
        for u, (h, t) in enumerate(units):
            if u >= 2:
                pe.wait_ge(took.sem, took.at(u - 1))
            p0, n = 64 * (h % 2), (t + 1) * P
            nc_matmul(k, k.bank[4 + u % 2][:, 0:n], qkT[p0:p0 + 64, h // 2, t * P:(t + 1) * P],
                      qkT[p0:p0 + 64, NB + h // 2, 0:n], True, True).then_inc(scored.sem, 1)
        for h in range(HEADS):
            pe.wait_ge(scaled[h % 2].sem, scaled[h % 2].at(h // 2 + 1))
            if h >= 2:
                pe.wait_ge(pread[h % 2].sem, pread[h % 2].at(h // 2))
            for i, (t, s) in enumerate(((0, 0), (1, 0), (1, 1))):
                ins = nc.tensor.transpose(k.bank[6 + h % 2][:, i * P:(i + 1) * P], S[:, h, t, s * P:(s + 1) * P],
                                          k.c("ident"))
            ins.then_inc(pturned.sem, 1)
            if h >= 1:
                mix(pe, h - 1)
        mix(pe, HEADS - 1)

    @block.vector
    def _(dve):
        for u in range(len(units) + 3):
            if u < len(units):
                h, t = units[u]
                n = (t + 1) * P
                dve.wait_ge(scored.sem, scored.at(u + 1))
                nc.vector.scalar_tensor_tensor(S[:, h, t, 0:n], k.bank[4 + u % 2][:, 0:n], DH ** -0.5,
                                               k.blocked[:, t, 0:n], ALU.mult, ALU.add).then_inc(took.sem, 1)
            if 1 <= u <= len(units):
                h, t = units[u - 1]
                dve.wait_ge(took.sem, took.at(u))
                nc.vector.tensor_reduce(mx[:, u - 1:u], S[:, h, t, 0:(t + 1) * P], AX.X, ALU.max,
                                        negate=True).then_inc(maxed.sem, 1)
            if u >= 3:
                h, t = units[u - 3]
                n = (t + 1) * P
                dve.wait_ge(powered.sem, powered.at(u - 2))
                k.dve_steps.did(nc.vector.scalar_tensor_tensor(
                    S[:, h, t, 0:n], S[:, h, t, 0:n], 1.0, k.count[:, t, 0:n], ALU.mult, ALU.mult,
                    accum_out=tot[:, u - 3:u - 2]))
        k.dve_steps.settle(dve)
        nc.vector.reciprocal(rec[:, 0:16], tot[:, 0:16]).then_inc(rec_ready.sem, 1)
        dve.wait_ge(rec_ready.sem, rec_ready.at(1))
        for h in range(1, HEADS, 2):
            for t in range(NT):
                n = (t + 1) * P
                ins = nc.vector.tensor_scalar(S[:, h, t, 0:n], S[:, h, t, 0:n], rec[:, 2 * h + t:2 * h + t + 1], None,
                                              ALU.mult)
            ins.then_inc(scaled[1].sem, 1)
        for h in range(1, HEADS, 2):
            dve.wait_ge(pturned.sem, pturned.at(h + 1))
            nc.vector.tensor_copy(PT[:, h, :], k.bank[6 + h % 2][:, 0:384]).then_inc(pread[1].sem, 1)

    @block.scalar
    def _(act):
        for u, (h, t) in enumerate(units):
            n = (t + 1) * P
            act.wait_ge(maxed.sem, maxed.at(u + 1))
            nc.scalar.activation(S[:, h, t, 0:n], S[:, h, t, 0:n], ACT.Exp, bias=mx[:, u:u + 1]).then_inc(powered.sem, 1)
        act.wait_ge(rec_ready.sem, rec_ready.at(1))
        for h in range(0, HEADS, 2):
            for t in range(NT):
                n = (t + 1) * P
                ins = nc.scalar.activation(S[:, h, t, 0:n], S[:, h, t, 0:n], ACT.Copy,
                                           scale=rec[:, 2 * h + t:2 * h + t + 1])
            ins.then_inc(scaled[0].sem, 1)
        for h in range(0, HEADS, 2):
            act.wait_ge(pturned.sem, pturned.at(h + 1))
            nc.scalar.copy(PT[:, h, :], k.bank[6 + h % 2][:, 0:384]).then_inc(pread[0].sem, 1)
            if h >= 2:
                out(act, h // 2 - 1)
        out(act, NB - 1)

    for s, n in ((scored, 16), (took, 16), (maxed, 16), (powered, 16), (rec_ready, 1), (scaled[0], 4), (scaled[1], 4),
                 (pturned, 8), (pread[0], 4), (pread[1], 4), (mixed, 8), (yread, 4)):
        s.base += n
    phase_end(block, k)
    a.at = mark


def turn_back(block, k, src, dst):
    turned, read = k.flag("turned"), k.flag("turn_read0")
    nc = k.nc

    @block.tensor
    def _(pe):
        for t in range(NT):
            for b in range(NB):
                ins = nc.tensor.transpose(k.bank[4 + t][:, b * P:(b + 1) * P], src[:, b, t * P:(t + 1) * P], k.c("ident"))
            ins.then_inc(turned.sem, 1)

    @block.scalar
    def _(act):
        for t in range(NT):
            act.wait_ge(turned.sem, turned.at(t + 1))
            nc.scalar.copy(dst[:, t, :], k.bank[4 + t][:, :]).then_inc(read.sem, 1)
    turned.base += NT
    read.base += NT
    phase_end(block, k)


def rwkv(block, k, zT, wide, scratch, keep, yT):
    nc, v = k.nc, k.nc.vector
    steps = k.dve_steps
    AR, BT, KT, g, bonus, Btok, Ktok, Vtok, y, S, W, U, ends = keep
    T2, T3, T4, small = scratch
    T0, T1, T5 = (flat4(x) for x in (k.xn[:, 0, :], k.xn[:, 1, :], y))
    T2, T3, T4 = flat4(T2), flat4(T3), flat4(T4)
    T0f = k.xn[:, 0, :]
    diff = k.arena.tile[:, k.tok_at:k.tok_at + NZ * TOK].rearrange("p (b t) -> p b t", t=TOK)
    R, K, V = zT[:, 0:4, :], zT[:, 4:8, :], zT[:, 8:12, :]
    th, sgx = small[:, 0:TOK], small[:, TOK:2 * TOK]
    lora, g_up = wide[:, 0:WIDTH], wide[:, WIDTH:2 * WIDTH]
    big = k.big
    four = lambda i: flat4(big[i])
    blk = lambda name, b: k.col[name][:, b:b + 1]

    @block.gpsimd
    def _(pool):
        nc.gpsimd.tensor_tensor(diff[:, 0:7, 1:TOK], zT[:, 0:7, 0:TOK - 1], zT[:, 0:7, 1:TOK], ALU.subtract)
        nc.gpsimd.tensor_scalar(diff[:, 0:7, 0:1], zT[:, 0:7, 0:1], -1.0, None, ALU.mult)

    @block.vector
    def _(dve):
        v.tensor_tensor(diff[:, 7:NZ, 1:TOK], zT[:, 7:NZ, 0:TOK - 1], zT[:, 7:NZ, 1:TOK], ALU.subtract)
        v.tensor_scalar(diff[:, 7:NZ, 0:1], zT[:, 7:NZ, 0:1], -1.0, None, ALU.mult)
    phase_end(block, k)

    @block.vector
    def _(dve):
        for b in list(range(12, NZ)) + list(range(12)):
            v.scalar_tensor_tensor(zT[:, b, :], diff[:, b, :], k.col["mu"][:, b:b + 1], zT[:, b, :], ALU.mult, ALU.add)
    phase_end(block, k)

    @block.scalar
    def _(act):
        nc.scalar.activation(th[0:64, :], zT[0:64, 12, :], ACT.Tanh)
        nc.scalar.activation(sgx, zT[:, 13, :], ACT.Sigmoid)
    phase_end(block, k)

    @block.tensor
    def _(pe):
        for t in range(NT):
            o = big[0][:, t * WIDTH:(t + 1) * WIDTH]
            nc_matmul(k, o, th[0:64, t * P:(t + 1) * P], lora[0:64, :], True, False)
            nc_matmul(k, o, k.c("ones")[0:1, :], k.w0[0:1, :], False, True)
        for b in range(NB):
            nc_matmul(k, big[1][:, b * TOK:(b + 1) * TOK], lora[64:P, b * P:(b + 1) * P], zT[64:P, 12, :], True, True)
            nc_matmul(k, big[2][:, b * TOK:(b + 1) * TOK], g_up[:, b * P:(b + 1) * P], sgx, True, True)
    phase_end(block, k)

    @block.scalar
    def _(act):
        nc.scalar.activation(T0f, big[0], ACT.Sigmoid)
        for b in range(NB):
            nc.scalar.activation(T1[:, b, :], four(1)[:, b, :], ACT.Sigmoid, bias=blk("a0", b))

    @block.vector
    def _(dve):
        v.tensor_copy(g, big[2])
        for b in range(NB):
            steps.did(v.tensor_scalar(T5[:, b, :], K[:, b, :], blk("k_k", b), None, ALU.mult))
    phase_end(block, k)

    @block.tensor
    def _(pe):
        for n, m in ((0, "incl_up"), (1, "strict_up")):
            for b in range(NB):
                for t in range(NT):
                    nc_matmul(k, four(n)[:, b, t * P:(t + 1) * P], T0f[:, t * WIDTH + b * P:t * WIDTH + (b + 1) * P],
                              k.c(m), True, True)

    @block.vector
    def _(dve):
        v.tensor_tensor(diff[:, 0:4, :], T5, T5, ALU.mult)
        for b in range(NB):
            steps.did(v.tensor_scalar(diff[:, 4 + b, :], T1[:, b, :], -1.0, blk("k_a", b), ALU.add, ALU.mult))
        steps.settle(dve)
        v.scalar_tensor_tensor(K, diff[:, 4:8, :], 1.0, K, ALU.add, ALU.mult)
    phase_end(block, k)

    @block.tensor
    def _(pe):
        for half in range(2):
            nc_matmul(k, big[2][:, half * 512:(half + 1) * 512], k.c("blockones"),
                      diff[:, 2 * half:2 * half + 2, :].rearrange("p b t -> p (b t)"), True, True)

    @block.scalar
    def _(act):
        nc.scalar.activation(T2, four(0), ACT.Exp, scale=-DECAY)
        nc.scalar.activation(T3, four(0), ACT.Exp, scale=DECAY)
        nc.scalar.activation(T4, four(1), ACT.Exp, scale=-DECAY)

    @block.vector
    def _(dve):
        steps.did(v.tensor_tensor(T0, R, K, ALU.mult))
        steps.settle(dve)
        for b in range(NB):
            v.tensor_scalar(T0[:, b, :], T0[:, b, :], blk("r_k", b), None, ALU.mult)
    phase_end(block, k)

    @block.tensor
    def _(pe):
        for half in range(2):
            nc_matmul(k, big[3][:, half * 512:(half + 1) * 512], k.c("blockones"), T0f[:, half * 512:(half + 1) * 512],
                      True, True)

    @block.scalar
    def _(act):
        nc.scalar.activation(diff[:, 4:8, :], four(2), ACT.Sqrt)

    @block.gpsimd
    def _(pool):
        nc.gpsimd.tensor_copy(ends, T2[:, :, CHUNK - 1:TOK:CHUNK])
        nc.gpsimd.tensor_tensor(AR[:, :, 1, :], R, T2, ALU.mult)
        nc.gpsimd.tensor_tensor(KT, K, T3, ALU.mult)
    phase_end(block, k)

    @block.vector
    def _(dve):
        v.tensor_tensor(flat4(bonus), four(3), V, ALU.mult)
        steps.did(v.tensor_scalar(diff[:, 4:8, :], diff[:, 4:8, :], 1e-12, None, ALU.max))
        steps.settle(dve)
        steps.did(v.reciprocal(diff[:, 4:8, :], diff[:, 4:8, :]))
        steps.settle(dve)
        steps.did(v.tensor_tensor(T5, T5, diff[:, 4:8, :], ALU.mult))
        steps.settle(dve)
        v.scalar_tensor_tensor(AR[:, :, 0, :], T5, -1.0, T4, ALU.mult, ALU.mult)
        steps.did(v.tensor_tensor(T1, T5, T1, ALU.mult))
        steps.settle(dve)
        v.tensor_tensor(BT, T1, T3, ALU.mult)
    phase_end(block, k)
    for src, dst in ((BT, Btok), (KT, Ktok), (V, Vtok)):
        turn_back(block, k, src, dst)

    @block.vector
    def _(dve):
        v.memset(S[:, 0], 0.0)
    phase_end(block, k)
    wide8 = lambda x: x.rearrange("p (h t) -> p h t", h=HEADS)
    L, AK, RB, RK, Z, X, T = (k.arena.tile[:, k.gram_at + n * D:k.gram_at + (n + 1) * D] for n in range(7))
    over = lambda m: k.c(m).unsqueeze(1).to_broadcast([P, HEADS, P])

    for t in range(NT):
        tt = slice(t * P, (t + 1) * P)
        head = lambda h: slice(64 * (h % 2), 64 * (h % 2) + 64)
        A_ = lambda h: AR[head(h), h // 2, 0, tt]
        R_ = lambda h: AR[head(h), h // 2, 1, tt]
        B_ = lambda h: BT[head(h), h // 2, tt]
        K_ = lambda h: KT[head(h), h // 2, tt]
        hp = lambda h: slice(((h % 2) * NB + h // 2) * P, ((h % 2) * NB + h // 2 + 1) * P)

        def gram(pairs):
            @block.tensor
            def _(pe):
                for n, (lhs, rhs) in enumerate(pairs):
                    for h in range(HEADS):
                        nc_matmul(k, big[n][:, hp(h)], lhs(h), rhs(h), True, True)
            phase_end(block, k)
        gram([(B_, A_), (A_, B_), (K_, A_), (B_, R_)])

        @block.vector
        def _(dve):
            steps.did(v.tensor_tensor(wide8(Z), wide8(big[0]), over("level0"), ALU.mult))
            v.tensor_tensor(wide8(L), wide8(big[1]), over("strict_lo"), ALU.mult)
            steps.did(v.tensor_tensor(wide8(X), wide8(big[1]), over("lower0"), ALU.mult))
            v.tensor_tensor(wide8(AK), wide8(big[2]), over("strict_up"), ALU.mult)
            v.tensor_tensor(wide8(RB), wide8(big[3]), over("incl_up"), ALU.mult)
            steps.settle(dve)
            v.tensor_tensor(wide8(Z), wide8(Z), over("ident"), ALU.add)
            v.tensor_tensor(wide8(X), wide8(X), over("ident"), ALU.add)
        phase_end(block, k)
        gram([(K_, R_)])

        @block.vector
        def _(dve):
            v.tensor_tensor(wide8(RK), wide8(big[0]), over("incl_up"), ALU.mult)
        phase_end(block, k)
        for level in range(1, 6):
            @block.tensor
            def _(pe):
                for h in range(HEADS):
                    nc_matmul(k, big[1][:, hp(h)], L[:, hp(h)], Z[:, hp(h)], True, True)
            phase_end(block, k)

            @block.vector
            def _(dve):
                v.tensor_tensor(wide8(T), wide8(big[1]), over(f"level{level}"), ALU.mult)
            phase_end(block, k)

            @block.tensor
            def _(pe):
                for h in range(HEADS):
                    nc_matmul(k, big[2][:, hp(h)], X[:, hp(h)], T[:, hp(h)], True, True)
                    if level < 5:
                        nc_matmul(k, big[3][:, hp(h)], T[:, hp(h)], X[:, hp(h)], True, True)
            phase_end(block, k)

            @block.vector
            def _(dve):
                v.tensor_tensor(Z, Z, big[2], ALU.add)
                if level < 5:
                    v.tensor_tensor(X, X, big[3], ALU.add)
            phase_end(block, k)
        hv = lambda h: slice(h * DH, (h + 1) * DH)
        AV = k.xn[:, 0, 0:WIDTH]
        yt = flat4(y)[:, :, tt]

        @block.tensor
        def _(pe):
            for h in range(HEADS):
                nc_matmul(k, k.bank[7][:, hv(h)], AK[:, hp(h)], Vtok[:, t, hv(h)], True, True)
        phase_end(block, k)

        @block.scalar
        def _(act):
            nc.scalar.copy(AV, k.bank[7])
        phase_end(block, k)
        for c in (2 * t, 2 * t + 1):
            p0 = 64 * (c % 2)
            rows = slice(p0, p0 + 64)
            now, nxt = S[:, c % 2], S[:, (c + 1) % 2]
            cc = slice(c * CHUNK, (c + 1) * CHUNK)
            inner = lambda h: slice(hp(h).start + p0, hp(h).start + p0 + 64)

            @block.tensor
            def _(pe):
                for h in range(HEADS):
                    nc_matmul(k, k.bank[h % 2][rows, (h // 2) * DH:(h // 2 + 1) * DH], AR[head(h), h // 2, 0, cc],
                              now[head(h), h // 2, :], True, True)
            phase_end(block, k)

            @block.vector
            def _(dve):
                pairs = lambda x: x[rows, :].rearrange("p (b x d) -> p x b d", x=2, d=DH)
                for x in range(2):
                    v.tensor_tensor(pairs(W)[:, x], k.bank[x][rows, 0:256].rearrange("p (b d) -> p b d", d=DH),
                                    pairs(AV)[:, x], ALU.add)
            phase_end(block, k)

            @block.tensor
            def _(pe):
                for h in range(HEADS):
                    nc_matmul(k, k.bank[2][rows, hv(h)], Z[rows, inner(h)], W[rows, hv(h)], True, True)
            phase_end(block, k)

            @block.vector
            def _(dve):
                v.tensor_copy(U[rows, :], k.bank[2][rows, :])
            phase_end(block, k)

            @block.tensor
            def _(pe):
                for h in range(HEADS):
                    o = k.bank[4][head(h), (h // 2) * 64:(h // 2) * 64 + 64]
                    nc_matmul(k, o, Btok[rows, t, hv(h)], U[rows, hv(h)], True, False)
                    nc_matmul(k, o, Ktok[rows, t, hv(h)], Vtok[rows, t, hv(h)], False, True)
                for h in range(HEADS):
                    nc_matmul(k, k.bank[6][head(h), (h // 2) * 64:(h // 2) * 64 + 64], now[head(h), h // 2, :],
                              AR[head(h), h // 2, 1, cc], True, True)
            phase_end(block, k)

            @block.vector
            def _(dve):
                sf = lambda x: x.rearrange("p b t -> p (b t)")
                steps.did(v.tensor_tensor(sf(nxt), sf(now), k.bank[4][:, 0:256], ALU.add))
                steps.settle(dve)
                v.tensor_tensor(nxt, nxt, ends[:, :, c:c + 1].to_broadcast([P, NB, 64]), ALU.mult)

            @block.scalar
            def _(act):
                nc.scalar.copy(flat4(y)[:, :, cc], k.bank[6][:, 0:256].rearrange("p (b t) -> p b t", b=NB))
            phase_end(block, k)

        @block.tensor
        def _(pe):
            for h in range(HEADS):
                o = k.bank[7][head(h), (h // 2) * P:(h // 2 + 1) * P]
                nc_matmul(k, o, U[:, hv(h)], RB[:, hp(h)], True, False)
                nc_matmul(k, o, Vtok[:, t, hv(h)], RK[:, hp(h)], False, True)
        phase_end(block, k)

        @block.vector
        def _(dve):
            v.tensor_tensor(yt, yt, flat4(k.bank[7]), ALU.add)
        phase_end(block, k)

    def head_sum(x):
        @block.tensor
        def _(pe):
            for half in range(2):
                nc_matmul(k, big[0][:, half * 512:(half + 1) * 512], k.c("blockones"), x[:, half * 512:(half + 1) * 512],
                          True, True)
        phase_end(block, k)
    head_sum(y)

    @block.vector
    def _(dve):
        steps.did(v.scalar_tensor_tensor(y, big[0], -1.0 / DH, y, ALU.mult, ALU.add))
        steps.settle(dve)
        v.tensor_tensor(T0f, y, y, ALU.mult)
    phase_end(block, k)
    head_sum(T0f)

    @block.vector
    def _(dve):
        v.tensor_scalar(T0f, big[0], 1.0 / DH, GN_EPS, ALU.mult, ALU.add)
    phase_end(block, k)

    @block.scalar
    def _(act):
        nc.scalar.activation(T0f, T0f, ACT.Sqrt)
    phase_end(block, k)

    @block.vector
    def _(dve):
        steps.did(v.reciprocal(T0f, T0f))
        steps.settle(dve)
        steps.did(v.tensor_tensor(y, y, T0f, ALU.mult))
        steps.settle(dve)
        for b in range(NB):
            steps.did(v.tensor_scalar(flat4(y)[:, b, :], flat4(y)[:, b, :], blk("gn_w", b), blk("gn_b", b), ALU.mult, ALU.add))
        steps.settle(dve)
        steps.did(v.tensor_tensor(y, y, bonus, ALU.add))
        steps.settle(dve)
        v.tensor_tensor(yT, flat4(y), flat4(g), ALU.mult)
    phase_end(block, k)


def flat4(x):
    return x.rearrange("p (b t) -> p b t", b=NB)


def gmlp(block, k, uv, w_s, yT):
    nc, v = k.nc, k.nc.vector
    steps = k.dve_steps
    ln_g, ln_b = k.spread[:, 2 * D:2 * D + WIDTH], k.spread[:, 2 * D + WIDTH:2 * D + 2 * WIDTH]
    vv = lambda t: uv[:, t, WIDTH:2 * WIDTH]

    @block.gpsimd
    def _(pool):
        nc.gpsimd.tensor_tensor(w_s.rearrange("p (g i) -> p g i", g=HEADS), w_s.rearrange("p (g i) -> p g i", g=HEADS),
                                k.c("upper").unsqueeze(1).to_broadcast([P, HEADS, P]), ALU.mult)

    @block.vector
    def _(dve):
        for t in range(NT):
            steps.did(v.tensor_reduce(k.stat[:, t:t + 1], vv(t), AX.X, ALU.add))
        steps.settle(dve)
        steps.did(v.tensor_scalar(k.stat[:, 2:4], k.stat[:, 0:2], -1.0 / WIDTH, None, ALU.mult))
        steps.settle(dve)
        for t in range(NT):
            v.tensor_scalar(vv(t), vv(t), k.stat[:, 2 + t:3 + t], None, ALU.add)
    phase_end(block, k)

    @block.scalar
    def _(act):
        for t in range(NT):
            nc.scalar.activation(k.xn[:, t, 0:WIDTH], vv(t), ACT.Square, accum_out=k.stat[:, t:t + 1])
    phase_end(block, k)

    @block.vector
    def _(dve):
        v.tensor_scalar(k.stat[:, 2:4], k.stat[:, 0:2], 1.0 / WIDTH, LN_EPS, ALU.mult, ALU.add)
    phase_end(block, k)

    @block.scalar
    def _(act):
        nc.scalar.activation(k.stat[:, 4:6], k.stat[:, 2:4], ACT.Sqrt)
    phase_end(block, k)

    @block.vector
    def _(dve):
        steps.did(v.reciprocal(k.stat[:, 6:8], k.stat[:, 4:6]))
        steps.settle(dve)
        for t in range(NT):
            steps.did(v.scalar_tensor_tensor(vv(t), vv(t), k.stat[:, 6 + t:7 + t], ln_g, ALU.mult, ALU.mult))
        steps.settle(dve)
        for t in range(NT):
            v.tensor_tensor(vv(t), vv(t), ln_b, ALU.add)
    phase_end(block, k)

    @block.tensor
    def _(pe):
        for t in range(NT):
            for g in range(HEADS):
                nc_matmul(k, k.bank[4 + t][:, g * 64:(g + 1) * 64], w_s[:, g * P:(g + 1) * P],
                          uv[:, t, WIDTH + g * 64:WIDTH + (g + 1) * 64], True, True)
    phase_end(block, k)

    @block.vector
    def _(dve):
        for t in range(NT):
            for g in range(HEADS):
                u = uv[:, t, g * 64:(g + 1) * 64]
                v.scalar_tensor_tensor(u, k.bank[4 + t][:, g * 64:(g + 1) * 64], k.col["b_s"][:, g:g + 1], u, ALU.add,
                                       ALU.mult)
    phase_end(block, k)
    turn(block, k, uv, yT, NB)
    phase_end(block, k)


def chunk_arrays():
    def tiles(m):
        return m.reshape(-1, P, m.shape[1]).transpose(1, 0, 2).reshape(P, SLOT)

    def token(m, kt=4):
        n = SLOT // kt
        return [tiles(m[r:r + kt * P, c:c + n]) for c in range(0, m.shape[1], n) for r in range(0, m.shape[0], kt * P)]

    def channel(m):
        return token(m, 8)

    def ffn(a, g):
        return [x for pair in zip(channel(a), channel(g)) for x in pair]

    def rows(m):
        return [tiles(m[r:r + 2 * P]) for r in range(0, m.shape[0], 2 * P)]
    return token, channel, ffn, rows


def first_stream(v, l):
    token, channel, ffn, rows = chunk_arrays()
    w = v["w_in"][l]
    out = token(v["w_ada"][l]) + token(w[:, :RWKV0]) + channel(w[:, RWKV0:UV0]) + token(w[:, UV0:])
    out += [c for n in range(3) for c in token(v["w_branch"][l, n])] + token(v["w_out"][l])
    out += ffn(v["ffn_w_up"][l][:, :D_FF], v["ffn_w_up"][l][:, D_FF:]) + rows(v["ffn_w_down"][l])
    return np.stack(out)


FIRST_COLS = {"c": KD, "mu": NZ, "a0": NB, "k_k": NB, "k_a": NB, "r_k": NB, "gn_w": NB, "gn_b": NB,
              "conv_w": 3 * NF, "conv_b": NF, "b_s": HEADS}
FIRST_WIDE = {"lora": WIDTH, "g_up": WIDTH, "w_s": HEADS * P}


def first_small(v, l):
    col = lambda a: a.reshape(-1, P).T
    cols = [col(v["c"][0]), col(v["rwkv_mu"][l]), col(v["rwkv_a0"][l]), col(v["rwkv_k_k"][l]), col(v["rwkv_k_a"][l]),
            col(v["rwkv_r_k"][l].reshape(-1)), col(v["rwkv_gn_w"][l]), col(v["rwkv_gn_b"][l]),
            col(v["ffn_conv_w"][l].reshape(-1)), col(v["ffn_conv_b"][l]), v["gmlp_b_s"][l].T]
    wide = [np.concatenate([v["rwkv_w_up"][l], v["rwkv_a_up"][l]]), v["rwkv_g_up"][l],
            v["gmlp_w_s"][l].transpose(2, 0, 1).reshape(P, -1)]
    rows = [v["b_ada"][l], v["rwkv_w0"][l]]
    spread = [v["norm_mix"][l], v["norm_ffn"][l], v["gmlp_ln_g"][l], v["gmlp_ln_b"][l]]
    return [np.concatenate(cols, 1), np.concatenate(wide, 1), np.concatenate(rows), np.concatenate(spread)]


def columns(tile, sizes):
    out, at = {}, 0
    for name, n in sizes.items():
        out[name] = tile[:, at:at + n]
        at += n
    return out


def first_layer(block, k, A, l):
    nc = k.nc
    a = k.arena
    a.at = 0
    mod = a.take(6, D)
    yT = a.take(3 * NB, TOK)
    body = a.at
    small = k.flag("small_landed")
    spread = k.spread
    rowb = a.take(6 * D)
    cact, cb = a.take(KD), a.take(KD, P)
    row = lambda name: A[name][bass.ds(l, 1)]
    stream(block, k, A["stream1"][bass.ds(l, 1)].rearrange("a c p n -> (a c) p n"), k.chunks)

    @block.scalar
    def _(act):
        for dst, src in ((k.cols1[:], row("cols1").rearrange("a p n -> (a p) n")),
                         (rowb[0:1, :], row("rows1")[:, 0:6 * D]), (k.w0[0:1, :], row("rows1")[:, 6 * D:6 * D + WIDTH]),
                         (spread[:], row("spread1").partition_broadcast(P).rearrange("p a n -> p (a n)"))):
            act.dma_start(dst, src).then_inc(small.sem, 16)
        act.wait_ge(small.sem, 64)
        nc.scalar.activation(cact, k.col["c"], ACT.Silu).then_inc(k.flag("c_ready").sem, 1)

    @block.vector
    def _(dve):
        dve.wait_ge(k.flag("c_ready").sem, 1)
        for kt in range(KD):
            nc.vector.tensor_scalar(cb[:, kt, :], k.c("ones"), cact[:, kt:kt + 1], None, ALU.mult)
    small.base += 64
    k.flag("c_ready").base += 1
    phase_end(block, k)
    product(block, k, "token", 512, 12,
            stationary=lambda kt, t, i: cb[:, kt, :], row=lambda i: rowb[0:1, bass.ds(i * 512, 512)],
            dve=lambda i, j, ps: nc.vector.tensor_copy(mod_flat(k)[:, bass.ds(i * 512, 512)], ps[:, 1, :]))
    phase_end(block, k)

    @block.vector
    def _(dve):
        for sc, n in ((1, 0), (4, 1)):
            ins = nc.vector.scalar_tensor_tensor(mod[:, sc, :], mod[:, sc, :], 1.0, spread[:, n * D:(n + 1) * D], ALU.add,
                                                 ALU.mult)
            k.dve_steps.did(ins)
        k.dve_steps.settle(dve)
    rms_norm(block, k, mod[:, 1, :], mod[:, 0, :])
    turn(block, k, k.xn, k.hT, KD)
    phase_end(block, k)
    a.at = body
    tok = lambda kt, t, i: k.hT[:, kt, t * P:(t + 1) * P]
    att = a.take(NT, 3 * WIDTH)
    product(block, k, "token", 512, 3, stationary=tok,
            act=lambda i, j, ps: nc.scalar.copy(att[:, 0, i * 512:(i + 1) * 512], ps[:, 0, :]),
            dve=lambda i, j, ps: nc.vector.tensor_copy(att[:, 1, i * 512:(i + 1) * 512], ps[:, 1, :]))
    phase_end(block, k)
    attention(block, k, att, yT)
    k.yT = yT
    a.at = body
    AR = a.take(NB, 2, TOK)
    BT, KT = a.take(NB, TOK), a.take(NB, TOK)
    g, bonus = a.take(D), a.take(D)
    k.tok_at = a.at
    Btok, Ktok, Vtok = (a.take(NT, WIDTH) for _ in range(3))
    y = a.take(D)
    S, W, U, ends = a.take(2, NB, 64), a.take(WIDTH), a.take(WIDTH), a.take(NB, NCH)
    k.gram_at = a.at
    zT = a.take(NZ, TOK)
    lora = a.take(2 * WIDTH)
    scratch = [a.take(D), a.take(D), a.take(D), a.take(2 * TOK)]
    assert k.gram_at + 7 * D <= a.size

    @block.scalar
    def _(act):
        act.dma_start(lora, row("wide1")[:, :, 0:2 * WIDTH].rearrange("a p n -> (a p) n")).then_inc(small.sem, 16)
    small.base += 16
    zcopy = lambda f: lambda i, j, ps: f(zT[:, 2 * i:2 * i + 2, :].rearrange("p b t -> p (b t)"), ps[:, 0, :])
    product(block, k, "channel", 256, NZ // 2, moving=lambda kt: k.hT[:, kt, :], unroll=8, act=zcopy(nc.scalar.copy))

    @block.tensor
    def _(pe):
        pe.wait_ge(small.sem, small.base)
    phase_end(block, k)
    rwkv(block, k, zT, lora, scratch, (AR, BT, KT, g, bonus, Btok, Ktok, Vtok, y, S, W, U, ends), yT[:, NB:2 * NB, :])
    a.at = body
    uv = a.take(NT, 2 * WIDTH)
    w_s = a.take(HEADS * P)

    @block.scalar
    def _(act):
        act.dma_start(w_s, row("wide1")[:, :, 2 * WIDTH:].rearrange("a p n -> (a p) n")).then_inc(small.sem, 16)
        act.wait_ge(small.sem, small.base + 16)
    small.base += 16

    both = token_out_dyn
    product(block, k, "token", 512, 2, stationary=tok,
            act=both(lambda o, i: nc.scalar.activation(o, i, ACT.Gelu_apprx_tanh), uv))
    phase_end(block, k)
    gmlp(block, k, uv, w_s, yT[:, 2 * NB:, :])
    a.at = body
    gates = a.take(NT, 3 * D)
    product(block, k, "token", 512, 6, stationary=tok, act=both(lambda o, i: nc.scalar.activation(o, i, ACT.Sigmoid), gates))
    phase_end(block, k)
    product(block, k, "token", 512, 6, ktiles=4, unroll=4,
            stationary=lambda kt, t, i: yT[:, (i // 2) * NB + kt, t * P:(t + 1) * P],
            dve=both(lambda o, i: nc.vector.tensor_tensor(o, o, i, ALU.mult), gates))
    phase_end(block, k)

    def merge(op, steps, eng, t):
        for n in (1, 2):
            steps.did(op(gates[:, t, 0:D], gates[:, t, 0:D], gates[:, t, n * D:(n + 1) * D], ALU.add))
            steps.settle(eng)

    @block.vector
    def _(dve):
        merge(nc.vector.tensor_tensor, k.dve_steps, dve, 0)

    @block.gpsimd
    def _(pool):
        merge(nc.gpsimd.tensor_tensor, k.pool_steps, pool, 1)
    phase_end(block, k)
    turn(block, k, gates, k.hT, KD)
    phase_end(block, k)
    product(block, k, "token", 512, 2, stationary=tok, dve=lambda i, j, ps: gated_add(k, i, ps, mod[:, 2, :]))
    phase_end(block, k)
    rms_norm(block, k, mod[:, 4, :], mod[:, 3, :])
    turn(block, k, k.xn, k.hT, KD)
    phase_end(block, k)
    a.at = body
    k.hidden, k.ffn_act, k.ffn_conv = a.take(NF, TOK), a.take(2, 512), a.take(2, 512)
    gated(block, k, conv=(k.col["conv_w"].rearrange("p (j b) -> p j b", j=3), k.col["conv_b"]))
    phase_end(block, k)
    down(block, k, lambda dve, half, ps: gated_add(k, half, ps, mod[:, 5, :]))
    phase_end(block, k)


def gated_add(k, i, ps, gate):
    cols = slice(i * 512, (i + 1) * 512)
    for t in range(NT):
        k.dve_steps.did(k.nc.vector.tensor_tensor(k.xn[:, t, cols], ps[:, t, :], gate[:, cols], ALU.mult))
    k.dve_steps.settle(k.nc.vector)
    for t in range(NT):
        ins = k.nc.vector.tensor_tensor(k.x[:, t, cols], k.x[:, t, cols], k.xn[:, t, cols], ALU.add)
    return ins


def mod_flat(k):
    return k.arena.tile[:, 0:6 * D]


def second_stream(v, l):
    token, channel, ffn, rows = chunk_arrays()
    w = v["w_in_2"][l]
    out = ffn(v["ffn1_w_gate_2"][l], v["ffn1_w_up_2"][l]) + rows(v["ffn1_w_down_2"][l])
    out += channel(w[:, :S_GA]) + token(v["cmp_k_w1_2"][l], 8) + token(v["cmp_v_w1_2"][l], 8)
    out += channel(w[:, S_QB:S_VB]) + token(w[:, S_VB:S_AL]) + token(w[:, S_RB:])
    out += token(v["w_branch_nsa_2"][l]) + token(v["w_branch_gla_2"][l]) + token(v["w_out_2"][l])
    out += ffn(v["ffn2_w_gate_2"][l], v["ffn2_w_up_2"][l]) + rows(v["ffn2_w_down_2"][l])
    return np.stack(out)


SECOND_COLS = {"pos_k": 16, "pos_v": 16, "w_small": KD * 40, "w2_k": 2 * DH, "w2_v": 2 * DH}


def second_small(v, l):
    pos = lambda p: p.reshape(16, 2, DH).transpose(1, 2, 0).reshape(P, 16)
    tiles = lambda m: m.reshape(-1, P, m.shape[1]).transpose(1, 0, 2).reshape(P, -1)
    w = v["w_in_2"][l]
    cols = [pos(v["cmp_pos_k_2"][l]), pos(v["cmp_pos_v_2"][l]),
            tiles(np.concatenate([w[:, S_GA:S_QB], w[:, S_AL:S_RB]], 1)), tiles(v["cmp_k_w2_2"][l]),
            tiles(v["cmp_v_w2_2"][l])]
    rows = [v["gla_a_b_2"][l]]
    spread = [v["ffn1_norm_2"][l], v["mix_norm_2"][l], v["ffn2_norm_2"][l], v["gla_out_norm_2"][l]]
    return [np.concatenate(cols, 1), v["gla_a_w2_2"][l], np.concatenate(rows), np.concatenate(spread)]


def distance_bias(block, k, A, nc):
    a = k.arena
    a.at = 0
    k.bias = a.take(HEADS, NT, TOK)
    table, onehot, cols, line = a.take(HEADS), a.take(TOK), a.take(HEADS, P), a.take(HEADS, 512)
    loaded, v = k.flag("small_landed"), nc.vector
    pitch = HEADS * 512

    @block.sync
    def _(sp):
        sp.dma_start(table[0:32, :], A["rel_table"]).then_inc(loaded.sem, 16)
        sp.dma_start(onehot[0:32, :], A["c_onehot"]).then_inc(loaded.sem, 16)

    @block.vector
    def _(dve):
        dve.wait_ge(loaded.sem, loaded.at(32))
        for h in range(HEADS):
            v.tensor_scalar(cols[0:32, h, :], k.c("ones")[0:32, :], table[0:32, h:h + 1], None, ALU.mult)
        v.memset(line[:, :, TOK:512], NEG)
    phase_end(block, k)

    @block.tensor
    def _(pe):
        for h in range(HEADS):
            nc_matmul(k, k.bank[h][:, 0:TOK], cols[0:32, h, :], onehot[0:32, :], True, True)
    phase_end(block, k)

    @block.vector
    def _(dve):
        for h in range(HEADS):
            v.tensor_copy(line[:, h, 0:TOK], k.bank[h][:, 0:TOK])
    phase_end(block, k)

    @block.sync
    def _(sp):
        flat = k.lines.rearrange("(p n) -> p n", n=pitch)
        sp.wait_ge(k.flag("phase_arrived").sem, 4 * k.phase)
        sp.dma_start(flat[0:P, :].rearrange("p (h n) -> p h n", h=HEADS), line).then_inc(loaded.sem, 16)
        sp.wait_ge(loaded.sem, loaded.at(48))
        for t in range(NT):
            c = TOK - 1 - t * P
            skewed = k.lines[c:c + P * (pitch - 1)].rearrange("(p n) -> p n", n=pitch - 1)
            for h in range(HEADS):
                sp.dma_start(k.bias[:, h, t, :], skewed[:, h * 512:h * 512 + TOK]).then_inc(loaded.sem, 16)
        sp.wait_ge(loaded.sem, loaded.at(48 + 16 * NT * HEADS))
    loaded.base += 48 + 16 * NT * HEADS


def keys_values(block, k, keys, values):
    first, group0 = k.chunk, k.group
    nc = k.nc
    used, act_evac, dve_evac = k.flag("slot_used"), k.flag("act_evac"), k.flag("dve_evac")
    ps = k.pair[group0 % 2]

    @block.tensor
    def _(pe):
        for s in (act_evac, dve_evac):
            if s.base > 0:
                pe.wait_ge(s.sem, s.base)
        slot = slot_wait(pe, first, 0, 0, k)[:, :].rearrange("p (k n) -> p k n", k=8)
        for kt in range(8):
            nc_matmul(k, ps[:, 0, 0:TOK], slot[:, kt, 0:P], k.hT[:, kt, :], kt == 0, kt == 7)
        for t in range(NT):
            for kt in range(8):
                ins = nc_matmul(k, ps[:, 1, t * P:(t + 1) * P], k.hT[:, kt, t * P:(t + 1) * P], slot[:, kt, P:2 * P],
                                kt == 0, kt == 7)
        ins.then_inc(used.sem, 1)

    @block.scalar
    def _(act):
        act.wait_ge(used.sem, first + 1)
        for g in range(2):
            for half in range(2):
                ins = nc.scalar.copy(keys[half * 64:half * 64 + 64, g, :], ps[g * 64:g * 64 + 64, 0, 0:TOK])
        ins.then_inc(act_evac.sem, 1)

    @block.vector
    def _(dve):
        dve.wait_ge(used.sem, first + 1)
        nc.vector.tensor_copy(values, ps[:, 1, 0:TOK].rearrange("p (t n) -> p t n", t=NT)).then_inc(dve_evac.sem, 1)
    act_evac.base += 1
    dve_evac.base += 1
    k.chunk += 1
    k.group += 1


def compress(block, k, pairs, keysT, values):
    nc, v = k.nc, k.nc.vector
    a = k.arena
    mark = a.at
    blocks = a.take(2, 16, 2, NC)
    hid = a.take(2, 2, 2 * NC)
    first = k.chunk
    used = k.flag("slot_used")

    @block.vector
    def _(dve):
        for n, name in enumerate(("pos_k", "pos_v")):
            for g in range(2):
                tokens = pairs[:, n, g, :].rearrange("p (c q) -> p q c", q=8)
                for late in range(2):
                    v.tensor_tensor(blocks[:, n, 8 * late:8 * late + 8, g, :], tokens[:, :, late:late + NC],
                                    k.col2[name][:, 8 * late:8 * late + 8].unsqueeze(2).to_broadcast([P, 8, NC]), ALU.add)
    phase_end(block, k)

    @block.tensor
    def _(pe):
        for n in range(2):
            for h in range(2):
                slot = slot_wait(pe, first, 2 * n + h, 2 * n + h, k)[:, :].rearrange("p (k n) -> p k n", k=8)
                for hb in range(2):
                    for kt in range(8):
                        ins = nc_matmul(k, k.bank[4 + 2 * n + hb][:, 0:2 * NC], slot[:, kt, hb * P:(hb + 1) * P],
                                        blocks[:, n, 8 * h + kt, :, :].rearrange("p g c -> p (g c)"), h + kt == 0, h * 8 + kt == 15)
                ins.then_inc(used.sem, 1)
    k.chunk += 4
    phase_end(block, k)

    @block.scalar
    def _(act):
        for n in range(2):
            for hb in range(2):
                nc.scalar.activation(hid[:, n, hb, :], k.bank[4 + 2 * n + hb][:, 0:2 * NC], ACT.Silu)
    phase_end(block, k)

    @block.tensor
    def _(pe):
        for hb in range(2):
            nc_matmul(k, k.bank[4][0:64, 0:2 * NC], k.col2["w2_k"][:, hb * DH:(hb + 1) * DH], hid[:, 0, hb, :], hb == 0, hb == 1)
        for g in range(2):
            for hb in range(2):
                nc_matmul(k, k.bank[5][0:NC, g * DH:(g + 1) * DH], hid[:, 1, hb, g * NC:(g + 1) * NC],
                          k.col2["w2_v"][:, hb * DH:(hb + 1) * DH], hb == 0, hb == 1)
    phase_end(block, k)

    @block.vector
    def _(dve):
        for half in range(2):
            v.tensor_copy(keysT[half * 64:half * 64 + 64, 0:2 * NC], k.bank[4][0:64, 0:2 * NC])
        v.tensor_copy(values[0:NC, :], k.bank[5][0:NC, 0:2 * DH])
    phase_end(block, k)
    a.at = mark


def nsa(block, k, qT, keysT, valuesT, kc, vc, gates, oT):
    nc, v = k.nc, k.nc.vector
    a = k.arena
    mark = a.at
    S = a.take(HEADS, NT, 2 * TOK)
    C = a.take(HEADS, NT, 16)
    PT = a.take(HEADS, 2, 384)
    CT = a.take(HEADS, TOK)
    stat = lambda tile: tile[:, 0:48].rearrange("p (t h b) -> p t h b", t=NT, h=HEADS)
    mx, tot, rec = stat(k.mx), stat(k.tot), stat(k.rec)
    units = [(h, t) for h in range(HEADS) for t in range(NT)]
    scored, took, maxed = k.flag("scored"), k.flag("score_read"), k.flag("maxed")
    SS = lambda h, t: S[:, h, t, :].rearrange("p (b s) -> p b s", b=2)[:, :, 0:(t + 1) * P]

    @block.tensor
    def _(pe):
        for u, (h, t) in enumerate(units):
            if u >= 2:
                pe.wait_ge(took.sem, took.at(2 * (u - 1)))
            p0, n, g = 64 * (h % 2), (t + 1) * P, h // 4
            q = qT[p0:p0 + 64, h // 2, t * P:(t + 1) * P]
            for b in range(2):
                nc_matmul(k, k.bank[4 + u % 2][:, b * TOK:b * TOK + n], q, keysT[b][p0:p0 + 64, g, 0:n], True, True)
            nc_matmul(k, k.bank[6 + u % 2][:, 0:NC], q, kc[p0:p0 + 64, g * NC:(g + 1) * NC], True,
                      True).then_inc(scored.sem, 1)

    @block.vector
    def _(dve):
        for u in range(len(units) + 1):
            if u < len(units):
                h, t = units[u]
                n = (t + 1) * P
                dve.wait_ge(scored.sem, scored.at(u + 1))
                v.tensor_tensor(SS(h, t), k.bank[4 + u % 2][:, :].rearrange("p (b s) -> p b s", b=2)[:, :, 0:n],
                                k.bias[:, h, t, 0:n].unsqueeze(1).to_broadcast([P, 2, n]), ALU.add).then_inc(took.sem, 1)
                v.tensor_tensor(C[:, h, t, 0:NC], k.bank[6 + u % 2][:, 0:NC], k.bias[:, h, t, 31:TOK:16],
                                ALU.add).then_inc(took.sem, 1)
            if u >= 1:
                h, t = units[u - 1]
                dve.wait_ge(took.sem, took.at(2 * u))
                v.tensor_reduce(mx[:, t, h, 1:3], SS(h, t), AX.X, ALU.max, negate=True)
                v.tensor_reduce(mx[:, t, h, 0:1], C[:, h, t, 0:NC], AX.X, ALU.max, negate=True).then_inc(maxed.sem, 1)

    @block.scalar
    def _(act):
        for u, (h, t) in enumerate(units):
            act.wait_ge(maxed.sem, maxed.at(u + 1))
            for b in range(3):
                x = C[:, h, t, 0:NC] if b == 0 else SS(h, t)[:, b - 1, :]
                nc.scalar.activation(x, x, ACT.Exp, bias=mx[:, t, h, b:b + 1], accum_out=tot[:, t, h, b:b + 1])
    scored.base += 16
    took.base += 32
    maxed.base += 16
    phase_end(block, k)

    @block.vector
    def _(dve):
        k.dve_steps.did(v.reciprocal(k.rec[:, 0:48], k.tot[:, 0:48]))
        k.dve_steps.settle(dve)
        v.tensor_tensor(k.rec[:, 0:48], k.rec[:, 0:48], gates, ALU.mult)
    phase_end(block, k)
    scaled = [k.flag("scaled_act"), k.flag("scaled_dve")]
    pturned, pread = k.flag("probs_turned"), [k.flag("probs_read_act"), k.flag("probs_read_dve")]
    mixed, yread = k.flag("mixed"), k.flag("mixed_read")
    base = lambda h: 4 * (h % 2)

    def mix(pe, h):
        for s in pread:
            pe.wait_ge(s.sem, s.at(h + 1))
        b = h // 2
        if h % 2 == 0 and b >= 2:
            pe.wait_ge(yread.sem, yread.at(b - 1))
        o = k.bank[3 + 4 * (b % 2)][64 * (h % 2):64 * (h % 2) + 64, 0:TOK]
        g = slice((h // 4) * DH, (h // 4 + 1) * DH)
        for n in range(2):
            nc_matmul(k, o, valuesT[n][:, 0, g], PT[:, h, n, 0:TOK], n == 0, False)
            nc_matmul(k, o[:, P:TOK], valuesT[n][:, 1, g], PT[:, h, n, TOK:384], False, False)
        nc_matmul(k, o, vc[0:NC, g], CT[0:NC, h, :], False, True).then_inc(mixed.sem, 1)

    @block.tensor
    def _(pe):
        for h in range(HEADS):
            for s in scaled:
                pe.wait_ge(s.sem, s.at(h + 1))
            if h >= 2:
                for s in pread:
                    pe.wait_ge(s.sem, s.at(h - 1))
            for n in range(2):
                for i, (t, s) in enumerate(((0, 0), (1, 0), (1, 1))):
                    nc.tensor.transpose(k.bank[base(h) + n][:, i * P:(i + 1) * P],
                                        S[:, h, t, n * TOK + s * P:n * TOK + (s + 1) * P], k.c("ident"))
            for t in range(NT):
                ins = nc.tensor.transpose(k.bank[base(h) + 2][0:NC, t * P:(t + 1) * P], C[:, h, t, 0:NC], k.c("ident"))
            ins.then_inc(pturned.sem, 1)
            if h >= 1:
                mix(pe, h - 1)
        mix(pe, HEADS - 1)

    def out(act, b):
        act.wait_ge(mixed.sem, mixed.at(2 * b + 2))
        nc.scalar.copy(oT[:, b, :], k.bank[3 + 4 * (b % 2)][:, 0:TOK]).then_inc(yread.sem, 1)

    @block.scalar
    def _(act):
        def scale(h):
            for t in range(NT):
                ins = nc.scalar.activation(SS(h, t)[:, 0, :], SS(h, t)[:, 0, :], ACT.Copy, scale=rec[:, t, h, 1:2])
            ins.then_inc(scaled[0].sem, 1)
        scale(0)
        for h in range(HEADS):
            if h + 1 < HEADS:
                scale(h + 1)
            act.wait_ge(pturned.sem, pturned.at(h + 1))
            nc.scalar.copy(PT[:, h, 0, :], k.bank[base(h)][:, 0:384]).then_inc(pread[0].sem, 1)
            if h % 2 == 1 and h >= 3:
                out(act, h // 2 - 1)
        out(act, NB - 1)

    @block.vector
    def _(dve):
        def scale(h):
            for t in range(NT):
                v.tensor_scalar(SS(h, t)[:, 1, :], SS(h, t)[:, 1, :], rec[:, t, h, 2:3], None, ALU.mult)
                ins = v.scalar_tensor_tensor(C[:, h, t, 0:NC], C[:, h, t, 0:NC], rec[:, t, h, 0:1], k.seen[:, t, :],
                                             ALU.mult, ALU.mult)
            ins.then_inc(scaled[1].sem, 1)
        scale(0)
        for h in range(HEADS):
            if h + 1 < HEADS:
                scale(h + 1)
            dve.wait_ge(pturned.sem, pturned.at(h + 1))
            v.tensor_copy(PT[:, h, 1, :], k.bank[base(h) + 1][:, 0:384])
            v.tensor_copy(CT[0:NC, h, :], k.bank[base(h) + 2][0:NC, 0:TOK]).then_inc(pread[1].sem, 1)
    for s, n in ((scaled[0], 8), (scaled[1], 8), (pturned, 8), (pread[0], 8), (pread[1], 8), (mixed, 8), (yread, 4)):
        s.base += n
    phase_end(block, k)
    a.at = mark


def gla(block, k, qT, kT, vb, rb, alT, gain, oT):
    nc, v = k.nc, k.nc.vector
    steps = k.dve_steps
    a = k.arena
    mark = a.at
    la, ex = a.take(NT * WIDTH), a.take(NT * WIDTH)
    B, qd, ki, ks = (a.take(GH, TOK) for _ in range(4))
    kst, AT = a.take(NT, WIDTH), a.take(NT * GH, P)
    S, ends = a.take(2, GH, GV), a.take(GH, NCH)
    o = a.take(NT, GH * GV)
    big = k.big
    chunks = lambda x: x.rearrange("p h (c t) -> p h c t", c=NCH)

    @block.tensor
    def _(pe):
        for t in range(NT):
            d = big[0][:, t * WIDTH:(t + 1) * WIDTH]
            nc_matmul(k, d, alT[0:16, t * P:(t + 1) * P], k.a_w2[0:16, :], True, False)
            nc_matmul(k, d, k.c("ones")[0:1, :], k.w0[0:1, :], False, True)
    phase_end(block, k)

    @block.scalar
    def _(act):
        k.act_steps.did(nc.scalar.activation(ex, big[0], ACT.Abs))
        k.act_steps.settle(act)
        k.act_steps.did(nc.scalar.activation(ex, ex, ACT.Exp, scale=-1.0))
        k.act_steps.settle(act)
        nc.scalar.activation(ex, ex, ACT.Ln, bias=1.0)
    phase_end(block, k)

    @block.vector
    def _(dve):
        v.scalar_tensor_tensor(la, big[0], 0.0, ex, ALU.min, ALU.subtract)
    phase_end(block, k)

    @block.tensor
    def _(pe):
        for h in range(GH):
            for t in range(NT):
                nc_matmul(k, flat4(big[0])[:, h, t * P:(t + 1) * P], la[:, t * WIDTH + h * P:t * WIDTH + (h + 1) * P],
                          k.c("incl_up"), True, True)
    phase_end(block, k)

    @block.vector
    def _(dve):
        v.tensor_copy(B, flat4(big[0]))
    phase_end(block, k)

    @block.vector
    def _(dve):
        last = chunks(B)[:, :, :, CHUNK - 1:CHUNK]
        for h in range(GH):
            v.tensor_tensor(chunks(ks)[:, h], last[:, h].to_broadcast([P, NCH, CHUNK]), chunks(B)[:, h], ALU.subtract)

    @block.scalar
    def _(act):
        nc.scalar.activation(qd, flat4(big[0]), ACT.Exp, scale=1.0 / 16)
        nc.scalar.activation(ki, flat4(big[0]), ACT.Exp, scale=-1.0 / 16)
        nc.scalar.activation(ends, B[:, :, CHUNK - 1:TOK:CHUNK], ACT.Exp, scale=1.0 / 16)
    phase_end(block, k)

    @block.scalar
    def _(act):
        nc.scalar.activation(ks, ks, ACT.Exp, scale=1.0 / 16)

    @block.vector
    def _(dve):
        v.tensor_tensor(qd, qd, qT, ALU.mult)
        v.tensor_tensor(ki, ki, kT, ALU.mult)
    phase_end(block, k)

    @block.vector
    def _(dve):
        v.tensor_tensor(ks, ks, kT, ALU.mult)
        v.memset(S[:, 0], 0.0)

    @block.tensor
    def _(pe):
        for n in range(NT * GH):
            h, t = n % GH, slice((n // GH) * P, (n // GH + 1) * P)
            nc_matmul(k, big[1][:, n * P:(n + 1) * P], ki[:, h, t], qd[:, h, t], True, True)
    phase_end(block, k)

    @block.vector
    def _(dve):
        v.tensor_tensor(AT, big[1].rearrange("p (n t) -> p n t", t=P),
                        k.c("incl_up").unsqueeze(1).to_broadcast([P, NT * GH, P]), ALU.mult)
    turn_back(block, k, ks, kst)
    for c in range(NCH):
        t, p0 = c // 2, 64 * (c % 2)
        rows, cc = slice(p0, p0 + 64), slice(c * CHUNK, (c + 1) * CHUNK)
        now, nxt = S[:, c % 2], S[:, (c + 1) % 2]

        @block.tensor
        def _(pe):
            for h in range(GH):
                vv = vb[:, t, h * GV:(h + 1) * GV]
                d = big[0][rows, h * GV:(h + 1) * GV]
                nc_matmul(k, d, qd[:, h, cc], now[:, h, :], True, False)
                nc_matmul(k, d, AT[:, t * GH + h, p0:p0 + 64], vv, False, True)
                nc_matmul(k, big[1][:, h * GV:(h + 1) * GV], kst[rows, t, h * P:(h + 1) * P], vv[rows], True, True)
        phase_end(block, k)

        @block.vector
        def _(dve):
            for h in range(GH):
                v.scalar_tensor_tensor(nxt[:, h, :], now[:, h, :], ends[:, h, c:c + 1],
                                       big[1][:, h * GV:(h + 1) * GV], ALU.mult, ALU.add)

        @block.scalar
        def _(act):
            nc.scalar.copy(o[rows, t, :], big[0][rows, :])
        phase_end(block, k)
    ss = k.mx[:, 0:8]

    @block.scalar
    def _(act):
        for t in range(NT):
            for h in range(GH):
                nc.scalar.activation(k.xn[:, t, h * GV:(h + 1) * GV], o[:, t, h * GV:(h + 1) * GV], ACT.Square,
                                     accum_out=ss[:, t * GH + h:t * GH + h + 1])
    phase_end(block, k)

    @block.vector
    def _(dve):
        v.tensor_scalar(k.tot[:, 0:8], ss, 1.0 / GV, RMS_EPS, ALU.mult, ALU.add)
    phase_end(block, k)

    @block.scalar
    def _(act):
        nc.scalar.activation(k.rec[:, 0:8], k.tot[:, 0:8], ACT.Sqrt)
    phase_end(block, k)

    @block.vector
    def _(dve):
        steps.did(v.reciprocal(ss, k.rec[:, 0:8]))
        steps.settle(dve)
        for t in range(NT):
            for h in range(GH):
                x = o[:, t, h * GV:(h + 1) * GV]
                steps.did(v.scalar_tensor_tensor(x, x, ss[:, t * GH + h:t * GH + h + 1], gain[:, h * GV:(h + 1) * GV],
                                                 ALU.mult, ALU.mult))
        steps.settle(dve)
        for t in range(NT):
            v.tensor_tensor(o[:, t, :], o[:, t, :], rb[:, t, :], ALU.mult)
    phase_end(block, k)
    turn(block, k, o, oT, NG)
    phase_end(block, k)
    a.at = mark


def second_layer(block, k, A, l):
    nc = k.nc
    a = k.arena
    a.at = HEADS * NT * TOK
    small = k.flag("small_landed")
    row = lambda name: A[name][bass.ds(l, 1)]
    tok = lambda kt, t, i: k.hT[:, kt, t * P:(t + 1) * P]
    cols = a.take(sum(SECOND_COLS.values()))
    k.col2 = columns(cols, SECOND_COLS)
    out_norm, k.a_w2 = a.take(D), a.take(WIDTH)
    body = a.at
    norms = k.spread[:, 0:3 * D]
    stream(block, k, A["stream2"][bass.ds(l, 1)].rearrange("a c p n -> (a c) p n"), 105)

    @block.scalar
    def _(act):
        spread = row("spread2").partition_broadcast(P).rearrange("p a n -> p (a n)")
        for dst, src in ((norms, spread[:, 0:3 * D]), (cols, row("cols2").rearrange("a p n -> (a p) n")),
                         (k.a_w2[0:16, :], row("a_w2").rearrange("a p n -> (a p) n")), (k.w0[0:1, :], row("rows2")),
                         (out_norm, spread[:, 3 * D:4 * D])):
            act.dma_start(dst, src).then_inc(small.sem, 16)
        act.wait_ge(small.sem, 80)
    small.base += 80
    phase_end(block, k)
    norm = lambda n: norms[:, n * D:(n + 1) * D]

    def ffn(n):
        a.at = body
        rms_norm(block, k, norm(n))
        turn(block, k, k.xn, k.hT, KD)
        phase_end(block, k)
        k.hidden, k.ffn_act = a.take(NF, TOK), a.take(2, 512)
        gated(block, k)
        phase_end(block, k)
        down(block, k, lambda dve, half, ps: scaled_add(k, half, ps, 0.5))
        phase_end(block, k)
    ffn(0)
    a.at = body
    oT, obT = a.take(NB, TOK), a.take(NG, TOK)
    alT = a.take(TOK)
    mixers = a.at
    rms_norm(block, k, norm(1))
    turn(block, k, k.xn, k.hT, KD)
    phase_end(block, k)
    qT, pairs, keys, values = a.take(NB, TOK), a.take(2, 2, P), a.take(2, 2, TOK), a.take(2, NT, P)
    gates, kc, vc = a.take(NT * 24), a.take(32), a.take(2 * DH)
    flat = lambda x: x.rearrange("p b t -> p (b t)")
    product(block, k, "channel", 256, 2, moving=lambda kt: k.hT[:, kt, :], unroll=4,
            act=lambda i, j, ps: nc.scalar.activation(flat(qT[:, 2 * i:2 * i + 2, :]), ps[:, 0, :], ACT.Copy,
                                                      scale=DH ** -0.5))

    def split_pairs(i, j, ps):
        for n in range(2):
            for g in range(2):
                for par in range(2):
                    ins = nc.scalar.copy(pairs[par * 64:par * 64 + 64, n, g, :],
                                         ps[g * 64:g * 64 + 64, 0, n * TOK + par:(n + 1) * TOK:2])
        return ins
    product(block, k, "channel", 256, 1, moving=lambda kt: k.hT[:, kt, :], act=split_pairs)
    for n in range(2):
        keys_values(block, k, keys[:, n], values[:, n])
    wsm = k.col2["w_small"].rearrange("p (k n) -> p k n", k=KD)

    @block.tensor
    def _(pe):
        for t in range(NT):
            for kt in range(KD):
                nc_matmul(k, k.bank[4][:, t * 24:(t + 1) * 24], tok(kt, t, 0), wsm[:, kt, 0:24], kt == 0, kt == KD - 1)
        for kt in range(KD):
            nc_matmul(k, k.bank[5][0:16, 0:TOK], wsm[:, kt, 24:40], k.hT[:, kt, :], kt == 0, kt == KD - 1)
    phase_end(block, k)

    @block.scalar
    def _(act):
        nc.scalar.activation(gates, k.bank[4][:, 0:48], ACT.Sigmoid)
        nc.scalar.copy(alT[0:16, :], k.bank[5][0:16, 0:TOK])
    compress(block, k, pairs, kc, vc)
    nsa(block, k, qT, [keys[:, 0], keys[:, 1]], [values[:, 0], values[:, 1]], kc, vc, gates, oT)
    a.at = mixers
    qb, kb, vb, rb = a.take(GH, TOK), a.take(GH, TOK), a.take(NT, GH * GV), a.take(NT, GH * GV)
    for dst, scale in ((qb, P ** -0.5), (kb, 1.0)):
        product(block, k, "channel", 256, 2, moving=lambda kt: k.hT[:, kt, :], unroll=4,
                act=lambda i, j, ps, dst=dst, scale=scale: nc.scalar.activation(
                    flat(dst[:, 2 * i:2 * i + 2, :]), ps[:, 0, :], ACT.Copy, scale=scale))
    token_out = lambda op, dst: (lambda i, j, ps: [op(dst[:, t, i * 512:(i + 1) * 512], ps[:, t, :]) for t in range(NT)][-1])
    product(block, k, "token", 512, 2, stationary=tok, dve=token_out(nc.vector.tensor_copy, vb))
    product(block, k, "token", 512, 2, stationary=tok,
            act=token_out(lambda o, i: nc.scalar.activation(o, i, ACT.Silu), rb))
    phase_end(block, k)
    gla(block, k, qb, kb, vb, rb, alT, out_norm, obT)
    a.at = mixers
    gm = a.take(NT, 2 * D)
    product(block, k, "token", 512, 4, stationary=tok,
            act=token_out_dyn(lambda o, i: nc.scalar.activation(o, i, ACT.Sigmoid), gm))
    phase_end(block, k)
    mul = lambda o, i: nc.vector.tensor_tensor(o, o, i, ALU.mult)
    product(block, k, "token", 512, 2, ktiles=4, unroll=4, stationary=lambda kt, t, i: oT[:, kt, t * P:(t + 1) * P],
            dve=token_out(mul, gm[:, :, 0:D]))
    product(block, k, "token", 512, 2, stationary=lambda kt, t, i: obT[:, kt, t * P:(t + 1) * P],
            dve=token_out(mul, gm[:, :, D:2 * D]))
    phase_end(block, k)

    @block.vector
    def _(dve):
        nc.vector.tensor_tensor(gm[:, 0, 0:D], gm[:, 0, 0:D], gm[:, 0, D:2 * D], ALU.add)

    @block.gpsimd
    def _(pool):
        nc.gpsimd.tensor_tensor(gm[:, 1, 0:D], gm[:, 1, 0:D], gm[:, 1, D:2 * D], ALU.add)
    phase_end(block, k)
    turn(block, k, gm, k.hT, KD)
    phase_end(block, k)
    product(block, k, "token", 512, 2, stationary=tok, dve=lambda i, j, ps: scaled_add(k, i, ps, 1.0))
    phase_end(block, k)
    ffn(2)
    assert k.chunk == 105, k.chunk


def token_out_dyn(op, dst):
    def out(i, j, ps):
        for t in range(NT):
            ins = op(dst[:, t, bass.ds(i * 512, 512)], ps[:, t, :])
        return ins
    return out


def scaled_add(k, i, ps, factor):
    cols = slice(i * 512, (i + 1) * 512)
    for t in range(NT):
        ins = k.nc.vector.scalar_tensor_tensor(k.x[:, t, cols], ps[:, t, :], factor, k.x[:, t, cols], ALU.mult, ALU.add)
    return ins


def build(nc, A, O, dump=None):
    with ExitStack() as ctx:
        k = Program(nc, ctx)
        square = k.sb("c_square", [P, len(CONSTS) * P])
        rows = k.sb("c_rows", [P, NT, 512 + 64 + NC])
        k.c = lambda name: square[:, CONSTS.index(name) * P:(CONSTS.index(name) + 1) * P]
        k.count, k.blocked = rows[:, :, 0:256], rows[:, :, 256:512]
        k.cos, k.sin, k.seen = rows[:, :, 512:544], rows[:, :, 544:576], rows[:, :, 576:576 + NC]
        k.x, k.hT = k.sb("x", [P, NT, D]), k.sb("hT", [P, KD, TOK])
        k.slots = [k.sb(f"slot{i}", [P, SLOT]) for i in range(SLOTS)]
        k.stat, k.mx, k.tot, k.rec = k.sb("stat", [P, 8]), k.sb("mx", [P, 64]), k.sb("tot", [P, 64]), k.sb("rec", [P, 64])
        k.cols1 = k.sb("cols1", [P, sum(FIRST_COLS.values())])
        k.col = columns(k.cols1, FIRST_COLS)
        k.w0, k.spread = k.sb("w0", [1, WIDTH]), k.sb("spread", [P, 2 * D + 2 * WIDTH])
        k.arena = Arena(k.sb("arena", [P, 29600]), 29600)
        k.xn = k.sb("xn", [P, NT, D])
        banks = [ctx.enter_context(nc.psum_tensor(f"pair{i}", [P, 2, 512], F32)) for i in range(4)]
        k.pair = banks[0:2]
        k.big = [b[:].rearrange("p a n -> p (a n)") for b in banks]
        k.bank = [banks[i // 2][:, i % 2, :] for i in range(8)]
        k.lines = nc.dram_tensor("bias_lines", [(P + 1) * HEADS * 512], F32, kind="Internal").ap()
        loaded = ctx.enter_context(nc.semaphore("consts_loaded"))
        with nc.Block() as block:
            @block.sync
            def _(sp):
                sp.dma_start(square[:], A["c_square"]).then_inc(loaded, 16)
                sp.dma_start(rows[:], A["c_rows"]).then_inc(loaded, 16)
                sp.dma_start(k.x[:], A["x"].rearrange("a (t p) n -> p (a t) n", p=P)).then_inc(loaded, 16)
                sp.wait_ge(loaded, 48)
        with nc.Fori(0, DEPTH) as l:
            with nc.Block() as block:
                first_layer(block, k, A, l)
            k.end_layer()
        small = k.flag("final_norm_landed")

        def final_norm(block, name):
            @block.sync
            def _(sp):
                sp.dma_start(k.spread[:, 0:D], A[name].partition_broadcast(P).rearrange("p a n -> p (a n)")
                             ).then_inc(small.sem, 16)

            @block.vector
            def _(dve):
                dve.wait_ge(small.sem, 16)
            small.base += 16
            rms_norm(block, k, k.spread[:, 0:D])
        with nc.Block() as block:
            final_norm(block, "norm_final")

            @block.vector
            def _(dve):
                nc.vector.tensor_copy(k.x[:], k.xn[:])
            phase_end(block, k)
            distance_bias(block, k, A, nc)
        k.end_layer()
        with nc.Fori(0, DEPTH) as l:
            with nc.Block() as block:
                second_layer(block, k, A, l)
            k.end_layer()
        stored = ctx.enter_context(nc.semaphore("stored"))
        with nc.Block() as block:
            final_norm(block, "final_norm_2")

            @block.sync
            def _(sp):
                sp.wait_ge(k.flag("phase_arrived").sem, 4 * k.phase)
                sp.dma_start(O["out"].rearrange("a (t p) n -> p (a t) n", p=P), k.xn[:]).then_inc(stored, 16)
                sp.wait_ge(stored, 16)


def host_arrays(v):
    f = lambda a: np.ascontiguousarray(a)
    out = dict(shape_constants())
    out["x"] = v["x"]
    out["stream1"] = f(np.stack([first_stream(v, l) for l in range(DEPTH)]))
    for name, parts in zip(("cols1", "wide1", "rows1", "spread1"), zip(*[first_small(v, l) for l in range(DEPTH)])):
        out[name] = f(np.stack(parts))
    out["stream2"] = f(np.stack([second_stream(v, l) for l in range(DEPTH)]))
    for name, parts in zip(("cols2", "a_w2", "rows2", "spread2"), zip(*[second_small(v, l) for l in range(DEPTH)])):
        out[name] = f(np.stack(parts))
    out["rel_table"] = v["rel_table_2"]
    out["norm_final"] = v["norm_final"][None]
    out["final_norm_2"] = v["final_norm_2"][None]
    return out


def program(nc, A, out):
    build(nc, A, {"out": out})


def kernel(**inputs):
    import concourse.bacc as _bacc
    from concourse.bass_utils import run_bass_kernel_spmd as _run

    nc = _bacc.Bacc("TRN2", target_bir_lowering=False, num_devices=1)
    arrays = {f"in_{n}": a for n, a in host_arrays({n: np.asarray(a) for n, a in inputs.items()}).items()}
    A = {n[3:]: nc.dram_tensor(n, a.shape, mybir.dt.from_np(a.dtype), kind="ExternalInput").ap() for n, a in arrays.items()}
    out = nc.dram_tensor("out", [1, TOK, D], F32, kind="ExternalOutput").ap()
    program(nc, A, out)
    return _run(nc, [arrays], core_ids=[0]).results[0]["out"]
```

```python
from contextlib import ExitStack, contextmanager

import numpy as np

import concourse.bass as bass
from concourse import mybir

ALU = mybir.AluOpType
ACT = mybir.ActivationFunctionType
AX = mybir.AxisListType
F32 = mybir.dt.float32
F32R = mybir.dt.float32r

P = 128
TOK = 256
NT = TOK // P
D = 1024
KD = D // P
DEPTH = 2
HEADS = 8
DH = 64
WIDTH = HEADS * DH
NB = WIDTH // P
D_FF = 2816
NF = D_FF // P
RWKV_COLS = 3 * WIDTH + 64 + 64 + 128
NZ = RWKV_COLS // P
CHUNK = 64
NCH = TOK // CHUNK
ATT0, RWKV0 = 0, 3 * WIDTH
UV0 = RWKV0 + RWKV_COLS
GATE0 = UV0 + 2 * WIDTH
DECAY = float(np.exp(-0.5))
RMS_EPS, LN_EPS, GN_EPS = 1e-6, 1e-5, 64e-5
NEG = -1e30
SLOTS = 2
ADA_SLOTS = 3
SLOT = 2048
NC = 15
S_KV, S_GA, S_QB = 512, 1280, 1304
S_KB, S_VB, S_AL, S_RB, S_GM = 1816, 2328, 3352, 3368, 4392
GH, GV = 4, 256
NG = GH * GV // P


CONSTS = ["ident", "blockones", "ones", "strict_up", "incl_up", "strict_lo"] + [f"level{i}" for i in range(6)] + ["lower0", "upper"]


def shape_constants():
    i = np.arange(P)
    r, c = i[:, None], i[None, :]
    same = (r // CHUNK) == (c // CHUNK)
    m = {"ident": r == c, "blockones": (r // DH) == (c // DH), "ones": np.ones((P, P), bool),
         "strict_up": same & (r < c), "incl_up": same & (r <= c), "strict_lo": same & (r > c)}
    for k in range(6):
        b = 2 << k
        m[f"level{k}"] = ((r // b) == (c // b)) & (r % b < b // 2) & (c % b >= b // 2)
    m["lower0"] = m["level0"].T
    m["upper"] = r <= c
    square = np.concatenate([m[n] for n in CONSTS], axis=1).astype(np.float32)
    t, s = np.arange(TOK)[:, None], np.arange(TOK)[None, :]
    count = ((t >= s) & (t - s <= 128)).astype(np.float32)
    for d in (4, 16):
        count += (t >= s) & ((t - s) % d == 0)
    blocked = np.where(count > 0, 0, NEG).astype(np.float32)
    ends = 16 * np.arange(NC)[None, :] + 31
    seen = (ends <= t).astype(np.float32)
    inv = 1.0 / (np.float32(10000.0) ** (np.arange(0, DH, 2, dtype=np.float32) / np.float32(DH)))
    ang = np.arange(TOK, dtype=np.float32)[:, None] * inv[None, :].astype(np.float32)
    rows = np.concatenate([count, blocked, np.cos(ang), np.sin(ang), seen], axis=1).astype(np.float32)
    tiles = rows.reshape(NT, P, -1).transpose(1, 0, 2)
    dist = np.arange(TOK)
    logb = 16 + (np.log(np.maximum(dist, 1).astype(np.float32) / np.float32(16)) / np.float32(np.log(64.0))
                 * np.float32(16)).astype(np.int32)
    bucket = np.where(dist < 16, dist, np.minimum(logb, 31))
    onehot = (np.arange(32)[:, None] == bucket[None, ::-1]).astype(np.float32)
    return {"c_square": square, "c_rows": np.ascontiguousarray(tiles), "c_onehot": onehot}


class Signal:

    def __init__(self, sem):
        self.sem, self.base = sem, 0

    def at(self, n):
        return self.base + n


class Steps(Signal):

    def __init__(self, sem):
        super().__init__(sem)
        self.moving = 0

    def did(self, ins):
        ins.then_inc(self.sem, 1)
        self.base += 1
        return ins

    def settle(self, eng):
        eng.wait_ge(self.sem, self.moving + self.base)


@contextmanager
def counted(steps, it, per):
    if steps is None:
        yield
        return
    start = steps.base
    steps.moving = it * per
    yield
    assert steps.base - start == per, (steps.base - start, per)
    steps.moving = 0


def repeat(eng, n, unroll, step, peel=0, steps=None, per=0):
    for i in range(min(peel, n)):
        step(i, i)
    turns = (n - peel) // unroll
    done = peel
    if turns >= 2:
        with eng.Fori(0, turns) as it:
            with counted(steps, it, per * unroll):
                for j in range(unroll):
                    step(it * unroll + (peel + j), peel + j)
        if steps is not None:
            steps.base += per * unroll * (turns - 1)
        done = peel + turns * unroll
    for i in range(done, n):
        step(i, i)


class Program:

    def __init__(self, nc, ctx):
        self.nc, self.ctx, self.flags = nc, ctx, {}
        self.chunk = self.group = self.phase = self.chunks = 0
        self.pe_steps = Steps(self.sem("pe_steps"))
        self.act_steps = Steps(self.sem("act_steps"))
        self.dve_steps = Steps(self.sem("dve_steps"))
        self.pool_steps = Steps(self.sem("pool_steps"))
        self.slot_landed = [Signal(self.sem(f"slot_landed{i}")) for i in range(SLOTS)]

    def sem(self, name):
        return self.ctx.enter_context(self.nc.semaphore(name))

    def sb(self, name, shape, dtype=F32):
        return self.ctx.enter_context(self.nc.sbuf_tensor(name, shape, dtype))

    def flag(self, name):
        if name not in self.flags:
            self.flags[name] = Signal(self.sem(name))
        return self.flags[name]

    def all_flags(self):
        return [self.pe_steps, self.act_steps, self.dve_steps, self.pool_steps] + self.slot_landed + list(self.flags.values())

    def end_layer(self):
        nc = self.nc
        engines = [nc.sync, nc.tensor, nc.scalar, nc.vector, nc.gpsimd]
        for n, s in enumerate(self.all_flags()):
            engines[n % 5].sem_clear(s.sem)
            s.base = 0
        self.chunk = self.group = self.phase = 0
        nc.all_engine_barrier()


def phase_end(block, k):
    k.phase += 1
    arrived = k.flag("phase_arrived")

    def meet(eng):
        eng.drain().then_inc(arrived.sem, 1)
        eng.wait_ge(arrived.sem, 4 * k.phase)

    @block.tensor
    def _(pe):
        meet(pe)

    @block.scalar
    def _(act):
        meet(act)

    @block.vector
    def _(dve):
        meet(dve)

    @block.gpsimd
    def _(pool):
        meet(pool)


def stream(block, k, weights, n):
    k.chunks = n

    @block.sync
    def _(sp):
        split = k.flag("split_low")

        def one(i, j):
            if not isinstance(i, int) or i >= SLOTS:
                sp.wait_ge(split.sem, i + (1 - SLOTS))
            source = weights[bass.ds(i, 1)].rearrange("a p n -> (a p) n")
            sp.dma_start(k.slots[j % SLOTS][:], source).then_inc(k.slot_landed[j % SLOTS].sem, 16)
        repeat(sp, n, SLOTS, one, peel=SLOTS)


def split_high(act, k, n, parity):
    if isinstance(n, int) and n >= k.chunks:
        return
    slot = parity % SLOTS
    act.wait_ge(k.slot_landed[slot].sem, n * 8 + (16 - 8 * slot))
    if not isinstance(n, int) or n >= SLOTS:
        act.wait_ge(k.flag("slot_used").sem, n + (1 - SLOTS))
    k.nc.scalar.activation(k.high[slot][:], k.slots[slot][:], ACT.Copy).then_inc(k.flag("split_high").sem, 1)


def split_low(eng, k, n, parity):
    if isinstance(n, int) and n >= k.chunks:
        return
    slot = parity % SLOTS
    eng.wait_ge(k.flag("split_high").sem, n + 1)
    eng.tensor_tensor(k.low[slot][:], k.slots[slot][:], k.high[slot][:].bitcast(F32),
                      ALU.subtract).then_inc(k.flag("split_low").sem, 1)


def slot_wait(pe, k, n, parity, shape):
    pe.wait_ge(k.flag("split_low").sem, n + 1)
    view = lambda s: s[:, :].rearrange("p (k n) -> p k n", k=shape)
    return view(k.high[parity % SLOTS]), view(k.low[parity % SLOTS])


def split_product(k, out, lhsT, rhs, start, stop):
    (lh, ll), (rh, rl) = lhsT, rhs
    nc_matmul(k, out, lh, rh, start, False)
    nc_matmul(k, out, lh, rl, False, False)
    return nc_matmul(k, out, ll, rh, False, stop)


def bank_wait(eng, k, i, evac):
    for name in ("act_evac", "dve_evac"):
        s = k.flag(name)
        if name in evac:
            v = s.base + i - 1
            if not isinstance(i, int) or v > 0:
                eng.wait_ge(s.sem, v)
        elif isinstance(i, int) and i == 0 and s.base > 0:
            eng.wait_ge(s.sem, s.base)


def product(block, k, kind, width, groups, ktiles=KD, moving=None, stationary=None,
            act=None, dve=None, dve_per=0, unroll=2, low="vector"):
    per = ktiles // 4 if kind == "token" else 1
    first, group0 = k.chunk, k.group
    used = k.flag("slot_used")
    evac = [n for n, f in (("act_evac", act), ("dve_evac", dve)) if f]
    nk = 4 if kind == "token" else 8
    peel = 2 if group0 == 0 else 0

    @block.tensor
    def _(pe):
        def step(i, j):
            ps = k.pair[(group0 + j) % 2]
            bank_wait(pe, k, i, evac)
            for h in range(per):
                wh, wl = slot_wait(pe, k, i * per + (first + h), first + j * per + h, nk)
                if kind == "token":
                    for kt in range(4):
                        for t in range(NT):
                            last = kt == 3 and h == per - 1
                            ins = split_product(k, ps[:, t, 0:width], stationary(4 * h + kt, t, i),
                                                (wh[:, kt, :], wl[:, kt, :]), kt == 0 and h == 0, last)
                else:
                    for b in range(width // P):
                        for kt in range(8):
                            cols = slice(b * P, (b + 1) * P)
                            ins = split_product(k, ps[:, 0, b * TOK:(b + 1) * TOK], (wh[:, kt, cols], wl[:, kt, cols]),
                                                moving(kt), kt == 0, kt == 7)
                ins.then_inc(used.sem, 1)
        repeat(pe, groups, unroll, step, peel=peel)

    def program(eng, fn, s, split, st, per_steps):
        def read_out(i, j):
            eng.wait_ge(used.sem, i * per + (first + per))
            fn(i, j, k.pair[(group0 + j) % 2]).then_inc(s.sem, 1)

        def step(i, j):
            for h in range(per):
                if split:
                    split(eng, k, i * per + (first + h + 1), first + j * per + h + 1)
                if fn and h == 0 and j >= 1:
                    read_out(i - 1, j - 1)
        repeat(eng, groups, unroll, step, peel=max(peel, 1), steps=st, per=per_steps)
        if fn:
            read_out(groups - 1, groups - 1)
            s.base += groups

    @block.scalar
    def _(eng):
        program(eng, act, k.flag("act_evac"), split_high, None, 0)

    @block.vector
    def _(eng):
        if dve or low == "vector":
            program(eng, dve, k.flag("dve_evac"), split_low if low == "vector" else None, k.dve_steps, dve_per)

    @block.gpsimd
    def _(eng):
        if low == "gpsimd":
            program(eng, None, None, split_low, None, 0)
    k.chunk += per * groups
    k.group += groups


def nc_matmul(k, out, lhsT, rhs, start, stop):
    return k.nc.tensor.matmul(out, lhsT, rhs, start=start, stop=stop)


def ffn_order(pairs, downs):
    out = list(pairs[0])
    for i in range(1, len(pairs)):
        out += list(pairs[i]) + [downs[i - 1]]
    return out + [downs[-1]]


def ffn(block, k, add, conv=None):
    first, group0, n = k.chunk, k.group, NF // 2
    assert n % 2 == 1
    used, hidden = k.flag("slot_used"), k.flag("hidden_ready")
    act_evac, dve_evac = k.flag("act_evac"), k.flag("dve_evac")
    convolved, activated = k.flag("convolved"), k.flag("activated")
    nc, v = k.nc, k.nc.vector
    a_at = lambda i: first if isinstance(i, int) and i == 0 else i * 3 + (first - 1)
    acc = k.acc
    two = lambda x: x.rearrange("p (b t) -> p b t", b=2)

    @block.tensor
    def _(pe):
        for s in (act_evac, dve_evac):
            if s.base > 0:
                pe.wait_ge(s.sem, s.base)

        def down(i, j, parity):
            pe.wait_ge(hidden.sem, i + hidden.at(1))
            n_ = i * 3 + (first + 4) if not (isinstance(i, int) and i == n - 1) else first + 3 * n - 1
            wh, wl = slot_wait(pe, k, n_, parity, 2)
            for kk in range(2):
                for t in range(NT):
                    tok = slice(kk * TOK + t * P, kk * TOK + (t + 1) * P)
                    hh, hl = k.hid_high[:, j % 2, tok], k.hid_low[:, j % 2, tok]
                    for half in range(2):
                        cols = slice(half * 512, (half + 1) * 512)
                        ins = split_product(k, acc[half][:, t, :], (hh, hl), (wh[:, kk, cols], wl[:, kk, cols]),
                                            isinstance(i, int) and i == 0 and kk == 0,
                                            isinstance(i, int) and i == n - 1 and kk == 1)
            ins.then_inc(used.sem, 1)

        def step(i, j):
            ps = k.pair[(group0 + j) % 2]
            if not isinstance(i, int) or i >= 2:
                pe.wait_ge(hidden.sem, i + hidden.at(-1))
            for h in range(2):
                wh, wl = slot_wait(pe, k, a_at(i) + h, a_at(j) + h, 8)
                for b in range(2):
                    for kt in range(8):
                        cols = slice(b * P, (b + 1) * P)
                        ins = split_product(k, ps[:, h, b * TOK:(b + 1) * TOK], (wh[:, kt, cols], wl[:, kt, cols]),
                                            k.h_parts(kt), kt == 0, kt == 7)
                ins.then_inc(used.sem, 1)
            if j >= 1:
                down(i - 1, j - 1, a_at(j) + 2)
        repeat(pe, n, 2, step, peel=3)
        down(n - 1, n - 1, first + 3 * n - 1)

    @block.scalar
    def _(act):
        def step(i, j):
            late = 1 if j == 0 else 2
            for h in range(1, late + 2):
                split_high(act, k, a_at(i) + h, a_at(j) + h)
            y = k.ffn_act[:, j % 2, :]
            if conv:
                act.wait_ge(convolved.sem, i + convolved.at(1))
                nc.scalar.activation(y, k.ffn_conv[:, j % 2, :], ACT.Gelu_apprx_tanh).then_inc(activated.sem, 1)
            else:
                act.wait_ge(used.sem, a_at(i) + 1)
                if not isinstance(i, int) or i >= 2:
                    act.wait_ge(hidden.sem, i + hidden.at(-1))
                nc.scalar.activation(y, k.pair[(group0 + j) % 2][:, 0, :], ACT.Silu).then_inc(activated.sem, 1)
        repeat(act, n, 2, step, peel=3)
        split_high(act, k, first + 3 * n, first + 3 * n)

    @block.vector
    def _(dve):
        def step(i, j):
            ps = k.pair[(group0 + j) % 2]
            late = 1 if j == 0 else 2
            for h in range(1, late + 1):
                split_low(dve, k, a_at(i) + h, a_at(j) + h)
            if conv:
                cw, cb = conv
                dve.wait_ge(used.sem, a_at(i) + 1)
                y, a = two(k.ffn_conv[:, j % 2, :]), two(ps[:, 0, :])
                for b in range(2):
                    k.dve_steps.did(v.tensor_scalar(y[:, b, :], a[:, b, :], cw[:, 2, bass.ds(i * 2 + b, 1)],
                                                    cb[:, bass.ds(i * 2 + b, 1)], ALU.mult, ALU.add))
                for s in (1, 2):
                    k.dve_steps.settle(dve)
                    for b in range(2):
                        ins = v.scalar_tensor_tensor(y[:, b, s:TOK], a[:, b, 0:TOK - s],
                                                     cw[:, 2 - s, bass.ds(i * 2 + b, 1)], y[:, b, s:TOK], ALU.mult, ALU.add)
                        if s == 1:
                            k.dve_steps.did(ins)
                ins.then_inc(convolved.sem, 1)
            split_low(dve, k, a_at(i) + late + 1, a_at(j) + late + 1)
            dve.wait_ge(used.sem, a_at(i) + 2)
            dve.wait_ge(activated.sem, i + activated.at(1))
            y = k.ffn_act[:, j % 2, :]
            k.dve_steps.did(v.tensor_tensor(y, y, ps[:, 1, :], ALU.mult))
            k.dve_steps.settle(dve)
            if not isinstance(i, int) or i >= 2:
                dve.wait_ge(used.sem, i * 3 + (first + 4 - 6 + 1))
            k.dve_steps.did(v.tensor_copy(k.hid_high[:, j % 2, :], y))
            k.dve_steps.settle(dve)
            v.tensor_tensor(k.hid_low[:, j % 2, :], y, k.hid_high[:, j % 2, :].bitcast(F32), ALU.subtract
                            ).then_inc(hidden.sem, 1)
        repeat(dve, n, 2, step, peel=3, steps=k.dve_steps, per=6 if conv else 2)
        split_low(dve, k, first + 3 * n, first + 3 * n)
        dve.wait_ge(used.sem, first + 3 * n)
        for half in range(2):
            add(dve, half, acc[half]).then_inc(dve_evac.sem, 1)
    for s in (activated, hidden) + ((convolved,) if conv else ()):
        s.base += n
    dve_evac.base += 2
    k.chunk += 3 * n
    k.group += n + 1


def turn(block, k, src, ntiles, dst=None):
    turned = k.flag("turned")
    nc = k.nc
    batches = [(t, b) for t in range(NT) for b in range(ntiles // 4)]
    assert len(batches) <= 4
    high = k.flag("operand_high")
    part = lambda x, t, b: x[:, 4 * b:4 * b + 4, t * P:(t + 1) * P]
    bank = lambda n: k.bank[4 + n][:, :].rearrange("p (b t) -> p b t", b=4)

    @block.tensor
    def _(pe):
        for n, (t, b) in enumerate(batches):
            for i in range(4):
                c = (4 * b + i) * P
                ins = nc.tensor.transpose(k.bank[4 + n][:, i * P:(i + 1) * P], src[:, t, c:c + P], k.c("ident"))
            ins.then_inc(turned.sem, 1)

    @block.scalar
    def _(act):
        for n, (t, b) in enumerate(batches):
            if dst is None:
                act.wait_ge(turned.sem, turned.at(n + 1))
                nc.scalar.copy(part(k.h_high, t, b), bank(n)).then_inc(high.sem, 1)
            elif n % 2 == 0:
                act.wait_ge(turned.sem, turned.at(n + 1))
                nc.scalar.copy(part(dst, t, b), bank(n))

    @block.vector
    def _(dve):
        for n, (t, b) in enumerate(batches):
            if dst is None:
                dve.wait_ge(high.sem, high.at(n + 1))
                nc.vector.tensor_tensor(part(k.h_low, t, b), bank(n), part(k.h_high, t, b).bitcast(F32), ALU.subtract)
            elif n % 2 == 1:
                dve.wait_ge(turned.sem, turned.at(n + 1))
                nc.vector.tensor_copy(part(dst, t, b), bank(n))
    turned.base += len(batches)
    if dst is None:
        high.base += len(batches)


def operand(block, k, src, half, free):
    high, low, used = k.flag("operand_high"), k.flag("operand_low"), k.flag("slot_used")
    part = lambda x: x[:, 4 * half:4 * half + 4, :]

    @block.scalar
    def _(act):
        act.wait_ge(used.sem, free)
        k.nc.scalar.copy(part(k.h_high), src).then_inc(high.sem, 1)

    @block.vector
    def _(dve):
        dve.wait_ge(high.sem, high.at(1))
        k.nc.vector.tensor_tensor(part(k.h_low), src, part(k.h_high).bitcast(F32), ALU.subtract).then_inc(low.sem, 1)

    @block.tensor
    def _(pe):
        pe.wait_ge(low.sem, low.at(1))
    high.base += 1
    low.base += 1


def rms_norm(block, k, gain, shift=None, eps=RMS_EPS):
    nc = k.nc
    squared, meaned, rooted = k.flag("squared"), k.flag("meaned"), k.flag("rooted")
    @block.scalar
    def _(act):
        for t in range(NT):
            ins = nc.scalar.activation(k.xn[:, t, :], k.x[:, t, :], ACT.Square, accum_out=k.stat[:, t:t + 1])
        ins.then_inc(squared.sem, 1)
        act.wait_ge(meaned.sem, meaned.at(1))
        nc.scalar.activation(k.stat[:, 4:6], k.stat[:, 2:4], ACT.Sqrt).then_inc(rooted.sem, 1)

    @block.vector
    def _(dve):
        dve.wait_ge(squared.sem, squared.at(1))
        nc.vector.tensor_scalar(k.stat[:, 2:4], k.stat[:, 0:2], 1.0 / D, eps, ALU.mult, ALU.add).then_inc(meaned.sem, 1)
        dve.wait_ge(rooted.sem, rooted.at(1))
        k.dve_steps.did(nc.vector.reciprocal(k.stat[:, 6:8], k.stat[:, 4:6]))
        k.dve_steps.settle(dve)
        for t in range(NT):
            k.dve_steps.did(nc.vector.scalar_tensor_tensor(k.xn[:, t, :], k.x[:, t, :], k.stat[:, 6 + t:7 + t], gain,
                                                           ALU.mult, ALU.mult))
        if shift is not None:
            k.dve_steps.settle(dve)
            for t in range(NT):
                k.dve_steps.did(nc.vector.tensor_tensor(k.xn[:, t, :], k.xn[:, t, :], shift, ALU.add))
    for s in (squared, meaned, rooted):
        s.base += 1
    phase_end(block, k)


class Arena:

    def __init__(self, tile, size):
        self.tile, self.size, self.at = tile, size, 0

    def take(self, *shape):
        n = int(np.prod(shape))
        assert self.at + n <= self.size, (self.at, n, self.size)
        v = self.tile[:, self.at:self.at + n]
        self.at += n
        if len(shape) == 1:
            return v
        names = "abcd"[:len(shape)]
        return v.rearrange("p (" + " ".join(names) + ") -> p " + " ".join(names),
                           **{c: m for c, m in zip(names, shape)})


def attention(block, k, qkv, yT):
    nc = k.nc
    a = k.arena
    mark = a.at
    place = a.take(4 * D)
    rot = place[:, 0:2 * D].rearrange("p (t n) -> p t n", t=NT)
    part = place[:, 2 * D:4 * D].rearrange("p (t a h d) -> p t a h d", t=NT, a=2, h=16)
    PT = place[:, 0:HEADS * 384].rearrange("p (h n) -> p h n", h=HEADS)
    qkT = a.take(2 * NB, TOK)
    S = a.take(HEADS, NT, TOK)
    mx, tot, rec = k.mx, k.tot, k.rec
    scored, took, maxed, powered = (k.flag(n) for n in ("scored", "score_read", "maxed", "powered"))
    scaled = [k.flag("scaled_act"), k.flag("scaled_dve")]
    pturned, pread = k.flag("probs_turned"), [k.flag("probs_read_act"), k.flag("probs_read_dve")]
    mixed, yread, rec_ready = k.flag("mixed"), k.flag("mixed_read"), k.flag("recip_ready")
    units = [(h, t) for h in range(HEADS) for t in range(NT)]

    def rotate(op, steps, eng, t):
        src = qkv[:, t, 0:2 * WIDTH].rearrange("p (h x d) -> p x h d", h=16, x=2)
        dst = rot[:, t, :].rearrange("p (h x d) -> p x h d", h=16, x=2)
        cos = k.cos[:, t, :].unsqueeze(1).to_broadcast([P, 16, 32])
        sin = k.sin[:, t, :].unsqueeze(1).to_broadcast([P, 16, 32])
        for x, second in ((0, ALU.subtract), (1, ALU.add)):
            steps.did(op(part[:, t, 0], src[:, x], cos, ALU.mult))
            steps.did(op(part[:, t, 1], src[:, 1 - x], sin, ALU.mult))
            steps.settle(eng)
            steps.did(op(dst[:, x], part[:, t, 0], part[:, t, 1], second))
            steps.settle(eng)

    @block.vector
    def _(dve):
        rotate(nc.vector.tensor_tensor, k.dve_steps, dve, 0)

    @block.gpsimd
    def _(pool):
        rotate(nc.gpsimd.tensor_tensor, k.pool_steps, pool, 1)
    phase_end(block, k)
    turn(block, k, rot, 2 * NB, qkT)
    phase_end(block, k)

    def mix(pe, h):
        pe.wait_ge(pread[h % 2].sem, pread[h % 2].at(h // 2 + 1))
        b = h // 2
        if h % 2 == 0 and b >= 2:
            pe.wait_ge(yread.sem, yread.at(b - 1))
        o = k.bank[4 + b % 2][64 * (h % 2):64 * (h % 2) + 64, 0:TOK]
        v = lambda s: qkv[:, s, 2 * WIDTH + h * DH:2 * WIDTH + (h + 1) * DH]
        nc_matmul(k, o, v(0), PT[:, h, 0:TOK], True, False)
        nc_matmul(k, o[:, P:TOK], v(1), PT[:, h, TOK:384], False, True).then_inc(mixed.sem, 1)

    def out(act, b):
        act.wait_ge(mixed.sem, mixed.at(2 * b + 2))
        nc.scalar.copy(yT[:, b, :], k.bank[4 + b % 2][:, 0:TOK]).then_inc(yread.sem, 1)
    @block.tensor
    def _(pe):
        for u, (h, t) in enumerate(units):
            if u >= 2:
                pe.wait_ge(took.sem, took.at(u - 1))
            p0, n = 64 * (h % 2), (t + 1) * P
            nc_matmul(k, k.bank[4 + u % 2][:, 0:n], qkT[p0:p0 + 64, h // 2, t * P:(t + 1) * P],
                      qkT[p0:p0 + 64, NB + h // 2, 0:n], True, True).then_inc(scored.sem, 1)
        for h in range(HEADS):
            pe.wait_ge(scaled[h % 2].sem, scaled[h % 2].at(h // 2 + 1))
            if h >= 2:
                pe.wait_ge(pread[h % 2].sem, pread[h % 2].at(h // 2))
            for i, (t, s) in enumerate(((0, 0), (1, 0), (1, 1))):
                ins = nc.tensor.transpose(k.bank[6 + h % 2][:, i * P:(i + 1) * P], S[:, h, t, s * P:(s + 1) * P],
                                          k.c("ident"))
            ins.then_inc(pturned.sem, 1)
            if h >= 1:
                mix(pe, h - 1)
        mix(pe, HEADS - 1)

    @block.vector
    def _(dve):
        for u in range(len(units) + 3):
            if u < len(units):
                h, t = units[u]
                n = (t + 1) * P
                dve.wait_ge(scored.sem, scored.at(u + 1))
                nc.vector.scalar_tensor_tensor(S[:, h, t, 0:n], k.bank[4 + u % 2][:, 0:n], DH ** -0.5,
                                               k.blocked[:, t, 0:n], ALU.mult, ALU.add).then_inc(took.sem, 1)
            if 1 <= u <= len(units):
                h, t = units[u - 1]
                dve.wait_ge(took.sem, took.at(u))
                nc.vector.tensor_reduce(mx[:, u - 1:u], S[:, h, t, 0:(t + 1) * P], AX.X, ALU.max,
                                        negate=True).then_inc(maxed.sem, 1)
            if u >= 3:
                h, t = units[u - 3]
                n = (t + 1) * P
                dve.wait_ge(powered.sem, powered.at(u - 2))
                k.dve_steps.did(nc.vector.scalar_tensor_tensor(
                    S[:, h, t, 0:n], S[:, h, t, 0:n], 1.0, k.count[:, t, 0:n], ALU.mult, ALU.mult,
                    accum_out=tot[:, u - 3:u - 2]))
        k.dve_steps.settle(dve)
        nc.vector.reciprocal(rec[:, 0:16], tot[:, 0:16]).then_inc(rec_ready.sem, 1)
        dve.wait_ge(rec_ready.sem, rec_ready.at(1))
        for h in range(1, HEADS, 2):
            for t in range(NT):
                n = (t + 1) * P
                ins = nc.vector.tensor_scalar(S[:, h, t, 0:n], S[:, h, t, 0:n], rec[:, 2 * h + t:2 * h + t + 1], None,
                                              ALU.mult)
            ins.then_inc(scaled[1].sem, 1)
        for h in range(1, HEADS, 2):
            dve.wait_ge(pturned.sem, pturned.at(h + 1))
            nc.vector.tensor_copy(PT[:, h, :], k.bank[6 + h % 2][:, 0:384]).then_inc(pread[1].sem, 1)

    @block.scalar
    def _(act):
        for u, (h, t) in enumerate(units):
            n = (t + 1) * P
            act.wait_ge(maxed.sem, maxed.at(u + 1))
            nc.scalar.activation(S[:, h, t, 0:n], S[:, h, t, 0:n], ACT.Exp, bias=mx[:, u:u + 1]).then_inc(powered.sem, 1)
        act.wait_ge(rec_ready.sem, rec_ready.at(1))
        for h in range(0, HEADS, 2):
            for t in range(NT):
                n = (t + 1) * P
                ins = nc.scalar.activation(S[:, h, t, 0:n], S[:, h, t, 0:n], ACT.Copy,
                                           scale=rec[:, 2 * h + t:2 * h + t + 1])
            ins.then_inc(scaled[0].sem, 1)
        for h in range(0, HEADS, 2):
            act.wait_ge(pturned.sem, pturned.at(h + 1))
            nc.scalar.copy(PT[:, h, :], k.bank[6 + h % 2][:, 0:384]).then_inc(pread[0].sem, 1)
            if h >= 2:
                out(act, h // 2 - 1)
        out(act, NB - 1)

    for s, n in ((scored, 16), (took, 16), (maxed, 16), (powered, 16), (rec_ready, 1), (scaled[0], 4), (scaled[1], 4),
                 (pturned, 8), (pread[0], 4), (pread[1], 4), (mixed, 8), (yread, 4)):
        s.base += n
    phase_end(block, k)
    a.at = mark


def turn_back(block, k, src, dst):
    turned, read = k.flag("turned"), k.flag("turn_read0")
    nc = k.nc

    @block.tensor
    def _(pe):
        for t in range(NT):
            for b in range(NB):
                ins = nc.tensor.transpose(k.bank[4 + t][:, b * P:(b + 1) * P], src[:, b, t * P:(t + 1) * P], k.c("ident"))
            ins.then_inc(turned.sem, 1)

    @block.scalar
    def _(act):
        for t in range(NT):
            act.wait_ge(turned.sem, turned.at(t + 1))
            nc.scalar.copy(dst[:, t, :], k.bank[4 + t][:, :]).then_inc(read.sem, 1)
    turned.base += NT
    read.base += NT
    phase_end(block, k)


def delta_rule(block, k, AR, BT, KT, Btok, Ktok, Vtok, S, W, U, ends, y):
    nc, v, big = k.nc, k.nc.vector, k.big
    steps = k.dve_steps
    LEVELS = range(1, 6)
    wide8 = lambda x: x.rearrange("p (h t) -> p h t", h=HEADS)
    L, AK, RB, RK, Z, X, T = (k.arena.tile[:, k.gram_at + n * D:k.gram_at + (n + 1) * D] for n in range(7))
    AV = k.xn[:, 0, 0:WIDTH]
    over = lambda m, n=HEADS: k.c(m).unsqueeze(1).to_broadcast([P, n, P])
    head = lambda h: slice(64 * (h % 2), 64 * (h % 2) + 64)
    hp = lambda h: slice(((h % 2) * NB + h // 2) * P, ((h % 2) * NB + h // 2 + 1) * P)
    hv = lambda h: slice(h * DH, (h + 1) * DH)
    side = lambda x: slice(x * 512, (x + 1) * 512)
    heads = lambda x: range(x, HEADS, 2)
    grams, masked = k.flag("grams_done"), k.flag("grams_masked")
    lz, t_ready, second, z_added = (k.flag(n) for n in ("lz_done", "t_ready", "z_products", "z_added"))
    av, av_read = k.flag("av_done"), k.flag("av_read")
    as_done, w_ready, zw_done, u_ready = (k.flag(n) for n in ("as_done", "w_ready", "zw_done", "u_ready"))
    kv_done, bu_done, s_ready = (k.flag(n) for n in ("kv_done", "bu_done", "s_ready"))
    rs_done, rs_read, inner_done, inner_read = (k.flag(n) for n in ("rs_done", "rs_read", "inner_done", "inner_read"))
    chunks = lambda t: (2 * t, 2 * t + 1)
    where = lambda c: slice(64 * (c % 2), 64 * (c % 2) + 64)
    tokens = lambda c: slice(c * CHUNK, (c + 1) * CHUNK)

    @block.tensor
    def _(pe):
        for t in range(NT):
            tt = slice(t * P, (t + 1) * P)
            A_ = lambda h: AR[head(h), h // 2, 0, tt]
            R_ = lambda h: AR[head(h), h // 2, 1, tt]
            B_ = lambda h: BT[head(h), h // 2, tt]
            K_ = lambda h: KT[head(h), h // 2, tt]

            def gram(n, lhs, rhs):
                for h in range(HEADS):
                    ins = nc_matmul(k, big[n][:, hp(h)], lhs(h), rhs(h), True, True)
                ins.then_inc(grams.sem, 1)
            if t > 0:
                pe.wait_ge(s_ready.sem, s_ready.at(2 * t))
            gram(0, B_, A_)
            gram(1, A_, B_)
            gram(2, K_, A_)
            if t > 0:
                pe.wait_ge(rs_read.sem, rs_read.at(2 * t))
                pe.wait_ge(inner_read.sem, inner_read.at(t))
            gram(3, B_, R_)
            pe.wait_ge(masked.sem, masked.at(t + 1))
            for n, level in enumerate(LEVELS):
                for x in range(2):
                    if n > 0:
                        pe.wait_ge(z_added.sem, z_added.at(t * 10 + 2 * (n - 1) + x + 1))
                    for h in heads(x):
                        ins = nc_matmul(k, big[1][:, hp(h)], L[:, hp(h)], Z[:, hp(h)], True, True)
                    ins.then_inc(lz.sem, 1)
                if n == 0:
                    gram(0, K_, R_)
                for x in range(2):
                    pe.wait_ge(t_ready.sem, t_ready.at(t * 10 + 2 * n + x + 1))
                    for h in heads(x):
                        ins = nc_matmul(k, big[2][:, hp(h)], X[:, hp(h)], T[:, hp(h)], True, True)
                    for h in heads(x):
                        if level < 5:
                            ins = nc_matmul(k, big[3][:, hp(h)], T[:, hp(h)], X[:, hp(h)], True, True)
                    ins.then_inc(second.sem, 1)
                if level == 5:
                    for h in range(HEADS):
                        ins = nc_matmul(k, k.bank[7][:, hv(h)], AK[:, hp(h)], Vtok[:, t, hv(h)], True, True)
                    ins.then_inc(av.sem, 1)
            pe.wait_ge(z_added.sem, z_added.at(t * 10 + 10))
            for c in chunks(t):
                rows, now = where(c), S[:, c % 2]
                if c > 0:
                    pe.wait_ge(s_ready.sem, s_ready.at(c))
                for h in range(HEADS):
                    ins = nc_matmul(k, k.bank[h % 2][rows, (h // 2) * DH:(h // 2 + 1) * DH],
                                    AR[head(h), h // 2, 0, tokens(c)], now[head(h), h // 2, :], True, True)
                ins.then_inc(as_done.sem, 1)
                for h in range(HEADS):
                    ins = nc_matmul(k, k.bank[5][head(h), (h // 2) * 64:(h // 2) * 64 + 64], Ktok[rows, t, hv(h)],
                                    Vtok[rows, t, hv(h)], True, True)
                ins.then_inc(kv_done.sem, 1)
                pe.wait_ge(w_ready.sem, w_ready.at(c + 1))
                for h in range(HEADS):
                    inner = slice(hp(h).start + rows.start, hp(h).start + rows.stop)
                    ins = nc_matmul(k, k.bank[2][rows, hv(h)], Z[rows, inner], W[rows, hv(h)], True, True)
                ins.then_inc(zw_done.sem, 1)
                if c > 0:
                    pe.wait_ge(rs_read.sem, rs_read.at(c))
                for h in range(HEADS):
                    ins = nc_matmul(k, k.bank[6][head(h), (h // 2) * 64:(h // 2) * 64 + 64], now[head(h), h // 2, :],
                                    AR[head(h), h // 2, 1, tokens(c)], True, True)
                ins.then_inc(rs_done.sem, 1)
                pe.wait_ge(u_ready.sem, u_ready.at(c + 1))
                for h in range(HEADS):
                    ins = nc_matmul(k, k.bank[4][head(h), (h // 2) * 64:(h // 2) * 64 + 64], Btok[rows, t, hv(h)],
                                    U[rows, hv(h)], True, True)
                ins.then_inc(bu_done.sem, 1)
            for h in range(HEADS):
                o = k.bank[7][head(h), (h // 2) * P:(h // 2 + 1) * P]
                nc_matmul(k, o, U[:, hv(h)], RB[:, hp(h)], True, False)
                ins = nc_matmul(k, o, Vtok[:, t, hv(h)], RK[:, hp(h)], False, True)
            ins.then_inc(inner_done.sem, 1)

    @block.vector
    def _(dve):
        for t in range(NT):
            dve.wait_ge(grams.sem, grams.at(5 * t + 1))
            steps.did(v.tensor_tensor(wide8(Z), wide8(big[0]), over("level0"), ALU.mult))
            dve.wait_ge(grams.sem, grams.at(5 * t + 2))
            v.tensor_tensor(wide8(L), wide8(big[1]), over("strict_lo"), ALU.mult)
            steps.did(v.tensor_tensor(wide8(X), wide8(big[1]), over("lower0"), ALU.mult))
            steps.settle(dve)
            v.tensor_tensor(wide8(Z), wide8(Z), over("ident"), ALU.add)
            v.tensor_tensor(wide8(X), wide8(X), over("ident"), ALU.add).then_inc(masked.sem, 1)
            for n, dst, m in ((3, AK, "strict_up"), (4, RB, "incl_up")):
                dve.wait_ge(grams.sem, grams.at(5 * t + n))
                v.tensor_tensor(wide8(dst), wide8(big[n - 1]), over(m), ALU.mult)
            for n, level in enumerate(LEVELS):
                for x in range(2):
                    dve.wait_ge(lz.sem, lz.at(t * 10 + 2 * n + x + 1))
                    four_heads = lambda a: a[:, side(x)].rearrange("p (h t) -> p h t", h=NB)
                    v.tensor_tensor(four_heads(T), four_heads(big[1]), over(f"level{level}", NB), ALU.mult
                                    ).then_inc(t_ready.sem, 1)
                if n == 0:
                    dve.wait_ge(grams.sem, grams.at(5 * t + 5))
                    v.tensor_tensor(wide8(RK), wide8(big[0]), over("incl_up"), ALU.mult)
                for x in range(2):
                    dve.wait_ge(second.sem, second.at(t * 10 + 2 * n + x + 1))
                    v.tensor_tensor(Z[:, side(x)], Z[:, side(x)], big[2][:, side(x)], ALU.add).then_inc(z_added.sem, 1)
                    if level < 5:
                        v.tensor_tensor(X[:, side(x)], X[:, side(x)], big[3][:, side(x)], ALU.add)
            dve.wait_ge(av_read.sem, av_read.at(t + 1))
            for c in chunks(t):
                rows, now, nxt = where(c), S[:, c % 2], S[:, (c + 1) % 2]
                pairs = lambda x: x[rows, :].rearrange("p (b x d) -> p x b d", x=2, d=DH)
                flat = lambda x: x.rearrange("p b t -> p (b t)")
                dve.wait_ge(as_done.sem, as_done.at(c + 1))
                for x in range(2):
                    ins = v.tensor_tensor(pairs(W)[:, x], k.bank[x][rows, 0:256].rearrange("p (b d) -> p b d", d=DH),
                                          pairs(AV)[:, x], ALU.add)
                ins.then_inc(w_ready.sem, 1)
                dve.wait_ge(kv_done.sem, kv_done.at(c + 1))
                steps.did(v.tensor_tensor(flat(nxt), flat(now), k.bank[5][:, 0:256], ALU.add))
                steps.settle(dve)
                steps.did(v.tensor_tensor(nxt, nxt, ends[:, :, c:c + 1].to_broadcast([P, NB, 64]), ALU.mult))
                dve.wait_ge(zw_done.sem, zw_done.at(c + 1))
                v.tensor_copy(U[rows, :], k.bank[2][rows, :]).then_inc(u_ready.sem, 1)
                dve.wait_ge(bu_done.sem, bu_done.at(c + 1))
                steps.settle(dve)
                for b in range(NB):
                    ins = v.scalar_tensor_tensor(nxt[:, b, :], k.bank[4][:, b * 64:(b + 1) * 64], ends[:, b, c:c + 1],
                                                 nxt[:, b, :], ALU.mult, ALU.add)
                ins.then_inc(s_ready.sem, 1)
            yt = flat4(y)[:, :, t * P:(t + 1) * P]
            dve.wait_ge(rs_read.sem, rs_read.at(2 * t + 2))
            dve.wait_ge(inner_done.sem, inner_done.at(t + 1))
            v.tensor_tensor(yt, yt, flat4(k.bank[7]), ALU.add).then_inc(inner_read.sem, 1)

    @block.scalar
    def _(act):
        for t in range(NT):
            act.wait_ge(av.sem, av.at(t + 1))
            nc.scalar.copy(AV, k.bank[7]).then_inc(av_read.sem, 1)
            for c in chunks(t):
                act.wait_ge(rs_done.sem, rs_done.at(c + 1))
                nc.scalar.copy(flat4(y)[:, :, tokens(c)], k.bank[6][:, 0:256].rearrange("p (b t) -> p b t", b=NB)
                               ).then_inc(rs_read.sem, 1)
    for s, n in ((grams, 5), (masked, 1), (lz, 10), (t_ready, 10), (second, 10), (z_added, 10), (av, 1), (av_read, 1),
                 (as_done, 2), (w_ready, 2), (zw_done, 2), (u_ready, 2), (kv_done, 2), (bu_done, 2), (s_ready, 2),
                 (rs_done, 2), (rs_read, 2), (inner_done, 1), (inner_read, 1)):
        s.base += NT * n


def rwkv(block, k, zT, wide, scratch, keep, yT):
    nc, v = k.nc, k.nc.vector
    steps = k.dve_steps
    AR, BT, KT, g, bonus, Btok, Ktok, Vtok, y, S, W, U, ends = keep
    T2, T3, T4, small = scratch
    T0, T1, T5 = (flat4(x) for x in (k.xn[:, 0, :], k.xn[:, 1, :], y))
    T2, T3, T4 = flat4(T2), flat4(T3), flat4(T4)
    T0f = k.xn[:, 0, :]
    diff = k.arena.tile[:, k.tok_at:k.tok_at + NZ * TOK].rearrange("p (b t) -> p b t", t=TOK)
    R, K, V = zT[:, 0:4, :], zT[:, 4:8, :], zT[:, 8:12, :]
    th, sgx = small[:, 0:TOK], small[:, TOK:2 * TOK]
    lora, g_up = wide[:, 0:WIDTH], wide[:, WIDTH:2 * WIDTH]
    big = k.big
    four = lambda i: flat4(big[i])
    blk = lambda name, b: k.col[name][:, b:b + 1]

    @block.gpsimd
    def _(pool):
        nc.gpsimd.tensor_tensor(diff[:, 0:7, 1:TOK], zT[:, 0:7, 0:TOK - 1], zT[:, 0:7, 1:TOK], ALU.subtract)
        nc.gpsimd.tensor_scalar(diff[:, 0:7, 0:1], zT[:, 0:7, 0:1], -1.0, None, ALU.mult)

    @block.vector
    def _(dve):
        v.tensor_tensor(diff[:, 7:NZ, 1:TOK], zT[:, 7:NZ, 0:TOK - 1], zT[:, 7:NZ, 1:TOK], ALU.subtract)
        v.tensor_scalar(diff[:, 7:NZ, 0:1], zT[:, 7:NZ, 0:1], -1.0, None, ALU.mult)
    phase_end(block, k)

    @block.vector
    def _(dve):
        for b in list(range(12, NZ)) + list(range(12)):
            v.scalar_tensor_tensor(zT[:, b, :], diff[:, b, :], k.col["mu"][:, b:b + 1], zT[:, b, :], ALU.mult, ALU.add)
    phase_end(block, k)

    @block.scalar
    def _(act):
        nc.scalar.activation(th[0:64, :], zT[0:64, 12, :], ACT.Tanh)
        nc.scalar.activation(sgx, zT[:, 13, :], ACT.Sigmoid)
    phase_end(block, k)

    @block.tensor
    def _(pe):
        for t in range(NT):
            o = big[0][:, t * WIDTH:(t + 1) * WIDTH]
            nc_matmul(k, o, th[0:64, t * P:(t + 1) * P], lora[0:64, :], True, False)
            nc_matmul(k, o, k.c("ones")[0:1, :], k.w0[0:1, :], False, True)
        for b in range(NB):
            nc_matmul(k, big[1][:, b * TOK:(b + 1) * TOK], lora[64:P, b * P:(b + 1) * P], zT[64:P, 12, :], True, True)
            nc_matmul(k, big[2][:, b * TOK:(b + 1) * TOK], g_up[:, b * P:(b + 1) * P], sgx, True, True)
    phase_end(block, k)

    @block.scalar
    def _(act):
        nc.scalar.activation(T0f, big[0], ACT.Sigmoid)
        for b in range(NB):
            nc.scalar.activation(T1[:, b, :], four(1)[:, b, :], ACT.Sigmoid, bias=blk("a0", b))

    @block.vector
    def _(dve):
        v.tensor_copy(g, big[2])
        for b in range(NB):
            steps.did(v.tensor_scalar(T5[:, b, :], K[:, b, :], blk("k_k", b), None, ALU.mult))
    phase_end(block, k)

    @block.tensor
    def _(pe):
        for n, m in ((0, "incl_up"), (1, "strict_up")):
            for b in range(NB):
                for t in range(NT):
                    nc_matmul(k, four(n)[:, b, t * P:(t + 1) * P], T0f[:, t * WIDTH + b * P:t * WIDTH + (b + 1) * P],
                              k.c(m), True, True)

    @block.vector
    def _(dve):
        v.tensor_tensor(diff[:, 0:4, :], T5, T5, ALU.mult)
        for b in range(NB):
            steps.did(v.tensor_scalar(diff[:, 4 + b, :], T1[:, b, :], -1.0, blk("k_a", b), ALU.add, ALU.mult))
        steps.settle(dve)
        v.scalar_tensor_tensor(K, diff[:, 4:8, :], 1.0, K, ALU.add, ALU.mult)
    phase_end(block, k)

    @block.tensor
    def _(pe):
        for half in range(2):
            nc_matmul(k, big[2][:, half * 512:(half + 1) * 512], k.c("blockones"),
                      diff[:, 2 * half:2 * half + 2, :].rearrange("p b t -> p (b t)"), True, True)

    @block.scalar
    def _(act):
        nc.scalar.activation(T2, four(0), ACT.Exp, scale=-DECAY)
        nc.scalar.activation(T3, four(0), ACT.Exp, scale=DECAY)
        nc.scalar.activation(T4, four(1), ACT.Exp, scale=-DECAY)

    @block.vector
    def _(dve):
        steps.did(v.tensor_tensor(T0, R, K, ALU.mult))
        steps.settle(dve)
        for b in range(NB):
            v.tensor_scalar(T0[:, b, :], T0[:, b, :], blk("r_k", b), None, ALU.mult)
    phase_end(block, k)

    @block.tensor
    def _(pe):
        for half in range(2):
            nc_matmul(k, big[3][:, half * 512:(half + 1) * 512], k.c("blockones"), T0f[:, half * 512:(half + 1) * 512],
                      True, True)

    @block.scalar
    def _(act):
        nc.scalar.activation(diff[:, 4:8, :], four(2), ACT.Sqrt)

    @block.gpsimd
    def _(pool):
        nc.gpsimd.tensor_copy(ends, T2[:, :, CHUNK - 1:TOK:CHUNK])
        nc.gpsimd.tensor_tensor(AR[:, :, 1, :], R, T2, ALU.mult)
        nc.gpsimd.tensor_tensor(KT, K, T3, ALU.mult)
    phase_end(block, k)

    @block.vector
    def _(dve):
        v.tensor_tensor(flat4(bonus), four(3), V, ALU.mult)
        steps.did(v.tensor_scalar(diff[:, 4:8, :], diff[:, 4:8, :], 1e-12, None, ALU.max))
        steps.settle(dve)
        steps.did(v.reciprocal(diff[:, 4:8, :], diff[:, 4:8, :]))
        steps.settle(dve)
        steps.did(v.tensor_tensor(T5, T5, diff[:, 4:8, :], ALU.mult))
        steps.settle(dve)
        v.scalar_tensor_tensor(AR[:, :, 0, :], T5, -1.0, T4, ALU.mult, ALU.mult)
        steps.did(v.tensor_tensor(T1, T5, T1, ALU.mult))
        steps.settle(dve)
        v.tensor_tensor(BT, T1, T3, ALU.mult)
    phase_end(block, k)
    for src, dst in ((BT, Btok), (KT, Ktok), (V, Vtok)):
        turn_back(block, k, src, dst)

    @block.vector
    def _(dve):
        v.memset(S[:, 0], 0.0)
    phase_end(block, k)
    delta_rule(block, k, AR, BT, KT, Btok, Ktok, Vtok, S, W, U, ends, y)
    phase_end(block, k)

    def head_sum(x):
        @block.tensor
        def _(pe):
            for half in range(2):
                nc_matmul(k, big[0][:, half * 512:(half + 1) * 512], k.c("blockones"), x[:, half * 512:(half + 1) * 512],
                          True, True)
        phase_end(block, k)
    head_sum(y)

    @block.vector
    def _(dve):
        steps.did(v.scalar_tensor_tensor(y, big[0], -1.0 / DH, y, ALU.mult, ALU.add))
        steps.settle(dve)
        v.tensor_tensor(T0f, y, y, ALU.mult)
    phase_end(block, k)
    head_sum(T0f)

    @block.vector
    def _(dve):
        v.tensor_scalar(T0f, big[0], 1.0 / DH, GN_EPS, ALU.mult, ALU.add)
    phase_end(block, k)

    @block.scalar
    def _(act):
        nc.scalar.activation(T0f, T0f, ACT.Sqrt)
    phase_end(block, k)

    @block.vector
    def _(dve):
        steps.did(v.reciprocal(T0f, T0f))
        steps.settle(dve)
        steps.did(v.tensor_tensor(y, y, T0f, ALU.mult))
        steps.settle(dve)
        for b in range(NB):
            steps.did(v.tensor_scalar(flat4(y)[:, b, :], flat4(y)[:, b, :], blk("gn_w", b), blk("gn_b", b), ALU.mult, ALU.add))
        steps.settle(dve)
        steps.did(v.tensor_tensor(y, y, bonus, ALU.add))
        steps.settle(dve)
        v.tensor_tensor(yT, flat4(y), flat4(g), ALU.mult)
    phase_end(block, k)


def flat4(x):
    return x.rearrange("p (b t) -> p b t", b=NB)


def gmlp(block, k, uv, w_s, yT):
    nc, v = k.nc, k.nc.vector
    steps = k.dve_steps
    ln_g, ln_b = k.ln[:, 0:WIDTH], k.ln[:, WIDTH:2 * WIDTH]
    vv = lambda t: uv[:, t, WIDTH:2 * WIDTH]

    @block.gpsimd
    def _(pool):
        nc.gpsimd.tensor_tensor(w_s.rearrange("p (g i) -> p g i", g=HEADS), w_s.rearrange("p (g i) -> p g i", g=HEADS),
                                k.c("upper").unsqueeze(1).to_broadcast([P, HEADS, P]), ALU.mult)

    @block.vector
    def _(dve):
        for t in range(NT):
            steps.did(v.tensor_reduce(k.stat[:, t:t + 1], vv(t), AX.X, ALU.add))
        steps.settle(dve)
        steps.did(v.tensor_scalar(k.stat[:, 2:4], k.stat[:, 0:2], -1.0 / WIDTH, None, ALU.mult))
        steps.settle(dve)
        for t in range(NT):
            v.tensor_scalar(vv(t), vv(t), k.stat[:, 2 + t:3 + t], None, ALU.add)
    phase_end(block, k)

    @block.scalar
    def _(act):
        for t in range(NT):
            nc.scalar.activation(k.xn[:, t, 0:WIDTH], vv(t), ACT.Square, accum_out=k.stat[:, t:t + 1])
    phase_end(block, k)

    @block.vector
    def _(dve):
        v.tensor_scalar(k.stat[:, 2:4], k.stat[:, 0:2], 1.0 / WIDTH, LN_EPS, ALU.mult, ALU.add)
    phase_end(block, k)

    @block.scalar
    def _(act):
        nc.scalar.activation(k.stat[:, 4:6], k.stat[:, 2:4], ACT.Sqrt)
    phase_end(block, k)

    @block.vector
    def _(dve):
        steps.did(v.reciprocal(k.stat[:, 6:8], k.stat[:, 4:6]))
        steps.settle(dve)
        for t in range(NT):
            steps.did(v.scalar_tensor_tensor(vv(t), vv(t), k.stat[:, 6 + t:7 + t], ln_g, ALU.mult, ALU.mult))
        steps.settle(dve)
        for t in range(NT):
            v.tensor_tensor(vv(t), vv(t), ln_b, ALU.add)
    phase_end(block, k)

    @block.tensor
    def _(pe):
        for t in range(NT):
            for g in range(HEADS):
                nc_matmul(k, k.bank[4 + t][:, g * 64:(g + 1) * 64], w_s[:, g * P:(g + 1) * P],
                          uv[:, t, WIDTH + g * 64:WIDTH + (g + 1) * 64], True, True)
    phase_end(block, k)

    @block.vector
    def _(dve):
        for t in range(NT):
            for g in range(HEADS):
                u = uv[:, t, g * 64:(g + 1) * 64]
                v.scalar_tensor_tensor(u, k.bank[4 + t][:, g * 64:(g + 1) * 64], k.col["b_s"][:, g:g + 1], u, ALU.add,
                                       ALU.mult)
    phase_end(block, k)
    turn(block, k, uv, NB, yT)
    phase_end(block, k)


def chunk_arrays():
    def tiles(m):
        return m.reshape(-1, P, m.shape[1]).transpose(1, 0, 2).reshape(P, SLOT)

    def token(m, kt=4):
        n = SLOT // kt
        return [tiles(m[r:r + kt * P, c:c + n]) for c in range(0, m.shape[1], n) for r in range(0, m.shape[0], kt * P)]

    def channel(m):
        return token(m, 8)

    def ffn(a, g, d):
        return ffn_order(list(zip(channel(a), channel(g))), [tiles(d[r:r + 2 * P]) for r in range(0, D_FF, 2 * P)])
    return token, channel, ffn


def first_stream(v, l):
    token, channel, ffn = chunk_arrays()
    w = v["w_in"][l]
    out = token(w[:, :RWKV0]) + channel(w[:, RWKV0:UV0]) + token(w[:, UV0:])
    out += [c for n in range(3) for c in token(v["w_branch"][l, n])] + token(v["w_out"][l])
    out += ffn(v["ffn_w_up"][l][:, :D_FF], v["ffn_w_up"][l][:, D_FF:], v["ffn_w_down"][l])
    return np.stack(out)


FIRST_COLS = {"c": KD, "mu": NZ, "a0": NB, "k_k": NB, "k_a": NB, "r_k": NB, "gn_w": NB, "gn_b": NB,
              "conv_w": 3 * NF, "conv_b": NF, "b_s": HEADS}
FIRST_WIDE = {"lora": WIDTH, "g_up": WIDTH, "w_s": HEADS * P}


def first_small(v, l):
    col = lambda a: a.reshape(-1, P).T
    cols = [col(v["c"][0]), col(v["rwkv_mu"][l]), col(v["rwkv_a0"][l]), col(v["rwkv_k_k"][l]), col(v["rwkv_k_a"][l]),
            col(v["rwkv_r_k"][l].reshape(-1)), col(v["rwkv_gn_w"][l]), col(v["rwkv_gn_b"][l]),
            col(v["ffn_conv_w"][l].reshape(-1)), col(v["ffn_conv_b"][l]), v["gmlp_b_s"][l].T]
    wide = [np.concatenate([v["rwkv_w_up"][l], v["rwkv_a_up"][l]]), v["rwkv_g_up"][l],
            v["gmlp_w_s"][l].transpose(2, 0, 1).reshape(P, -1)]
    rows = [v["b_ada"][l], v["rwkv_w0"][l]]
    spread = [v["norm_mix"][l], v["norm_ffn"][l], v["gmlp_ln_g"][l], v["gmlp_ln_b"][l]]
    return [np.concatenate(cols, 1), np.concatenate(wide, 1), np.concatenate(rows), np.concatenate(spread)]


def columns(tile, sizes):
    out, at = {}, 0
    for name, n in sizes.items():
        out[name] = tile[:, at:at + n]
        at += n
    return out


def modulation(block, k, weights, cact, rowb, ring, sums):
    nc, v = k.nc, k.nc.vector
    landed = [k.flag(f"ada_landed{i}") for i in range(ADA_SLOTS)]
    used, summed, copied, c_ready = k.flag("ada_used"), k.flag("ada_summed"), k.flag("ada_copied"), k.flag("c_ready")
    groups = 3
    both = lambda g: [k.big[2 * (g % 2) + half] for half in range(2)]

    @block.sync
    def _(sp):
        for n in range(groups * KD):
            if n >= ADA_SLOTS:
                sp.wait_ge(used.sem, n + 1 - ADA_SLOTS)
            sp.dma_start(ring[n % ADA_SLOTS], weights[n]).then_inc(landed[n % ADA_SLOTS].sem, 16)

    @block.vector
    def _(dve):
        dve.wait_ge(c_ready.sem, c_ready.at(1))
        for n in range(groups * KD):
            g, kt = divmod(n, KD)
            w, total, scale = ring[n % ADA_SLOTS], sums[g % 2], cact[:, kt:kt + 1]
            dve.wait_ge(landed[n % ADA_SLOTS].sem, 16 * (n // ADA_SLOTS + 1))
            if kt == 0:
                if g >= 2:
                    dve.wait_ge(summed.sem, summed.at(g - 1))
                ins = v.tensor_scalar(total, w, scale, None, ALU.mult)
            else:
                dve.wait_ge(used.sem, used.at(n))
                ins = v.scalar_tensor_tensor(total, w, scale, total, ALU.mult, ALU.add)
            ins.then_inc(used.sem, 1)

    @block.tensor
    def _(pe):
        pe.wait_ge(k.flag("small_landed").sem, k.flag("small_landed").base)
        for g in range(groups):
            pe.wait_ge(used.sem, used.at(KD * (g + 1)))
            if g >= 2:
                pe.wait_ge(copied.sem, copied.at(g - 1))
            for q in range(4):
                o, at = both(g)[q // 2][:, (q % 2) * 512:(q % 2 + 1) * 512], g * SLOT + q * 512
                nc_matmul(k, o, k.c("ones"), sums[g % 2][:, q * 512:(q + 1) * 512], True, False)
                ins = nc_matmul(k, o, k.c("ones")[0:1, :], rowb[0:1, at:at + 512], False, True)
            ins.then_inc(summed.sem, 1)

    @block.scalar
    def _(act):
        for g in range(groups):
            act.wait_ge(summed.sem, summed.at(g + 1))
            for half in range(2):
                at = g * SLOT + half * D
                ins = nc.scalar.copy(mod_flat(k)[:, at:at + D], both(g)[half])
            ins.then_inc(copied.sem, 1)
    used.base += groups * KD
    summed.base += groups
    copied.base += groups
    c_ready.base += 1
    for s in landed:
        s.base += 16 * (groups * KD // ADA_SLOTS)


def first_layer(block, k, A, l):
    nc = k.nc
    a = k.arena
    a.at = 0
    mod = a.take(6, D)
    yT = a.take(3 * NB, TOK)
    body = a.at
    small = k.flag("small_landed")
    rowb = a.take(6 * D)
    cact, spread = a.take(KD), a.take(2 * D)
    parts = lambda kt, t: (k.h_high[:, kt, t * P:(t + 1) * P], k.h_low[:, kt, t * P:(t + 1) * P])
    tok = lambda kt, t, i: parts(kt, t)
    row = lambda name: A[name][bass.ds(l, 1)]
    ring = [a.take(SLOT) for _ in range(ADA_SLOTS)]

    @block.scalar
    def _(act):
        act.dma_start(k.cols1[:], row("cols1").rearrange("a p n -> (a p) n")).then_inc(k.flag("cols_landed").sem, 16)
        for dst, src in ((rowb[0:1, :], row("rows1")[:, 0:6 * D]), (k.w0[0:1, :], row("rows1")[:, 6 * D:6 * D + WIDTH]),
                         (spread, row("spread1")[:, 0:2 * D].partition_broadcast(P).rearrange("p a n -> p (a n)"))):
            act.dma_start(dst, src).then_inc(small.sem, 16)
        act.wait_ge(k.flag("cols_landed").sem, 16)
        nc.scalar.activation(cact, k.col["c"], ACT.Silu).then_inc(k.flag("c_ready").sem, 1)

    small.base += 48
    modulation(block, k, row("ada").rearrange("a c p n -> (a c) p n"), cact, rowb, ring,
               [k.xn[:, :, :].rearrange("p t n -> p (t n)"), yT.rearrange("p b t -> p (b t)")[:, 0:SLOT]])
    stream(block, k, A["stream1"][bass.ds(l, 1)].rearrange("a c p n -> (a c) p n"), 72)

    @block.scalar
    def _(act):
        split_high(act, k, 0, 0)
    phase_end(block, k)

    @block.vector
    def _(dve):
        for sc, n in ((1, 0), (4, 1)):
            ins = nc.vector.scalar_tensor_tensor(mod[:, sc, :], mod[:, sc, :], 1.0, spread[:, n * D:(n + 1) * D], ALU.add,
                                                 ALU.mult)
            k.dve_steps.did(ins)
        k.dve_steps.settle(dve)
        split_low(dve, k, 0, 0)
    rms_norm(block, k, mod[:, 1, :], mod[:, 0, :])
    turn(block, k, k.xn, KD)
    phase_end(block, k)
    a.at = body
    att = a.take(NT, 3 * WIDTH)
    product(block, k, "token", 512, 3, stationary=tok,
            act=lambda i, j, ps: nc.scalar.copy(att[:, 0, i * 512:(i + 1) * 512], ps[:, 0, :]),
            dve=lambda i, j, ps: nc.vector.tensor_copy(att[:, 1, i * 512:(i + 1) * 512], ps[:, 1, :]))
    phase_end(block, k)
    attention(block, k, att, yT)
    k.yT = yT
    a.at = body
    AR = mod[:, 0:2, :].rearrange("p m n -> p (m n)").rearrange("p (b x t) -> p b x t", b=NB, x=2)
    BT, KT = a.take(NB, TOK), a.take(NB, TOK)
    g, bonus = (yT[:, n * NB:(n + 1) * NB, :].rearrange("p b t -> p (b t)") for n in (2, 1))
    k.tok_at = a.at
    Btok, Ktok, Vtok = (a.take(NT, WIDTH) for _ in range(3))
    y = a.take(D)
    S, W, U, ends = a.take(2, NB, 64), a.take(WIDTH), a.take(WIDTH), a.take(NB, NCH)
    k.gram_at = a.at
    zT = a.take(NZ, TOK)
    lora = a.take(2 * WIDTH)
    scratch = [a.take(D), a.take(D), a.take(D), a.take(2 * TOK)]
    assert k.gram_at + 7 * D <= a.size

    @block.scalar
    def _(act):
        act.dma_start(lora, row("wide1")[:, :, 0:2 * WIDTH].rearrange("a p n -> (a p) n")).then_inc(small.sem, 16)
    small.base += 16
    zcopy = lambda f: lambda i, j, ps: f(zT[:, 2 * i:2 * i + 2, :].rearrange("p b t -> p (b t)"), ps[:, 0, :])
    product(block, k, "channel", 256, NZ // 2, moving=k.h_parts, unroll=8, act=zcopy(nc.scalar.copy))

    @block.tensor
    def _(pe):
        pe.wait_ge(small.sem, small.base)
    phase_end(block, k)
    rwkv(block, k, zT, lora, scratch, (AR, BT, KT, g, bonus, Btok, Ktok, Vtok, y, S, W, U, ends), yT[:, NB:2 * NB, :])
    a.at = body
    uv = a.take(NT, 2 * WIDTH)
    w_s, k.ln = a.take(HEADS * P), a.take(2 * WIDTH)

    @block.scalar
    def _(act):
        act.dma_start(k.ln, row("spread1")[:, 2 * D:2 * D + 2 * WIDTH].partition_broadcast(P).rearrange("p a n -> p (a n)")
                      ).then_inc(small.sem, 16)
        act.dma_start(w_s, row("wide1")[:, :, 2 * WIDTH:].rearrange("a p n -> (a p) n")).then_inc(small.sem, 16)
        act.wait_ge(small.sem, small.base + 32)
    small.base += 32

    both = token_out_dyn
    product(block, k, "token", 512, 2, stationary=tok,
            act=both(lambda o, i: nc.scalar.activation(o, i, ACT.Gelu_apprx_tanh), uv))
    phase_end(block, k)
    gmlp(block, k, uv, w_s, yT[:, 2 * NB:, :])
    a.at = body
    gates = a.take(NT, 3 * D)
    product(block, k, "token", 512, 6, stationary=tok, act=both(lambda o, i: nc.scalar.activation(o, i, ACT.Sigmoid), gates))
    phase_end(block, k)
    y4 = lambda n: yT[:, n * NB:(n + 1) * NB, :]
    done = k.chunk
    operand(block, k, y4(0), 0, done)
    operand(block, k, y4(1), 1, done)
    for n in range(3):
        product(block, k, "token", 512, 2, ktiles=4, stationary=lambda kt, t, i, n=n: parts(4 * (n % 2) + kt, t),
                dve=both(lambda o, i: nc.vector.tensor_tensor(o, o, i, ALU.mult), gates[:, :, n * D:(n + 1) * D]))
        if n == 0:
            operand(block, k, y4(2), 0, k.chunk)
    phase_end(block, k)

    def merge(op, steps, eng, t):
        for n in (1, 2):
            steps.did(op(gates[:, t, 0:D], gates[:, t, 0:D], gates[:, t, n * D:(n + 1) * D], ALU.add))
            steps.settle(eng)

    @block.vector
    def _(dve):
        merge(nc.vector.tensor_tensor, k.dve_steps, dve, 0)

    @block.gpsimd
    def _(pool):
        merge(nc.gpsimd.tensor_tensor, k.pool_steps, pool, 1)
    phase_end(block, k)
    turn(block, k, gates, KD)
    phase_end(block, k)
    product(block, k, "token", 512, 2, stationary=tok, dve=lambda i, j, ps: gated_add(k, i, ps, mod[:, 2, :]))
    phase_end(block, k)
    rms_norm(block, k, mod[:, 4, :], mod[:, 3, :])
    turn(block, k, k.xn, KD)
    phase_end(block, k)
    a.at = body
    k.ffn_act, k.ffn_conv = a.take(2, 512), a.take(2, 512)
    ffn(block, k, lambda dve, half, ps: gated_add(k, half, ps, mod[:, 5, :]),
        conv=(k.col["conv_w"].rearrange("p (j b) -> p j b", j=3), k.col["conv_b"]))
    phase_end(block, k)


def gated_add(k, i, ps, gate):
    cols = slice(i * 512, (i + 1) * 512)
    for t in range(NT):
        k.dve_steps.did(k.nc.vector.tensor_tensor(k.xn[:, t, cols], ps[:, t, :], gate[:, cols], ALU.mult))
    k.dve_steps.settle(k.nc.vector)
    for t in range(NT):
        ins = k.nc.vector.tensor_tensor(k.x[:, t, cols], k.x[:, t, cols], k.xn[:, t, cols], ALU.add)
    return ins


def mod_flat(k):
    return k.arena.tile[:, 0:6 * D]


def second_stream(v, l):
    token, channel, ffn = chunk_arrays()
    w = v["w_in_2"][l]
    out = ffn(v["ffn1_w_gate_2"][l], v["ffn1_w_up_2"][l], v["ffn1_w_down_2"][l])
    out += channel(w[:, :S_GA]) + token(v["cmp_k_w1_2"][l], 8) + token(v["cmp_v_w1_2"][l], 8)
    out += channel(w[:, S_QB:S_VB]) + token(w[:, S_VB:S_AL]) + token(w[:, S_RB:])
    out += token(v["w_branch_nsa_2"][l]) + token(v["w_branch_gla_2"][l]) + token(v["w_out_2"][l])
    out += ffn(v["ffn2_w_gate_2"][l], v["ffn2_w_up_2"][l], v["ffn2_w_down_2"][l])
    return np.stack(out)


SECOND_COLS = {"pos_k": 16, "pos_v": 16, "w_small": KD * 40, "w2_k": 2 * DH, "w2_v": 2 * DH}


def second_small(v, l):
    pos = lambda p: p.reshape(16, 2, DH).transpose(1, 2, 0).reshape(P, 16)
    tiles = lambda m: m.reshape(-1, P, m.shape[1]).transpose(1, 0, 2).reshape(P, -1)
    w = v["w_in_2"][l]
    cols = [pos(v["cmp_pos_k_2"][l]), pos(v["cmp_pos_v_2"][l]),
            tiles(np.concatenate([w[:, S_GA:S_QB], w[:, S_AL:S_RB]], 1)), tiles(v["cmp_k_w2_2"][l]),
            tiles(v["cmp_v_w2_2"][l])]
    rows = [v["gla_a_b_2"][l]]
    spread = [v["ffn1_norm_2"][l], v["mix_norm_2"][l], v["ffn2_norm_2"][l], v["gla_out_norm_2"][l]]
    return [np.concatenate(cols, 1), v["gla_a_w2_2"][l], np.concatenate(rows), np.concatenate(spread)]


def distance_bias(block, k, A, nc):
    a = k.arena
    a.at = 0
    k.bias = a.take(HEADS, NT, TOK)
    table, onehot, cols, line = a.take(HEADS), a.take(TOK), a.take(HEADS, P), a.take(HEADS, 512)
    loaded, v = k.flag("small_landed"), nc.vector
    pitch = HEADS * 512

    @block.sync
    def _(sp):
        sp.dma_start(table[0:32, :], A["rel_table"]).then_inc(loaded.sem, 16)
        sp.dma_start(onehot[0:32, :], A["c_onehot"]).then_inc(loaded.sem, 16)

    @block.vector
    def _(dve):
        dve.wait_ge(loaded.sem, loaded.at(32))
        for h in range(HEADS):
            v.tensor_scalar(cols[0:32, h, :], k.c("ones")[0:32, :], table[0:32, h:h + 1], None, ALU.mult)
        v.memset(line[:, :, TOK:512], NEG)
    phase_end(block, k)

    @block.tensor
    def _(pe):
        for h in range(HEADS):
            nc_matmul(k, k.bank[h][:, 0:TOK], cols[0:32, h, :], onehot[0:32, :], True, True)
    phase_end(block, k)

    @block.vector
    def _(dve):
        for h in range(HEADS):
            v.tensor_copy(line[:, h, 0:TOK], k.bank[h][:, 0:TOK])
    phase_end(block, k)

    @block.sync
    def _(sp):
        flat = k.lines.rearrange("(p n) -> p n", n=pitch)
        sp.wait_ge(k.flag("phase_arrived").sem, 4 * k.phase)
        sp.dma_start(flat[0:P, :].rearrange("p (h n) -> p h n", h=HEADS), line).then_inc(loaded.sem, 16)
        sp.wait_ge(loaded.sem, loaded.at(48))
        for t in range(NT):
            c = TOK - 1 - t * P
            skewed = k.lines[c:c + P * (pitch - 1)].rearrange("(p n) -> p n", n=pitch - 1)
            for h in range(HEADS):
                sp.dma_start(k.bias[:, h, t, :], skewed[:, h * 512:h * 512 + TOK]).then_inc(loaded.sem, 16)
        sp.wait_ge(loaded.sem, loaded.at(48 + 16 * NT * HEADS))
    loaded.base += 48 + 16 * NT * HEADS


def keys_values(block, k, keys, values):
    first, group0 = k.chunk, k.group
    nc = k.nc
    used, act_evac, dve_evac = k.flag("slot_used"), k.flag("act_evac"), k.flag("dve_evac")
    ps = k.pair[group0 % 2]

    @block.tensor
    def _(pe):
        for s in (act_evac, dve_evac):
            if s.base > 0:
                pe.wait_ge(s.sem, s.base)
        wh, wl = slot_wait(pe, k, first, first, 8)
        for kt in range(8):
            split_product(k, ps[:, 0, 0:TOK], (wh[:, kt, 0:P], wl[:, kt, 0:P]), k.h_parts(kt), kt == 0, kt == 7)
        for t in range(NT):
            for kt in range(8):
                x = tuple(h[:, t * P:(t + 1) * P] for h in k.h_parts(kt))
                ins = split_product(k, ps[:, 1, t * P:(t + 1) * P], x, (wh[:, kt, P:2 * P], wl[:, kt, P:2 * P]),
                                    kt == 0, kt == 7)
        ins.then_inc(used.sem, 1)

    @block.scalar
    def _(act):
        split_high(act, k, first + 1, first + 1)
        act.wait_ge(used.sem, first + 1)
        for g in range(2):
            for half in range(2):
                ins = nc.scalar.copy(keys[half * 64:half * 64 + 64, g, :], ps[g * 64:g * 64 + 64, 0, 0:TOK])
        ins.then_inc(act_evac.sem, 1)

    @block.vector
    def _(dve):
        split_low(dve, k, first + 1, first + 1)
        dve.wait_ge(used.sem, first + 1)
        nc.vector.tensor_copy(values, ps[:, 1, 0:TOK].rearrange("p (t n) -> p t n", t=NT)).then_inc(dve_evac.sem, 1)
    act_evac.base += 1
    dve_evac.base += 1
    k.chunk += 1
    k.group += 1


def compress(block, k, pairs, keysT, values):
    nc, v = k.nc, k.nc.vector
    a = k.arena
    mark = a.at
    blocks = a.take(2, 16, 2, NC)
    hid = a.take(2, 2, 2 * NC)
    first = k.chunk
    used = k.flag("slot_used")

    @block.vector
    def _(dve):
        for n, name in enumerate(("pos_k", "pos_v")):
            for g in range(2):
                tokens = pairs[:, n, g, :].rearrange("p (c q) -> p q c", q=8)
                for late in range(2):
                    v.tensor_tensor(blocks[:, n, 8 * late:8 * late + 8, g, :], tokens[:, :, late:late + NC],
                                    k.col2[name][:, 8 * late:8 * late + 8].unsqueeze(2).to_broadcast([P, 8, NC]), ALU.add)
    phase_end(block, k)
    size = 2 * 16 * 2 * NC
    whole = blocks.rearrange("p n q g c -> p (n q g c)")
    parts = [x[:, :, :].rearrange("p a n -> p (a n)")[:, 0:size] for x in (k.hid_high, k.hid_low)]
    bh, bl = (x.rearrange("p (n q c) -> p n q c", n=2, q=16) for x in parts)

    @block.scalar
    def _(act):
        nc.scalar.copy(parts[0], whole)
    phase_end(block, k)

    @block.vector
    def _(dve):
        v.tensor_tensor(parts[1], whole, parts[0].bitcast(F32), ALU.subtract)
    phase_end(block, k)

    @block.tensor
    def _(pe):
        for n in range(2):
            for h in range(2):
                c = first + 2 * n + h
                wh, wl = slot_wait(pe, k, c, c, 8)
                for hb in range(2):
                    for kt in range(8):
                        cols, q = slice(hb * P, (hb + 1) * P), 8 * h + kt
                        ins = split_product(k, k.bank[4 + 2 * n + hb][:, 0:2 * NC], (wh[:, kt, cols], wl[:, kt, cols]),
                                            (bh[:, n, q, :], bl[:, n, q, :]), q == 0, q == 15)
                ins.then_inc(used.sem, 1)

    @block.scalar
    def _(act):
        for c in range(first + 1, first + 5):
            split_high(act, k, c, c)

    @block.vector
    def _(dve):
        for c in range(first + 1, first + 5):
            split_low(dve, k, c, c)
    k.chunk += 4
    phase_end(block, k)

    @block.scalar
    def _(act):
        for n in range(2):
            for hb in range(2):
                nc.scalar.activation(hid[:, n, hb, :], k.bank[4 + 2 * n + hb][:, 0:2 * NC], ACT.Silu)
    phase_end(block, k)

    @block.tensor
    def _(pe):
        for hb in range(2):
            nc_matmul(k, k.bank[4][0:64, 0:2 * NC], k.col2["w2_k"][:, hb * DH:(hb + 1) * DH], hid[:, 0, hb, :], hb == 0, hb == 1)
        for g in range(2):
            for hb in range(2):
                nc_matmul(k, k.bank[5][0:NC, g * DH:(g + 1) * DH], hid[:, 1, hb, g * NC:(g + 1) * NC],
                          k.col2["w2_v"][:, hb * DH:(hb + 1) * DH], hb == 0, hb == 1)
    phase_end(block, k)

    @block.vector
    def _(dve):
        for half in range(2):
            v.tensor_copy(keysT[half * 64:half * 64 + 64, 0:2 * NC], k.bank[4][0:64, 0:2 * NC])
        v.tensor_copy(values[0:NC, :], k.bank[5][0:NC, 0:2 * DH])
    phase_end(block, k)
    a.at = mark


def nsa(block, k, qT, keysT, valuesT, kc, vc, gates, oT):
    nc, v = k.nc, k.nc.vector
    a = k.arena
    mark = a.at
    S = a.take(HEADS, NT, 2 * TOK)
    C = a.take(HEADS, NT, 16)
    PT = a.take(2, 2, 384)
    CT = a.take(2, TOK)
    stat = lambda tile: tile[:, 0:48].rearrange("p (t h b) -> p t h b", t=NT, h=HEADS)
    mx, tot, rec = stat(k.mx), stat(k.tot), stat(k.rec)
    units = [(h, t) for h in range(HEADS) for t in range(NT)]
    scored, took, maxed = k.flag("scored"), k.flag("score_read"), k.flag("maxed")
    SS = lambda h, t: S[:, h, t, :].rearrange("p (b s) -> p b s", b=2)[:, :, 0:(t + 1) * P]

    @block.tensor
    def _(pe):
        for u, (h, t) in enumerate(units):
            if u >= 2:
                pe.wait_ge(took.sem, took.at(2 * (u - 1)))
            p0, n, g = 64 * (h % 2), (t + 1) * P, h // 4
            q = qT[p0:p0 + 64, h // 2, t * P:(t + 1) * P]
            for b in range(2):
                nc_matmul(k, k.bank[4 + u % 2][:, b * TOK:b * TOK + n], q, keysT[b][p0:p0 + 64, g, 0:n], True, True)
            nc_matmul(k, k.bank[6 + u % 2][:, 0:NC], q, kc[p0:p0 + 64, g * NC:(g + 1) * NC], True,
                      True).then_inc(scored.sem, 1)

    @block.vector
    def _(dve):
        for u in range(len(units) + 1):
            if u < len(units):
                h, t = units[u]
                n = (t + 1) * P
                dve.wait_ge(scored.sem, scored.at(u + 1))
                v.tensor_tensor(SS(h, t), k.bank[4 + u % 2][:, :].rearrange("p (b s) -> p b s", b=2)[:, :, 0:n],
                                k.bias[:, h, t, 0:n].unsqueeze(1).to_broadcast([P, 2, n]), ALU.add).then_inc(took.sem, 1)
                v.tensor_tensor(C[:, h, t, 0:NC], k.bank[6 + u % 2][:, 0:NC], k.bias[:, h, t, 31:TOK:16],
                                ALU.add).then_inc(took.sem, 1)
            if u >= 1:
                h, t = units[u - 1]
                dve.wait_ge(took.sem, took.at(2 * u))
                v.tensor_reduce(mx[:, t, h, 1:3], SS(h, t), AX.X, ALU.max, negate=True)
                v.tensor_reduce(mx[:, t, h, 0:1], C[:, h, t, 0:NC], AX.X, ALU.max, negate=True).then_inc(maxed.sem, 1)

    @block.scalar
    def _(act):
        for u, (h, t) in enumerate(units):
            act.wait_ge(maxed.sem, maxed.at(u + 1))
            for b in range(3):
                x = C[:, h, t, 0:NC] if b == 0 else SS(h, t)[:, b - 1, :]
                nc.scalar.activation(x, x, ACT.Exp, bias=mx[:, t, h, b:b + 1], accum_out=tot[:, t, h, b:b + 1])
    scored.base += 16
    took.base += 32
    maxed.base += 16
    phase_end(block, k)

    @block.vector
    def _(dve):
        k.dve_steps.did(v.reciprocal(k.rec[:, 0:48], k.tot[:, 0:48]))
        k.dve_steps.settle(dve)
        v.tensor_tensor(k.rec[:, 0:48], k.rec[:, 0:48], gates, ALU.mult)
    phase_end(block, k)
    scaled = [k.flag("scaled_act"), k.flag("scaled_dve")]
    pturned, pread = k.flag("probs_turned"), [k.flag("probs_read_act"), k.flag("probs_read_dve")]
    mixed, yread = k.flag("mixed"), k.flag("mixed_read")
    base = lambda h: 4 * (h % 2)

    def mix(pe, h):
        for s in pread:
            pe.wait_ge(s.sem, s.at(h + 1))
        b = h // 2
        if h % 2 == 0 and b >= 2:
            pe.wait_ge(yread.sem, yread.at(b - 1))
        o = k.bank[3 + 4 * (b % 2)][64 * (h % 2):64 * (h % 2) + 64, 0:TOK]
        g = slice((h // 4) * DH, (h // 4 + 1) * DH)
        for n in range(2):
            nc_matmul(k, o, valuesT[n][:, 0, g], PT[:, h % 2, n, 0:TOK], n == 0, False)
            nc_matmul(k, o[:, P:TOK], valuesT[n][:, 1, g], PT[:, h % 2, n, TOK:384], False, False)
        nc_matmul(k, o, vc[0:NC, g], CT[0:NC, h % 2, :], False, True).then_inc(mixed.sem, 1)

    @block.tensor
    def _(pe):
        for h in range(HEADS):
            for s in scaled:
                pe.wait_ge(s.sem, s.at(h + 1))
            if h >= 2:
                for s in pread:
                    pe.wait_ge(s.sem, s.at(h - 1))
            for n in range(2):
                for i, (t, s) in enumerate(((0, 0), (1, 0), (1, 1))):
                    nc.tensor.transpose(k.bank[base(h) + n][:, i * P:(i + 1) * P],
                                        S[:, h, t, n * TOK + s * P:n * TOK + (s + 1) * P], k.c("ident"))
            for t in range(NT):
                ins = nc.tensor.transpose(k.bank[base(h) + 2][0:NC, t * P:(t + 1) * P], C[:, h, t, 0:NC], k.c("ident"))
            ins.then_inc(pturned.sem, 1)
            if h >= 1:
                mix(pe, h - 1)
        mix(pe, HEADS - 1)

    def out(act, b):
        act.wait_ge(mixed.sem, mixed.at(2 * b + 2))
        nc.scalar.copy(oT[:, b, :], k.bank[3 + 4 * (b % 2)][:, 0:TOK]).then_inc(yread.sem, 1)

    @block.scalar
    def _(act):
        def scale(h):
            for t in range(NT):
                ins = nc.scalar.activation(SS(h, t)[:, 0, :], SS(h, t)[:, 0, :], ACT.Copy, scale=rec[:, t, h, 1:2])
            ins.then_inc(scaled[0].sem, 1)
        scale(0)
        for h in range(HEADS):
            if h + 1 < HEADS:
                scale(h + 1)
            act.wait_ge(pturned.sem, pturned.at(h + 1))
            if h >= 2:
                act.wait_ge(mixed.sem, mixed.at(h - 1))
            nc.scalar.copy(PT[:, h % 2, 0, :], k.bank[base(h)][:, 0:384]).then_inc(pread[0].sem, 1)
            if h % 2 == 1 and h >= 3:
                out(act, h // 2 - 1)
        out(act, NB - 1)

    @block.vector
    def _(dve):
        def scale(h):
            for t in range(NT):
                v.tensor_scalar(SS(h, t)[:, 1, :], SS(h, t)[:, 1, :], rec[:, t, h, 2:3], None, ALU.mult)
                ins = v.scalar_tensor_tensor(C[:, h, t, 0:NC], C[:, h, t, 0:NC], rec[:, t, h, 0:1], k.seen[:, t, :],
                                             ALU.mult, ALU.mult)
            ins.then_inc(scaled[1].sem, 1)
        scale(0)
        for h in range(HEADS):
            if h + 1 < HEADS:
                scale(h + 1)
            dve.wait_ge(pturned.sem, pturned.at(h + 1))
            if h >= 2:
                dve.wait_ge(mixed.sem, mixed.at(h - 1))
            v.tensor_copy(PT[:, h % 2, 1, :], k.bank[base(h) + 1][:, 0:384])
            v.tensor_copy(CT[0:NC, h % 2, :], k.bank[base(h) + 2][0:NC, 0:TOK]).then_inc(pread[1].sem, 1)
    for s, n in ((scaled[0], 8), (scaled[1], 8), (pturned, 8), (pread[0], 8), (pread[1], 8), (mixed, 8), (yread, 4)):
        s.base += n
    phase_end(block, k)
    a.at = mark


def gla(block, k, qT, kT, vb, rb, alT, gain, oT):
    nc, v = k.nc, k.nc.vector
    steps = k.dve_steps
    a = k.arena
    mark = a.at
    la, ex = k.xn[:, 0, :], k.xn[:, 1, :]
    o = a.take(NT, GH * GV)
    B, ki = (o[:, n, :].rearrange("p (h t) -> p h t", h=GH) for n in range(2))
    qd, ks = a.take(GH, TOK), a.take(GH, TOK)
    kst, AT = a.take(NT, WIDTH), a.take(NT * GH, P)
    S, ends = a.take(2, GH, GV), a.take(GH, NCH)
    big = k.big
    chunks = lambda x: x.rearrange("p h (c t) -> p h c t", c=NCH)

    @block.tensor
    def _(pe):
        for t in range(NT):
            d = big[0][:, t * WIDTH:(t + 1) * WIDTH]
            nc_matmul(k, d, alT[0:16, t * P:(t + 1) * P], k.a_w2[0:16, :], True, False)
            nc_matmul(k, d, k.c("ones")[0:1, :], k.w0[0:1, :], False, True)
    phase_end(block, k)

    @block.scalar
    def _(act):
        k.act_steps.did(nc.scalar.activation(ex, big[0], ACT.Abs))
        k.act_steps.settle(act)
        k.act_steps.did(nc.scalar.activation(ex, ex, ACT.Exp, scale=-1.0))
        k.act_steps.settle(act)
        nc.scalar.activation(ex, ex, ACT.Ln, bias=1.0)
    phase_end(block, k)

    @block.vector
    def _(dve):
        v.scalar_tensor_tensor(la, big[0], 0.0, ex, ALU.min, ALU.subtract)
    phase_end(block, k)

    @block.tensor
    def _(pe):
        for h in range(GH):
            for t in range(NT):
                nc_matmul(k, flat4(big[0])[:, h, t * P:(t + 1) * P], la[:, t * WIDTH + h * P:t * WIDTH + (h + 1) * P],
                          k.c("incl_up"), True, True)
    phase_end(block, k)

    @block.vector
    def _(dve):
        v.tensor_copy(B, flat4(big[0]))
    phase_end(block, k)

    @block.vector
    def _(dve):
        last = chunks(B)[:, :, :, CHUNK - 1:CHUNK]
        for h in range(GH):
            v.tensor_tensor(chunks(ks)[:, h], last[:, h].to_broadcast([P, NCH, CHUNK]), chunks(B)[:, h], ALU.subtract)

    @block.scalar
    def _(act):
        nc.scalar.activation(qd, flat4(big[0]), ACT.Exp, scale=1.0 / 16)
        nc.scalar.activation(ki, flat4(big[0]), ACT.Exp, scale=-1.0 / 16)
        nc.scalar.activation(ends, B[:, :, CHUNK - 1:TOK:CHUNK], ACT.Exp, scale=1.0 / 16)
    phase_end(block, k)

    @block.scalar
    def _(act):
        nc.scalar.activation(ks, ks, ACT.Exp, scale=1.0 / 16)

    @block.vector
    def _(dve):
        v.tensor_tensor(qd, qd, qT, ALU.mult)
        v.tensor_tensor(ki, ki, kT, ALU.mult)
    phase_end(block, k)

    @block.vector
    def _(dve):
        v.tensor_tensor(ks, ks, kT, ALU.mult)
        v.memset(S[:, 0], 0.0)

    @block.tensor
    def _(pe):
        for n in range(NT * GH):
            h, t = n % GH, slice((n // GH) * P, (n // GH + 1) * P)
            nc_matmul(k, big[1][:, n * P:(n + 1) * P], ki[:, h, t], qd[:, h, t], True, True)
    phase_end(block, k)

    @block.vector
    def _(dve):
        v.tensor_tensor(AT, big[1].rearrange("p (n t) -> p n t", t=P),
                        k.c("incl_up").unsqueeze(1).to_broadcast([P, NT * GH, P]), ALU.mult)
    turn_back(block, k, ks, kst)
    for c in range(NCH):
        t, p0 = c // 2, 64 * (c % 2)
        rows, cc = slice(p0, p0 + 64), slice(c * CHUNK, (c + 1) * CHUNK)
        now, nxt = S[:, c % 2], S[:, (c + 1) % 2]

        @block.tensor
        def _(pe):
            for h in range(GH):
                vv = vb[:, t, h * GV:(h + 1) * GV]
                d = big[0][rows, h * GV:(h + 1) * GV]
                nc_matmul(k, d, qd[:, h, cc], now[:, h, :], True, False)
                nc_matmul(k, d, AT[:, t * GH + h, p0:p0 + 64], vv, False, True)
                nc_matmul(k, big[1][:, h * GV:(h + 1) * GV], kst[rows, t, h * P:(h + 1) * P], vv[rows], True, True)
        phase_end(block, k)

        @block.vector
        def _(dve):
            for h in range(GH):
                v.scalar_tensor_tensor(nxt[:, h, :], now[:, h, :], ends[:, h, c:c + 1],
                                       big[1][:, h * GV:(h + 1) * GV], ALU.mult, ALU.add)

        @block.scalar
        def _(act):
            nc.scalar.copy(o[rows, t, :], big[0][rows, :])
        phase_end(block, k)
    ss = k.mx[:, 0:8]

    @block.scalar
    def _(act):
        for t in range(NT):
            for h in range(GH):
                nc.scalar.activation(k.xn[:, t, h * GV:(h + 1) * GV], o[:, t, h * GV:(h + 1) * GV], ACT.Square,
                                     accum_out=ss[:, t * GH + h:t * GH + h + 1])
    phase_end(block, k)

    @block.vector
    def _(dve):
        v.tensor_scalar(k.tot[:, 0:8], ss, 1.0 / GV, RMS_EPS, ALU.mult, ALU.add)
    phase_end(block, k)

    @block.scalar
    def _(act):
        nc.scalar.activation(k.rec[:, 0:8], k.tot[:, 0:8], ACT.Sqrt)
    phase_end(block, k)

    @block.vector
    def _(dve):
        steps.did(v.reciprocal(ss, k.rec[:, 0:8]))
        steps.settle(dve)
        for t in range(NT):
            for h in range(GH):
                x = o[:, t, h * GV:(h + 1) * GV]
                steps.did(v.scalar_tensor_tensor(x, x, ss[:, t * GH + h:t * GH + h + 1], gain[:, h * GV:(h + 1) * GV],
                                                 ALU.mult, ALU.mult))
        steps.settle(dve)
        for t in range(NT):
            v.tensor_tensor(o[:, t, :], o[:, t, :], rb[:, t, :], ALU.mult)
    phase_end(block, k)
    turn(block, k, o, NG, oT)
    phase_end(block, k)
    a.at = mark


def second_layer(block, k, A, l):
    nc = k.nc
    a = k.arena
    a.at = HEADS * NT * TOK
    small = k.flag("small_landed")
    row = lambda name: A[name][bass.ds(l, 1)]
    tok = lambda kt, t, i: parts(kt, t)
    cols = a.take(sum(SECOND_COLS.values()))
    k.col2 = columns(cols, SECOND_COLS)
    out_norm, k.a_w2 = a.take(D), a.take(WIDTH)
    body = a.at
    gain_landed = k.flag("gain_landed")
    parts = lambda kt, t: (k.h_high[:, kt, t * P:(t + 1) * P], k.h_low[:, kt, t * P:(t + 1) * P])
    stream(block, k, A["stream2"][bass.ds(l, 1)].rearrange("a c p n -> (a c) p n"), 105)

    @block.scalar
    def _(act):
        spread = row("spread2").partition_broadcast(P).rearrange("p a n -> p (a n)")
        for dst, src in ((k.spread[:], spread[:, 0:D]), (cols, row("cols2").rearrange("a p n -> (a p) n")),
                         (k.a_w2[0:16, :], row("a_w2").rearrange("a p n -> (a p) n")), (k.w0[0:1, :], row("rows2")),
                         (out_norm, spread[:, 3 * D:4 * D])):
            act.dma_start(dst, src).then_inc(small.sem, 16)
        split_high(act, k, 0, 0)
        act.wait_ge(small.sem, 80)

    @block.vector
    def _(dve):
        split_low(dve, k, 0, 0)
    small.base += 80
    phase_end(block, k)

    def norm(n):
        @block.vector
        def _(dve):
            if n:
                dve.wait_ge(gain_landed.sem, 16 * n)
        rms_norm(block, k, k.spread[:])
        if n < 2:
            @block.scalar
            def _(act):
                act.dma_start(k.spread[:], row("spread2")[:, (n + 1) * D:(n + 2) * D].partition_broadcast(P).rearrange(
                    "p a n -> p (a n)")).then_inc(gain_landed.sem, 16)

    def feed_forward(n):
        a.at = body
        norm(n)
        turn(block, k, k.xn, KD)
        phase_end(block, k)
        k.ffn_act = a.take(2, 512)
        ffn(block, k, lambda dve, half, ps: scaled_add(k, half, ps, 0.5))
        phase_end(block, k)
    feed_forward(0)
    a.at = body
    oT, obT = a.take(NB, TOK), a.take(NG, TOK)
    alT = a.take(TOK)
    mixers = a.at
    norm(1)
    turn(block, k, k.xn, KD)
    phase_end(block, k)
    qT, pairs, keys, values = a.take(NB, TOK), a.take(2, 2, P), a.take(2, 2, TOK), a.take(2, NT, P)
    gates, kc, vc = a.take(NT * 24), a.take(32), a.take(2 * DH)
    flat = lambda x: x.rearrange("p b t -> p (b t)")
    product(block, k, "channel", 256, 2, moving=k.h_parts, unroll=4,
            act=lambda i, j, ps: nc.scalar.activation(flat(qT[:, 2 * i:2 * i + 2, :]), ps[:, 0, :], ACT.Copy,
                                                      scale=DH ** -0.5))

    def split_pairs(i, j, ps):
        for n in range(2):
            for g in range(2):
                for par in range(2):
                    ins = nc.scalar.copy(pairs[par * 64:par * 64 + 64, n, g, :],
                                         ps[g * 64:g * 64 + 64, 0, n * TOK + par:(n + 1) * TOK:2])
        return ins
    product(block, k, "channel", 256, 1, moving=k.h_parts, act=split_pairs)
    for n in range(2):
        keys_values(block, k, keys[:, n], values[:, n])
    wsm = k.col2["w_small"].rearrange("p (k n) -> p k n", k=KD)

    @block.tensor
    def _(pe):
        for t in range(NT):
            for kt in range(KD):
                for n, x in enumerate(parts(kt, t)):
                    nc_matmul(k, k.bank[4][:, t * 24:(t + 1) * 24], x.bitcast(F32), wsm[:, kt, 0:24], kt + n == 0,
                              kt == KD - 1 and n == 1)
        for kt in range(KD):
            for n, x in enumerate(k.h_parts(kt)):
                nc_matmul(k, k.bank[5][0:16, 0:TOK], wsm[:, kt, 24:40], x.bitcast(F32), kt + n == 0,
                          kt == KD - 1 and n == 1)
    phase_end(block, k)

    @block.scalar
    def _(act):
        nc.scalar.activation(gates, k.bank[4][:, 0:48], ACT.Sigmoid)
        nc.scalar.copy(alT[0:16, :], k.bank[5][0:16, 0:TOK])
    compress(block, k, pairs, kc, vc)
    nsa(block, k, qT, [keys[:, 0], keys[:, 1]], [values[:, 0], values[:, 1]], kc, vc, gates, oT)
    a.at = mixers
    qb, kb, vb, rb = a.take(GH, TOK), a.take(GH, TOK), a.take(NT, GH * GV), a.take(NT, GH * GV)
    for dst, scale in ((qb, P ** -0.5), (kb, 1.0)):
        product(block, k, "channel", 256, 2, moving=k.h_parts, unroll=4,
                act=lambda i, j, ps, dst=dst, scale=scale: nc.scalar.activation(
                    flat(dst[:, 2 * i:2 * i + 2, :]), ps[:, 0, :], ACT.Copy, scale=scale))
    token_out = lambda op, dst: (lambda i, j, ps: [op(dst[:, t, i * 512:(i + 1) * 512], ps[:, t, :]) for t in range(NT)][-1])
    product(block, k, "token", 512, 2, stationary=tok, dve=token_out(nc.vector.tensor_copy, vb))
    product(block, k, "token", 512, 2, stationary=tok,
            act=token_out(lambda o, i: nc.scalar.activation(o, i, ACT.Silu), rb))
    phase_end(block, k)
    gla(block, k, qb, kb, vb, rb, alT, out_norm, obT)
    a.at = mixers
    gm = a.take(NT, 2 * D)
    product(block, k, "token", 512, 4, stationary=tok,
            act=token_out_dyn(lambda o, i: nc.scalar.activation(o, i, ACT.Sigmoid), gm))
    phase_end(block, k)
    mul = lambda o, i: nc.vector.tensor_tensor(o, o, i, ALU.mult)
    operand(block, k, oT, 0, k.chunk)
    operand(block, k, obT[:, 0:4, :], 1, k.chunk)
    product(block, k, "token", 512, 2, ktiles=4, stationary=tok, dve=token_out(mul, gm[:, :, 0:D]))
    operand(block, k, obT[:, 4:8, :], 0, k.chunk)
    product(block, k, "token", 512, 2, stationary=lambda kt, t, i: parts((kt + 4) % 8, t),
            dve=token_out(mul, gm[:, :, D:2 * D]))
    phase_end(block, k)

    @block.vector
    def _(dve):
        nc.vector.tensor_tensor(gm[:, 0, 0:D], gm[:, 0, 0:D], gm[:, 0, D:2 * D], ALU.add)

    @block.gpsimd
    def _(pool):
        nc.gpsimd.tensor_tensor(gm[:, 1, 0:D], gm[:, 1, 0:D], gm[:, 1, D:2 * D], ALU.add)
    phase_end(block, k)
    turn(block, k, gm, KD)
    phase_end(block, k)
    product(block, k, "token", 512, 2, stationary=tok, dve=lambda i, j, ps: scaled_add(k, i, ps, 1.0))
    phase_end(block, k)
    feed_forward(2)
    assert k.chunk == 105, k.chunk


def token_out_dyn(op, dst):
    def out(i, j, ps):
        for t in range(NT):
            ins = op(dst[:, t, bass.ds(i * 512, 512)], ps[:, t, :])
        return ins
    return out


def scaled_add(k, i, ps, factor):
    cols = slice(i * 512, (i + 1) * 512)
    for t in range(NT):
        ins = k.nc.vector.scalar_tensor_tensor(k.x[:, t, cols], ps[:, t, :], factor, k.x[:, t, cols], ALU.mult, ALU.add)
    return ins


def build(nc, A, O, dump=None):
    with ExitStack() as ctx:
        k = Program(nc, ctx)
        square = k.sb("c_square", [P, len(CONSTS) * P])
        rows = k.sb("c_rows", [P, NT, 512 + 64 + NC])
        k.c = lambda name: square[:, CONSTS.index(name) * P:(CONSTS.index(name) + 1) * P]
        k.count, k.blocked = rows[:, :, 0:256], rows[:, :, 256:512]
        k.cos, k.sin, k.seen = rows[:, :, 512:544], rows[:, :, 544:576], rows[:, :, 576:576 + NC]
        k.x = k.sb("x", [P, NT, D])
        k.h_high, k.h_low = k.sb("h_high", [P, KD, TOK], F32R), k.sb("h_low", [P, KD, TOK], F32R)
        k.hid_high, k.hid_low = k.sb("hid_high", [P, 2, 512], F32R), k.sb("hid_low", [P, 2, 512], F32R)
        k.high = [k.sb(f"high{i}", [P, SLOT], F32R) for i in range(SLOTS)]
        k.low = [k.sb(f"low{i}", [P, SLOT], F32R) for i in range(SLOTS)]
        k.h_parts = lambda kt: (k.h_high[:, kt, :], k.h_low[:, kt, :])
        k.slots = [k.sb(f"slot{i}", [P, SLOT]) for i in range(SLOTS)]
        k.stat, k.mx, k.tot, k.rec = k.sb("stat", [P, 8]), k.sb("mx", [P, 64]), k.sb("tot", [P, 64]), k.sb("rec", [P, 64])
        k.cols1 = k.sb("cols1", [P, sum(FIRST_COLS.values())])
        k.col = columns(k.cols1, FIRST_COLS)
        k.w0, k.spread = k.sb("w0", [1, WIDTH]), k.sb("spread", [P, D])
        k.arena = Arena(k.sb("arena", [P, 25200]), 25200)
        k.xn = k.sb("xn", [P, NT, D])
        banks = [ctx.enter_context(nc.psum_tensor(f"pair{i}", [P, 2, 512], F32)) for i in range(4)]
        k.pair, k.acc = banks[0:2], banks[2:4]
        k.big = [b[:].rearrange("p a n -> p (a n)") for b in banks]
        k.bank = [banks[i // 2][:, i % 2, :] for i in range(8)]
        k.lines = nc.dram_tensor("bias_lines", [(P + 1) * HEADS * 512], F32, kind="Internal").ap()
        loaded = ctx.enter_context(nc.semaphore("consts_loaded"))
        with nc.Block() as block:
            @block.sync
            def _(sp):
                sp.dma_start(square[:], A["c_square"]).then_inc(loaded, 16)
                sp.dma_start(rows[:], A["c_rows"]).then_inc(loaded, 16)
                sp.dma_start(k.x[:], A["x"].rearrange("a (t p) n -> p (a t) n", p=P)).then_inc(loaded, 16)
                sp.wait_ge(loaded, 48)
        with nc.Fori(0, DEPTH) as l:
            with nc.Block() as block:
                first_layer(block, k, A, l)
            k.end_layer()
        small = k.flag("final_norm_landed")

        def final_norm(block, name):
            @block.sync
            def _(sp):
                sp.dma_start(k.spread[:, 0:D], A[name].partition_broadcast(P).rearrange("p a n -> p (a n)")
                             ).then_inc(small.sem, 16)

            @block.vector
            def _(dve):
                dve.wait_ge(small.sem, 16)
            small.base += 16
            rms_norm(block, k, k.spread[:, 0:D])
        with nc.Block() as block:
            final_norm(block, "norm_final")

            @block.vector
            def _(dve):
                nc.vector.tensor_copy(k.x[:], k.xn[:])
            phase_end(block, k)
            distance_bias(block, k, A, nc)
        k.end_layer()
        with nc.Fori(0, DEPTH) as l:
            with nc.Block() as block:
                second_layer(block, k, A, l)
            k.end_layer()
        stored = ctx.enter_context(nc.semaphore("stored"))
        with nc.Block() as block:
            final_norm(block, "final_norm_2")

            @block.sync
            def _(sp):
                sp.wait_ge(k.flag("phase_arrived").sem, 4 * k.phase)
                sp.dma_start(O["out"].rearrange("a (t p) n -> p (a t) n", p=P), k.xn[:]).then_inc(stored, 16)
                sp.wait_ge(stored, 16)


def host_arrays(v):
    f = lambda a: np.ascontiguousarray(a)
    out = dict(shape_constants())
    out["x"] = v["x"]
    out["ada"] = f(v["w_ada"].reshape(DEPTH, KD, P, 3, SLOT).transpose(0, 3, 1, 2, 4)).reshape(DEPTH, 3 * KD, P, SLOT)
    out["stream1"] = f(np.stack([first_stream(v, l) for l in range(DEPTH)]))
    for name, parts in zip(("cols1", "wide1", "rows1", "spread1"), zip(*[first_small(v, l) for l in range(DEPTH)])):
        out[name] = f(np.stack(parts))
    out["stream2"] = f(np.stack([second_stream(v, l) for l in range(DEPTH)]))
    for name, parts in zip(("cols2", "a_w2", "rows2", "spread2"), zip(*[second_small(v, l) for l in range(DEPTH)])):
        out[name] = f(np.stack(parts))
    out["rel_table"] = v["rel_table_2"]
    out["norm_final"] = v["norm_final"][None]
    out["final_norm_2"] = v["final_norm_2"][None]
    return out


def program(nc, A, out):
    build(nc, A, {"out": out})


def kernel(**inputs):
    import concourse.bacc as _bacc
    from concourse.bass_utils import run_bass_kernel_spmd as _run

    nc = _bacc.Bacc("TRN2", target_bir_lowering=False, num_devices=1)
    arrays = {f"in_{n}": a for n, a in host_arrays({n: np.asarray(a) for n, a in inputs.items()}).items()}
    A = {n[3:]: nc.dram_tensor(n, a.shape, mybir.dt.from_np(a.dtype), kind="ExternalInput").ap() for n, a in arrays.items()}
    out = nc.dram_tensor("out", [1, TOK, D], F32, kind="ExternalOutput").ap()
    program(nc, A, out)
    return _run(nc, [arrays], core_ids=[0]).results[0]["out"]
```

```python
from contextlib import ExitStack, contextmanager

import numpy as np

import concourse.bass as bass
from concourse import mybir

ALU = mybir.AluOpType
ACT = mybir.ActivationFunctionType
AX = mybir.AxisListType
F32 = mybir.dt.float32
F32R = mybir.dt.float32r

P = 128
TOK = 256
NT = TOK // P
D = 1024
KD = D // P
DEPTH = 2
HEADS = 8
DH = 64
WIDTH = HEADS * DH
NB = WIDTH // P
D_FF = 2816
NF = D_FF // P
RWKV_COLS = 3 * WIDTH + 64 + 64 + 128
NZ = RWKV_COLS // P
CHUNK = 64
NCH = TOK // CHUNK
ATT0, RWKV0 = 0, 3 * WIDTH
UV0 = RWKV0 + RWKV_COLS
GATE0 = UV0 + 2 * WIDTH
DECAY = float(np.exp(-0.5))
RMS_EPS, LN_EPS, GN_EPS = 1e-6, 1e-5, 64e-5
NEG = -1e30
SLOTS = 2
ADA_SLOTS = 3
SLOT = 2048
NC = 15
GATE_AT, SMALL = 32, 56
S_KV, S_GA, S_QB = 512, 1280, 1304
S_KB, S_VB, S_AL, S_RB, S_GM = 1816, 2328, 3352, 3368, 4392
GH, GV = 4, 256
NG = GH * GV // P


CONSTS = ["ident", "blockones", "ones", "strict_up", "incl_up", "strict_lo"] + [f"level{i}" for i in range(6)] + ["lower0", "upper"]


def shape_constants():
    i = np.arange(P)
    r, c = i[:, None], i[None, :]
    same = (r // CHUNK) == (c // CHUNK)
    m = {"ident": r == c, "blockones": (r // DH) == (c // DH), "ones": np.ones((P, P), bool),
         "strict_up": same & (r < c), "incl_up": same & (r <= c), "strict_lo": same & (r > c)}
    for k in range(6):
        b = 2 << k
        m[f"level{k}"] = ((r // b) == (c // b)) & (r % b < b // 2) & (c % b >= b // 2)
    m["lower0"] = m["level0"].T
    m["upper"] = r <= c
    square = np.concatenate([m[n] for n in CONSTS], axis=1).astype(np.float32)
    t, s = np.arange(TOK)[:, None], np.arange(TOK)[None, :]
    count = ((t >= s) & (t - s <= 128)).astype(np.float32)
    for d in (4, 16):
        count += (t >= s) & ((t - s) % d == 0)
    blocked = np.where(count > 0, 0, NEG).astype(np.float32)
    ends = 16 * np.arange(NC)[None, :] + 31
    seen = (ends <= t).astype(np.float32)
    inv = 1.0 / (np.float32(10000.0) ** (np.arange(0, DH, 2, dtype=np.float32) / np.float32(DH)))
    ang = np.arange(TOK, dtype=np.float32)[:, None] * inv[None, :].astype(np.float32)
    rows = np.concatenate([count, blocked, np.cos(ang), np.sin(ang), seen], axis=1).astype(np.float32)
    tiles = rows.reshape(NT, P, -1).transpose(1, 0, 2)
    dist = np.arange(TOK)
    logb = 16 + (np.log(np.maximum(dist, 1).astype(np.float32) / np.float32(16)) / np.float32(np.log(64.0))
                 * np.float32(16)).astype(np.int32)
    bucket = np.where(dist < 16, dist, np.minimum(logb, 31))
    onehot = (np.arange(32)[:, None] == bucket[None, ::-1]).astype(np.float32)
    return {"c_square": square, "c_rows": np.ascontiguousarray(tiles), "c_onehot": onehot}


class Signal:

    def __init__(self, sem):
        self.sem, self.base = sem, 0

    def at(self, n):
        return self.base + n


class Steps(Signal):

    def __init__(self, sem):
        super().__init__(sem)
        self.moving = 0

    def did(self, ins):
        ins.then_inc(self.sem, 1)
        self.base += 1
        return ins

    def settle(self, eng):
        eng.wait_ge(self.sem, self.moving + self.base)


@contextmanager
def counted(steps, it, per):
    if steps is None:
        yield
        return
    start = steps.base
    steps.moving = it * per
    yield
    assert steps.base - start == per, (steps.base - start, per)
    steps.moving = 0


def repeat(eng, n, unroll, step, peel=0, steps=None, per=0):
    for i in range(min(peel, n)):
        step(i, i)
    turns = (n - peel) // unroll
    done = peel
    if turns >= 2:
        with eng.Fori(0, turns) as it:
            with counted(steps, it, per * unroll):
                for j in range(unroll):
                    step(it * unroll + (peel + j), peel + j)
        if steps is not None:
            steps.base += per * unroll * (turns - 1)
        done = peel + turns * unroll
    for i in range(done, n):
        step(i, i)


class Program:

    def __init__(self, nc, ctx):
        self.nc, self.ctx, self.flags = nc, ctx, {}
        self.chunk = self.group = self.phase = self.chunks = 0
        self.pe_steps = Steps(self.sem("pe_steps"))
        self.act_steps = Steps(self.sem("act_steps"))
        self.dve_steps = Steps(self.sem("dve_steps"))
        self.pool_steps = Steps(self.sem("pool_steps"))
        self.slot_landed = [Signal(self.sem(f"slot_landed{i}")) for i in range(SLOTS)]

    def sem(self, name):
        return self.ctx.enter_context(self.nc.semaphore(name))

    def sb(self, name, shape, dtype=F32):
        return self.ctx.enter_context(self.nc.sbuf_tensor(name, shape, dtype))

    def flag(self, name):
        if name not in self.flags:
            self.flags[name] = Signal(self.sem(name))
        return self.flags[name]

    def all_flags(self):
        return [self.pe_steps, self.act_steps, self.dve_steps, self.pool_steps] + self.slot_landed + list(self.flags.values())

    def end_layer(self):
        nc = self.nc
        engines = [nc.sync, nc.tensor, nc.scalar, nc.vector, nc.gpsimd]
        for n, s in enumerate(self.all_flags()):
            engines[n % 5].sem_clear(s.sem)
            s.base = 0
        self.chunk = self.group = self.phase = 0
        nc.all_engine_barrier()


def phase_end(block, k):
    k.phase += 1
    arrived = k.flag("phase_arrived")

    def meet(eng):
        eng.drain().then_inc(arrived.sem, 1)
        eng.wait_ge(arrived.sem, 4 * k.phase)

    @block.tensor
    def _(pe):
        meet(pe)

    @block.scalar
    def _(act):
        meet(act)

    @block.vector
    def _(dve):
        meet(dve)

    @block.gpsimd
    def _(pool):
        meet(pool)


def stream(block, k, weights, n):
    k.chunks = n

    @block.sync
    def _(sp):
        split = k.flag("split_low")

        def one(i, j):
            if not isinstance(i, int) or i >= SLOTS:
                sp.wait_ge(split.sem, i + (1 - SLOTS))
            source = weights[bass.ds(i, 1)].rearrange("a p n -> (a p) n")
            sp.dma_start(k.slots[j % SLOTS][:], source).then_inc(k.slot_landed[j % SLOTS].sem, 16)
        repeat(sp, n, SLOTS, one, peel=SLOTS)


def split_high(act, k, n, parity):
    if isinstance(n, int) and n >= k.chunks:
        return
    slot = parity % SLOTS
    act.wait_ge(k.slot_landed[slot].sem, n * 8 + (16 - 8 * slot))
    if not isinstance(n, int) or n >= SLOTS:
        act.wait_ge(k.flag("slot_used").sem, n + (1 - SLOTS))
    k.nc.scalar.activation(k.high[slot][:], k.slots[slot][:], ACT.Copy).then_inc(k.flag("split_high").sem, 1)


def split_low(eng, k, n, parity):
    if isinstance(n, int) and n >= k.chunks:
        return
    slot = parity % SLOTS
    eng.wait_ge(k.flag("split_high").sem, n + 1)
    eng.tensor_tensor(k.low[slot][:], k.slots[slot][:], k.high[slot][:].bitcast(F32),
                      ALU.subtract).then_inc(k.flag("split_low").sem, 1)


def take_over_low(eng, k):
    n = k.chunk
    slot = n % SLOTS
    eng.wait_ge(k.flag("split_low").sem, n + 1)
    eng.wait_ge(k.slot_landed[slot].sem, (n + 2) * 8 + (16 - 8 * slot))


def slot_wait(pe, k, n, parity, shape):
    pe.wait_ge(k.flag("split_low").sem, n + 1)
    view = lambda s: s[:, :].rearrange("p (k n) -> p k n", k=shape)
    return view(k.high[parity % SLOTS]), view(k.low[parity % SLOTS])


def split_product(k, out, lhsT, rhs, start, stop):
    (lh, ll), (rh, rl) = lhsT, rhs
    nc_matmul(k, out, lh, rh, start, False)
    nc_matmul(k, out, lh, rl, False, False)
    return nc_matmul(k, out, ll, rh, False, stop)


def bank_wait(eng, k, i, evac):
    for name in ("act_evac", "dve_evac"):
        s = k.flag(name)
        if name in evac:
            v = s.base + i - 1
            if not isinstance(i, int) or v > 0:
                eng.wait_ge(s.sem, v)
        elif isinstance(i, int) and i == 0 and s.base > 0:
            eng.wait_ge(s.sem, s.base)


def product(block, k, kind, width, groups, ktiles=KD, moving=None, stationary=None,
            act=None, dve=None, dve_per=0, unroll=2, low="vector"):
    per = ktiles // 4 if kind == "token" else 1
    first, group0 = k.chunk, k.group
    used = k.flag("slot_used")
    evac = [n for n, f in (("act_evac", act), ("dve_evac", dve)) if f]
    nk = 4 if kind == "token" else 8
    peel = 2 if group0 == 0 else 0

    @block.tensor
    def _(pe):
        def step(i, j):
            ps = k.pair[(group0 + j) % 2]
            bank_wait(pe, k, i, evac)
            for h in range(per):
                wh, wl = slot_wait(pe, k, i * per + (first + h), first + j * per + h, nk)
                if kind == "token":
                    for kt in range(4):
                        for t in range(NT):
                            last = kt == 3 and h == per - 1
                            ins = split_product(k, ps[:, t, 0:width], stationary(4 * h + kt, t, i),
                                                (wh[:, kt, :], wl[:, kt, :]), kt == 0 and h == 0, last)
                else:
                    for b in range(width // P):
                        for kt in range(8):
                            cols = slice(b * P, (b + 1) * P)
                            o = ps[:, b, 0:TOK] if act and dve else ps[:, 0, b * TOK:(b + 1) * TOK]
                            ins = split_product(k, o, (wh[:, kt, cols], wl[:, kt, cols]),
                                                moving(kt), kt == 0, kt == 7)
                ins.then_inc(used.sem, 1)
        repeat(pe, groups, unroll, step, peel=peel)

    def program(eng, fn, s, split, st, per_steps):
        def read_out(i, j):
            eng.wait_ge(used.sem, i * per + (first + per))
            fn(i, j, k.pair[(group0 + j) % 2]).then_inc(s.sem, 1)

        early = per == 1 and split is split_low

        def step(i, j):
            if fn and early and j >= 1:
                read_out(i - 1, j - 1)
            for h in range(per):
                if split:
                    split(eng, k, i * per + (first + h + 1), first + j * per + h + 1)
                if fn and not early and h == 0 and j >= 1:
                    read_out(i - 1, j - 1)
        repeat(eng, groups, unroll, step, peel=max(peel, 1), steps=st, per=per_steps)
        if fn:
            read_out(groups - 1, groups - 1)
            s.base += groups

    @block.scalar
    def _(eng):
        program(eng, act, k.flag("act_evac"), split_high, None, 0)

    @block.vector
    def _(eng):
        if dve or low == "vector":
            program(eng, dve, k.flag("dve_evac"), split_low if low == "vector" else None, k.dve_steps, dve_per)

    @block.gpsimd
    def _(eng):
        if low == "gpsimd":
            program(eng, None, None, split_low, None, 0)
    k.chunk += per * groups
    k.group += groups


def nc_matmul(k, out, lhsT, rhs, start, stop):
    return k.nc.tensor.matmul(out, lhsT, rhs, start=start, stop=stop)


def ffn_order(pairs, downs):
    out = list(pairs[0])
    for i in range(1, len(pairs)):
        out += list(pairs[i]) + [downs[i - 1]]
    return out + [downs[-1]]


def ffn(block, k, add, conv=None):
    first, group0, n = k.chunk, k.group, NF // 2
    assert n % 2 == 1
    used, hidden = k.flag("slot_used"), k.flag("hidden_ready")
    act_evac, dve_evac = k.flag("act_evac"), k.flag("dve_evac")
    convolved, activated = k.flag("convolved"), k.flag("activated")
    nc, v = k.nc, k.nc.vector
    a_at = lambda i: first if isinstance(i, int) and i == 0 else i * 3 + (first - 1)
    acc = k.acc
    two = lambda x: x.rearrange("p (b t) -> p b t", b=2)

    @block.tensor
    def _(pe):
        for s in (act_evac, dve_evac):
            if s.base > 0:
                pe.wait_ge(s.sem, s.base)

        def down(i, j, parity):
            pe.wait_ge(hidden.sem, i + hidden.at(1))
            n_ = i * 3 + (first + 4) if not (isinstance(i, int) and i == n - 1) else first + 3 * n - 1
            wh, wl = slot_wait(pe, k, n_, parity, 2)
            for kk in range(2):
                for t in range(NT):
                    tok = slice(kk * TOK + t * P, kk * TOK + (t + 1) * P)
                    hh, hl = k.hid_high[:, j % 2, tok], k.hid_low[:, j % 2, tok]
                    for half in range(2):
                        cols = slice(half * 512, (half + 1) * 512)
                        ins = split_product(k, acc[half][:, t, :], (hh, hl), (wh[:, kk, cols], wl[:, kk, cols]),
                                            isinstance(i, int) and i == 0 and kk == 0,
                                            isinstance(i, int) and i == n - 1 and kk == 1)
            ins.then_inc(used.sem, 1)

        def step(i, j):
            ps = k.pair[(group0 + j) % 2]
            if not isinstance(i, int) or i >= 2:
                pe.wait_ge(hidden.sem, i + hidden.at(-1))
            for h in range(2):
                wh, wl = slot_wait(pe, k, a_at(i) + h, a_at(j) + h, 8)
                for b in range(2):
                    for kt in range(8):
                        cols = slice(b * P, (b + 1) * P)
                        ins = split_product(k, ps[:, h, b * TOK:(b + 1) * TOK], (wh[:, kt, cols], wl[:, kt, cols]),
                                            k.h_parts(kt), kt == 0, kt == 7)
                ins.then_inc(used.sem, 1)
            if j >= 1:
                down(i - 1, j - 1, a_at(j) + 2)
        repeat(pe, n, 2, step, peel=3)
        down(n - 1, n - 1, first + 3 * n - 1)

    @block.scalar
    def _(act):
        def step(i, j):
            late = 1 if j == 0 else 2
            for h in range(1, late + 2):
                split_high(act, k, a_at(i) + h, a_at(j) + h)
            y = k.ffn_act[:, j % 2, :]
            if conv:
                act.wait_ge(convolved.sem, i + convolved.at(1))
                nc.scalar.activation(y, k.ffn_conv[:, j % 2, :], ACT.Gelu_apprx_tanh).then_inc(activated.sem, 1)
            else:
                act.wait_ge(used.sem, a_at(i) + 1)
                if not isinstance(i, int) or i >= 2:
                    act.wait_ge(hidden.sem, i + hidden.at(-1))
                nc.scalar.activation(y, k.pair[(group0 + j) % 2][:, 0, :], ACT.Silu).then_inc(activated.sem, 1)
        repeat(act, n, 2, step, peel=3)
        split_high(act, k, first + 3 * n, first + 3 * n)

    @block.vector
    def _(dve):
        def step(i, j):
            ps = k.pair[(group0 + j) % 2]
            late = 1 if j == 0 else 2
            for h in range(1, late + 1):
                split_low(dve, k, a_at(i) + h, a_at(j) + h)
            if conv:
                cw, cb = conv
                dve.wait_ge(used.sem, a_at(i) + 1)
                y, a = two(k.ffn_conv[:, j % 2, :]), two(ps[:, 0, :])
                for b in range(2):
                    k.dve_steps.did(v.tensor_scalar(y[:, b, :], a[:, b, :], cw[:, 2, bass.ds(i * 2 + b, 1)],
                                                    cb[:, bass.ds(i * 2 + b, 1)], ALU.mult, ALU.add))
                for s in (1, 2):
                    k.dve_steps.settle(dve)
                    for b in range(2):
                        ins = v.scalar_tensor_tensor(y[:, b, s:TOK], a[:, b, 0:TOK - s],
                                                     cw[:, 2 - s, bass.ds(i * 2 + b, 1)], y[:, b, s:TOK], ALU.mult, ALU.add)
                        if s == 1:
                            k.dve_steps.did(ins)
                ins.then_inc(convolved.sem, 1)
            split_low(dve, k, a_at(i) + late + 1, a_at(j) + late + 1)
            dve.wait_ge(used.sem, a_at(i) + 2)
            dve.wait_ge(activated.sem, i + activated.at(1))
            y = k.ffn_act[:, j % 2, :]
            k.dve_steps.did(v.tensor_tensor(y, y, ps[:, 1, :], ALU.mult))
            k.dve_steps.settle(dve)
            if not isinstance(i, int) or i >= 2:
                dve.wait_ge(used.sem, i * 3 + (first + 4 - 6 + 1))
            k.dve_steps.did(v.tensor_copy(k.hid_high[:, j % 2, :], y))
            k.dve_steps.settle(dve)
            v.tensor_tensor(k.hid_low[:, j % 2, :], y, k.hid_high[:, j % 2, :].bitcast(F32), ALU.subtract
                            ).then_inc(hidden.sem, 1)
        repeat(dve, n, 2, step, peel=3, steps=k.dve_steps, per=6 if conv else 2)
        split_low(dve, k, first + 3 * n, first + 3 * n)
        dve.wait_ge(used.sem, first + 3 * n)
        for half in range(2):
            add(dve, half, acc[half]).then_inc(dve_evac.sem, 1)
    for s in (activated, hidden) + ((convolved,) if conv else ()):
        s.base += n
    dve_evac.base += 2
    k.chunk += 3 * n
    k.group += n + 1


def turn(block, k, src, ntiles, dst=None, normed=False, ready=None):
    turned = k.flag("turned")
    nc = k.nc
    batches = [(t, b) for t in range(NT) for b in range(ntiles // 4)]
    assert len(batches) <= 4
    high = k.flag("operand_high")
    part = lambda x, t, b: x[:, 4 * b:4 * b + 4, t * P:(t + 1) * P]
    bank = lambda n: k.bank[4 + n][:, :].rearrange("p (b t) -> p b t", b=4)

    @block.tensor
    def _(pe):
        for n, (t, b) in enumerate(batches):
            if normed and b == 0:
                pe.wait_ge(k.flag("normed").sem, k.flag("normed").at(t + 1 - NT))
            if ready and b == 0:
                pe.wait_ge(ready[t].sem, ready[t].at(1))
            for i in range(4):
                c = (4 * b + i) * P
                ins = nc.tensor.transpose(k.bank[4 + n][:, i * P:(i + 1) * P], src[:, t, c:c + P], k.c("ident"))
            ins.then_inc(turned.sem, 1)

    @block.scalar
    def _(act):
        for n, (t, b) in enumerate(batches):
            if dst is None:
                act.wait_ge(turned.sem, turned.at(n + 1))
                nc.scalar.copy(part(k.h_high, t, b), bank(n)).then_inc(high.sem, 1)
            elif n % 2 == 0:
                act.wait_ge(turned.sem, turned.at(n + 1))
                nc.scalar.copy(part(dst, t, b), bank(n))

    @block.vector
    def _(dve):
        for n, (t, b) in enumerate(batches):
            if dst is None:
                dve.wait_ge(high.sem, high.at(n + 1))
                nc.vector.tensor_tensor(part(k.h_low, t, b), bank(n), part(k.h_high, t, b).bitcast(F32), ALU.subtract)
            elif n % 2 == 1:
                dve.wait_ge(turned.sem, turned.at(n + 1))
                nc.vector.tensor_copy(part(dst, t, b), bank(n))
    turned.base += len(batches)
    for s in ready or ():
        s.base += 1
    if dst is None:
        high.base += len(batches)


def operand(block, k, src, half, free):
    high, low, used = k.flag("operand_high"), k.flag("operand_low"), k.flag("slot_used")
    part = lambda x: x[:, 4 * half:4 * half + 4, :]

    @block.scalar
    def _(act):
        act.wait_ge(used.sem, free)
        k.nc.scalar.copy(part(k.h_high), src).then_inc(high.sem, 1)

    @block.vector
    def _(dve):
        dve.wait_ge(high.sem, high.at(1))
        k.nc.vector.tensor_tensor(part(k.h_low), src, part(k.h_high).bitcast(F32), ALU.subtract).then_inc(low.sem, 1)

    @block.tensor
    def _(pe):
        pe.wait_ge(low.sem, low.at(1))
    high.base += 1
    low.base += 1


def rms_norm(block, k, gain, shift=None, eps=RMS_EPS, after=None):
    nc = k.nc
    squared, meaned, rooted, normed = k.flag("squared"), k.flag("meaned"), k.flag("rooted"), k.flag("normed")

    @block.scalar
    def _(act):
        nc.scalar.activation(k.xn[:, 0, :], k.x[:, 0, :], ACT.Square, accum_out=k.stat[:, 0:1]).then_inc(squared.sem, 1)
        act.wait_ge(meaned.sem, meaned.at(1))
        nc.scalar.activation(k.stat[:, 4:6], k.stat[:, 2:4], ACT.Sqrt).then_inc(rooted.sem, 1)
        if after:
            after(act)

    @block.vector
    def _(dve):
        k.dve_steps.did(nc.vector.scalar_tensor_tensor(k.xn[:, 1, :], k.x[:, 1, :], 1.0, k.x[:, 1, :], ALU.mult, ALU.mult,
                                                       accum_out=k.stat[:, 1:2]))
        k.dve_steps.settle(dve)
        dve.wait_ge(squared.sem, squared.at(1))
        nc.vector.tensor_scalar(k.stat[:, 2:4], k.stat[:, 0:2], 1.0 / D, eps, ALU.mult, ALU.add).then_inc(meaned.sem, 1)
        dve.wait_ge(rooted.sem, rooted.at(1))
        k.dve_steps.did(nc.vector.reciprocal(k.stat[:, 6:8], k.stat[:, 4:6]))
        k.dve_steps.settle(dve)
        for t in range(NT):
            ins = nc.vector.scalar_tensor_tensor(k.xn[:, t, :], k.x[:, t, :], k.stat[:, 6 + t:7 + t], gain,
                                                 ALU.mult, ALU.mult)
            if shift is None:
                ins.then_inc(normed.sem, 1)
            else:
                k.dve_steps.did(ins)
        if shift is not None:
            k.dve_steps.settle(dve)
            for t in range(NT):
                nc.vector.tensor_tensor(k.xn[:, t, :], k.xn[:, t, :], shift, ALU.add).then_inc(normed.sem, 1)
    for s in (squared, meaned, rooted):
        s.base += 1
    normed.base += NT


class Arena:

    def __init__(self, tile, size):
        self.tile, self.size, self.at = tile, size, 0

    def take(self, *shape):
        n = int(np.prod(shape))
        assert self.at + n <= self.size, (self.at, n, self.size)
        v = self.tile[:, self.at:self.at + n]
        self.at += n
        if len(shape) == 1:
            return v
        names = "abcd"[:len(shape)]
        return v.rearrange("p (" + " ".join(names) + ") -> p " + " ".join(names),
                           **{c: m for c, m in zip(names, shape)})


def attention(block, k, qkv, yT):
    nc = k.nc
    a = k.arena
    mark = a.at
    place = a.take(4 * D)
    rot = place[:, 0:2 * D].rearrange("p (t n) -> p t n", t=NT)
    part = place[:, 2 * D:4 * D].rearrange("p (t a h d) -> p t a h d", t=NT, a=2, h=16)
    PT = place[:, 0:HEADS * 384].rearrange("p (h n) -> p h n", h=HEADS)
    qkT = a.take(2 * NB, TOK)
    S = a.take(HEADS, NT, TOK)
    mx, tot, rec = k.mx, k.tot, k.rec
    scored, took, maxed, powered = (k.flag(n) for n in ("scored", "score_read", "maxed", "powered"))
    scaled = [k.flag("scaled_act"), k.flag("scaled_dve")]
    pturned, pread = k.flag("probs_turned"), [k.flag("probs_read_act"), k.flag("probs_read_dve")]
    mixed, yread, rec_ready = k.flag("mixed"), k.flag("mixed_read"), k.flag("recip_ready")
    units = [(h, t) for h in range(HEADS) for t in range(NT)]

    def rotate(op, steps, eng, t):
        src = qkv[:, t, 0:2 * WIDTH].rearrange("p (h x d) -> p x h d", h=16, x=2)
        dst = rot[:, t, :].rearrange("p (h x d) -> p x h d", h=16, x=2)
        cos = k.cos[:, t, :].unsqueeze(1).to_broadcast([P, 16, 32])
        sin = k.sin[:, t, :].unsqueeze(1).to_broadcast([P, 16, 32])
        for x, second in ((0, ALU.subtract), (1, ALU.add)):
            steps.did(op(part[:, t, 0], src[:, x], cos, ALU.mult))
            steps.did(op(part[:, t, 1], src[:, 1 - x], sin, ALU.mult))
            steps.settle(eng)
            steps.did(op(dst[:, x], part[:, t, 0], part[:, t, 1], second))
            steps.settle(eng)

    @block.vector
    def _(dve):
        rotate(nc.vector.tensor_tensor, k.dve_steps, dve, 0)

    @block.gpsimd
    def _(pool):
        rotate(nc.gpsimd.tensor_tensor, k.pool_steps, pool, 1)
    phase_end(block, k)
    turn(block, k, rot, 2 * NB, qkT)
    phase_end(block, k)

    def mix(pe, h):
        pe.wait_ge(pread[h % 2].sem, pread[h % 2].at(h // 2 + 1))
        b = h // 2
        if h % 2 == 0 and b >= 2:
            pe.wait_ge(yread.sem, yread.at(b - 1))
        o = k.bank[4 + b % 2][64 * (h % 2):64 * (h % 2) + 64, 0:TOK]
        v = lambda s: qkv[:, s, 2 * WIDTH + h * DH:2 * WIDTH + (h + 1) * DH]
        nc_matmul(k, o, v(0), PT[:, h, 0:TOK], True, False)
        nc_matmul(k, o[:, P:TOK], v(1), PT[:, h, TOK:384], False, True).then_inc(mixed.sem, 1)

    def out(act, b):
        act.wait_ge(mixed.sem, mixed.at(2 * b + 2))
        nc.scalar.copy(yT[:, b, :], k.bank[4 + b % 2][:, 0:TOK]).then_inc(yread.sem, 1)
    @block.tensor
    def _(pe):
        for u, (h, t) in enumerate(units):
            if u >= 2:
                pe.wait_ge(took.sem, took.at(u - 1))
            p0, n = 64 * (h % 2), (t + 1) * P
            nc_matmul(k, k.bank[4 + u % 2][:, 0:n], qkT[p0:p0 + 64, h // 2, t * P:(t + 1) * P],
                      qkT[p0:p0 + 64, NB + h // 2, 0:n], True, True).then_inc(scored.sem, 1)
        for h in range(HEADS):
            pe.wait_ge(scaled[h % 2].sem, scaled[h % 2].at(h // 2 + 1))
            if h >= 2:
                pe.wait_ge(pread[h % 2].sem, pread[h % 2].at(h // 2))
            for i, (t, s) in enumerate(((0, 0), (1, 0), (1, 1))):
                ins = nc.tensor.transpose(k.bank[6 + h % 2][:, i * P:(i + 1) * P], S[:, h, t, s * P:(s + 1) * P],
                                          k.c("ident"))
            ins.then_inc(pturned.sem, 1)
            if h >= 1:
                mix(pe, h - 1)
        mix(pe, HEADS - 1)

    @block.vector
    def _(dve):
        for u in range(len(units) + 3):
            if u < len(units):
                h, t = units[u]
                n = (t + 1) * P
                dve.wait_ge(scored.sem, scored.at(u + 1))
                nc.vector.scalar_tensor_tensor(S[:, h, t, 0:n], k.bank[4 + u % 2][:, 0:n], DH ** -0.5,
                                               k.blocked[:, t, 0:n], ALU.mult, ALU.add).then_inc(took.sem, 1)
            if 1 <= u <= len(units):
                h, t = units[u - 1]
                dve.wait_ge(took.sem, took.at(u))
                nc.vector.tensor_reduce(mx[:, u - 1:u], S[:, h, t, 0:(t + 1) * P], AX.X, ALU.max,
                                        negate=True).then_inc(maxed.sem, 1)
            if u >= 3:
                h, t = units[u - 3]
                n = (t + 1) * P
                dve.wait_ge(powered.sem, powered.at(u - 2))
                k.dve_steps.did(nc.vector.scalar_tensor_tensor(
                    S[:, h, t, 0:n], S[:, h, t, 0:n], 1.0, k.count[:, t, 0:n], ALU.mult, ALU.mult,
                    accum_out=tot[:, u - 3:u - 2]))
        k.dve_steps.settle(dve)
        nc.vector.reciprocal(rec[:, 0:16], tot[:, 0:16]).then_inc(rec_ready.sem, 1)
        dve.wait_ge(rec_ready.sem, rec_ready.at(1))
        for h in range(1, HEADS, 2):
            for t in range(NT):
                n = (t + 1) * P
                ins = nc.vector.tensor_scalar(S[:, h, t, 0:n], S[:, h, t, 0:n], rec[:, 2 * h + t:2 * h + t + 1], None,
                                              ALU.mult)
            ins.then_inc(scaled[1].sem, 1)
        for h in range(1, HEADS, 2):
            dve.wait_ge(pturned.sem, pturned.at(h + 1))
            nc.vector.tensor_copy(PT[:, h, :], k.bank[6 + h % 2][:, 0:384]).then_inc(pread[1].sem, 1)

    @block.scalar
    def _(act):
        for u, (h, t) in enumerate(units):
            n = (t + 1) * P
            act.wait_ge(maxed.sem, maxed.at(u + 1))
            nc.scalar.activation(S[:, h, t, 0:n], S[:, h, t, 0:n], ACT.Exp, bias=mx[:, u:u + 1]).then_inc(powered.sem, 1)
        act.wait_ge(rec_ready.sem, rec_ready.at(1))
        for h in range(0, HEADS, 2):
            for t in range(NT):
                n = (t + 1) * P
                ins = nc.scalar.activation(S[:, h, t, 0:n], S[:, h, t, 0:n], ACT.Copy,
                                           scale=rec[:, 2 * h + t:2 * h + t + 1])
            ins.then_inc(scaled[0].sem, 1)
        for h in range(0, HEADS, 2):
            act.wait_ge(pturned.sem, pturned.at(h + 1))
            nc.scalar.copy(PT[:, h, :], k.bank[6 + h % 2][:, 0:384]).then_inc(pread[0].sem, 1)
            if h >= 2:
                out(act, h // 2 - 1)
        out(act, NB - 1)

    for s, n in ((scored, 16), (took, 16), (maxed, 16), (powered, 16), (rec_ready, 1), (scaled[0], 4), (scaled[1], 4),
                 (pturned, 8), (pread[0], 4), (pread[1], 4), (mixed, 8), (yread, 4)):
        s.base += n
    phase_end(block, k)
    a.at = mark


def turn_back(block, k, src, dst, bank):
    turned, read = k.flag("turned"), k.flag("turn_read0")
    nc = k.nc

    @block.tensor
    def _(pe):
        for t in range(NT):
            for b in range(NB):
                ins = nc.tensor.transpose(k.bank[bank + t][:, b * P:(b + 1) * P], src[:, b, t * P:(t + 1) * P], k.c("ident"))
            ins.then_inc(turned.sem, 1)

    @block.scalar
    def _(act):
        for t in range(NT):
            act.wait_ge(turned.sem, turned.at(t + 1))
            nc.scalar.copy(dst[:, t, :], k.bank[bank + t][:, :]).then_inc(read.sem, 1)
    turned.base += NT
    read.base += NT


def delta_rule(block, k, AR, BT, KT, Btok, Ktok, Vtok, S, W, U, ends, y):
    nc, v, big = k.nc, k.nc.vector, k.big
    steps = k.dve_steps
    LEVELS = range(1, 6)
    wide8 = lambda x: x.rearrange("p (h t) -> p h t", h=HEADS)
    L, AK, RB, RK, Z, X, T = (k.arena.tile[:, k.gram_at + n * D:k.gram_at + (n + 1) * D] for n in range(7))
    AV = k.xn[:, 0, 0:WIDTH]
    over = lambda m, n=HEADS: k.c(m).unsqueeze(1).to_broadcast([P, n, P])
    head = lambda h: slice(64 * (h % 2), 64 * (h % 2) + 64)
    hp = lambda h: slice(((h % 2) * NB + h // 2) * P, ((h % 2) * NB + h // 2 + 1) * P)
    hv = lambda h: slice(h * DH, (h + 1) * DH)
    side = lambda x: slice(x * 512, (x + 1) * 512)
    heads = lambda x: range(x, HEADS, 2)
    grams, masked = k.flag("grams_done"), k.flag("grams_masked")
    lz, t_ready, second, z_added = (k.flag(n) for n in ("lz_done", "t_ready", "z_products", "z_added"))
    av, av_read = k.flag("av_done"), k.flag("av_read")
    as_done, w_ready, zw_done, u_ready = (k.flag(n) for n in ("as_done", "w_ready", "zw_done", "u_ready"))
    kv_done, bu_done, s_ready = (k.flag(n) for n in ("kv_done", "bu_done", "s_ready"))
    rs_done, rs_read, inner_done, inner_read = (k.flag(n) for n in ("rs_done", "rs_read", "inner_done", "inner_read"))
    chunks = lambda t: (2 * t, 2 * t + 1)
    where = lambda c: slice(64 * (c % 2), 64 * (c % 2) + 64)
    tokens = lambda c: slice(c * CHUNK, (c + 1) * CHUNK)

    @block.tensor
    def _(pe):
        for t in range(NT):
            tt = slice(t * P, (t + 1) * P)
            A_ = lambda h: AR[head(h), h // 2, 0, tt]
            R_ = lambda h: AR[head(h), h // 2, 1, tt]
            B_ = lambda h: BT[head(h), h // 2, tt]
            K_ = lambda h: KT[head(h), h // 2, tt]

            def gram(n, lhs, rhs):
                for h in range(HEADS):
                    ins = nc_matmul(k, big[n][:, hp(h)], lhs(h), rhs(h), True, True)
                ins.then_inc(grams.sem, 1)
            if t > 0:
                pe.wait_ge(s_ready.sem, s_ready.at(2 * t))
            gram(0, B_, A_)
            gram(1, A_, B_)
            gram(2, K_, A_)
            if t > 0:
                pe.wait_ge(rs_read.sem, rs_read.at(2 * t))
                pe.wait_ge(inner_read.sem, inner_read.at(t))
            gram(3, B_, R_)
            pe.wait_ge(masked.sem, masked.at(t + 1))
            for n, level in enumerate(LEVELS):
                for x in range(2):
                    if n > 0:
                        pe.wait_ge(z_added.sem, z_added.at(t * 10 + 2 * (n - 1) + x + 1))
                    for h in heads(x):
                        ins = nc_matmul(k, big[1][:, hp(h)], L[:, hp(h)], Z[:, hp(h)], True, True)
                    ins.then_inc(lz.sem, 1)
                if n == 0:
                    gram(0, K_, R_)
                for x in range(2):
                    pe.wait_ge(t_ready.sem, t_ready.at(t * 10 + 2 * n + x + 1))
                    for h in heads(x):
                        ins = nc_matmul(k, big[2][:, hp(h)], X[:, hp(h)], T[:, hp(h)], True, True)
                    for h in heads(x):
                        if level < 5:
                            ins = nc_matmul(k, big[3][:, hp(h)], T[:, hp(h)], X[:, hp(h)],
                                            True, True)
                    ins.then_inc(second.sem, 1)
                if level == 5:
                    for h in range(HEADS):
                        ins = nc_matmul(k, k.bank[7][:, hv(h)], AK[:, hp(h)], Vtok[:, t, hv(h)], True, True)
                    ins.then_inc(av.sem, 1)
            pe.wait_ge(z_added.sem, z_added.at(t * 10 + 10))
            for c in chunks(t):
                rows, now = where(c), S[:, c % 2]
                if c > 0:
                    pe.wait_ge(s_ready.sem, s_ready.at(c))
                for h in range(HEADS):
                    ins = nc_matmul(k, k.bank[h % 2][rows, (h // 2) * DH:(h // 2 + 1) * DH],
                                    AR[head(h), h // 2, 0, tokens(c)], now[head(h), h // 2, :], True, True)
                ins.then_inc(as_done.sem, 1)
                for h in range(HEADS):
                    ins = nc_matmul(k, k.bank[5][head(h), (h // 2) * 64:(h // 2) * 64 + 64], Ktok[rows, t, hv(h)],
                                    Vtok[rows, t, hv(h)], True, True)
                ins.then_inc(kv_done.sem, 1)
                pe.wait_ge(w_ready.sem, w_ready.at(c + 1))
                for h in range(HEADS):
                    inner = slice(hp(h).start + rows.start, hp(h).start + rows.stop)
                    ins = nc_matmul(k, k.bank[2][rows, hv(h)], Z[rows, inner], W[rows, hv(h)], True, True)
                ins.then_inc(zw_done.sem, 1)
                if c > 0:
                    pe.wait_ge(rs_read.sem, rs_read.at(c))
                for h in range(HEADS):
                    ins = nc_matmul(k, k.bank[6][head(h), (h // 2) * 64:(h // 2) * 64 + 64], now[head(h), h // 2, :],
                                    AR[head(h), h // 2, 1, tokens(c)], True, True)
                ins.then_inc(rs_done.sem, 1)
                pe.wait_ge(u_ready.sem, u_ready.at(c + 1))
                for h in range(HEADS):
                    ins = nc_matmul(k, k.bank[4][head(h), (h // 2) * 64:(h // 2) * 64 + 64], Btok[rows, t, hv(h)],
                                    U[rows, hv(h)], True, True)
                ins.then_inc(bu_done.sem, 1)
            for h in range(HEADS):
                o = k.bank[7][head(h), (h // 2) * P:(h // 2 + 1) * P]
                nc_matmul(k, o, U[:, hv(h)], RB[:, hp(h)], True, False)
                ins = nc_matmul(k, o, Vtok[:, t, hv(h)], RK[:, hp(h)], False, True)
            ins.then_inc(inner_done.sem, 1)

    @block.vector
    def _(dve):
        for t in range(NT):
            dve.wait_ge(grams.sem, grams.at(5 * t + 1))
            steps.did(v.tensor_tensor(wide8(Z), wide8(big[0]), over("level0"), ALU.mult))
            dve.wait_ge(grams.sem, grams.at(5 * t + 2))
            v.tensor_tensor(wide8(L), wide8(big[1]), over("strict_lo"), ALU.mult)
            steps.did(v.tensor_tensor(wide8(X), wide8(big[1]), over("lower0"), ALU.mult))
            steps.settle(dve)
            v.tensor_tensor(wide8(Z), wide8(Z), over("ident"), ALU.add)
            v.tensor_tensor(wide8(X), wide8(X), over("ident"), ALU.add).then_inc(masked.sem, 1)
            for n, dst, m in ((3, AK, "strict_up"), (4, RB, "incl_up")):
                dve.wait_ge(grams.sem, grams.at(5 * t + n))
                v.tensor_tensor(wide8(dst), wide8(big[n - 1]), over(m), ALU.mult)
            for n, level in enumerate(LEVELS):
                for x in range(2):
                    dve.wait_ge(lz.sem, lz.at(t * 10 + 2 * n + x + 1))
                    four_heads = lambda a: a[:, side(x)].rearrange("p (h t) -> p h t", h=NB)
                    v.tensor_tensor(four_heads(T), four_heads(big[1]), over(f"level{level}", NB), ALU.mult
                                    ).then_inc(t_ready.sem, 1)
                if n == 0:
                    dve.wait_ge(grams.sem, grams.at(5 * t + 5))
                    v.tensor_tensor(wide8(RK), wide8(big[0]), over("incl_up"), ALU.mult)
                for x in range(2):
                    dve.wait_ge(second.sem, second.at(t * 10 + 2 * n + x + 1))
                    v.tensor_tensor(Z[:, side(x)], Z[:, side(x)], big[2][:, side(x)], ALU.add).then_inc(z_added.sem, 1)
                    if level < 5:
                        v.tensor_tensor(X[:, side(x)], X[:, side(x)], big[3][:, side(x)], ALU.add)
            dve.wait_ge(av_read.sem, av_read.at(t + 1))
            for c in chunks(t):
                rows, now, nxt = where(c), S[:, c % 2], S[:, (c + 1) % 2]
                pairs = lambda x: x[rows, :].rearrange("p (b x d) -> p x b d", x=2, d=DH)
                flat = lambda x: x.rearrange("p b t -> p (b t)")
                dve.wait_ge(as_done.sem, as_done.at(c + 1))
                for x in range(2):
                    ins = v.tensor_tensor(pairs(W)[:, x], k.bank[x][rows, 0:256].rearrange("p (b d) -> p b d", d=DH),
                                          pairs(AV)[:, x], ALU.add)
                ins.then_inc(w_ready.sem, 1)
                dve.wait_ge(kv_done.sem, kv_done.at(c + 1))
                steps.did(v.tensor_tensor(flat(nxt), flat(now), k.bank[5][:, 0:256], ALU.add))
                steps.settle(dve)
                steps.did(v.tensor_tensor(nxt, nxt, ends[:, :, c:c + 1].to_broadcast([P, NB, 64]), ALU.mult))
                dve.wait_ge(zw_done.sem, zw_done.at(c + 1))
                v.tensor_copy(U[rows, :], k.bank[2][rows, :]).then_inc(u_ready.sem, 1)
                dve.wait_ge(bu_done.sem, bu_done.at(c + 1))
                steps.settle(dve)
                for b in range(NB):
                    ins = v.scalar_tensor_tensor(nxt[:, b, :], k.bank[4][:, b * 64:(b + 1) * 64], ends[:, b, c:c + 1],
                                                 nxt[:, b, :], ALU.mult, ALU.add)
                ins.then_inc(s_ready.sem, 1)
            yt = flat4(y)[:, :, t * P:(t + 1) * P]
            dve.wait_ge(rs_read.sem, rs_read.at(2 * t + 2))
            dve.wait_ge(inner_done.sem, inner_done.at(t + 1))
            v.tensor_tensor(yt, yt, flat4(k.bank[7]), ALU.add).then_inc(inner_read.sem, 1)

    @block.scalar
    def _(act):
        for t in range(NT):
            act.wait_ge(av.sem, av.at(t + 1))
            nc.scalar.copy(AV, k.bank[7]).then_inc(av_read.sem, 1)
            for c in chunks(t):
                act.wait_ge(rs_done.sem, rs_done.at(c + 1))
                nc.scalar.copy(flat4(y)[:, :, tokens(c)], k.bank[6][:, 0:256].rearrange("p (b t) -> p b t", b=NB)
                               ).then_inc(rs_read.sem, 1)
    for s, n in ((grams, 5), (masked, 1), (lz, 10), (t_ready, 10), (second, 10), (z_added, 10), (av, 1), (av_read, 1),
                 (as_done, 2), (w_ready, 2), (zw_done, 2), (u_ready, 2), (kv_done, 2), (bu_done, 2), (s_ready, 2),
                 (rs_done, 2), (rs_read, 2), (inner_done, 1), (inner_read, 1)):
        s.base += NT * n


def rwkv(block, k, zT, wide, scratch, keep, yT):
    nc, v = k.nc, k.nc.vector
    steps = k.dve_steps
    AR, BT, KT, g, bonus, Btok, Ktok, Vtok, y, S, W, U, ends = keep
    T2, T3, T4, small = scratch
    T0, T1, T5 = (flat4(x) for x in (k.xn[:, 0, :], k.xn[:, 1, :], y))
    T2, T3, T4 = flat4(T2), flat4(T3), flat4(T4)
    T0f = k.xn[:, 0, :]
    diff = k.arena.tile[:, k.tok_at:k.tok_at + NZ * TOK].rearrange("p (b t) -> p b t", t=TOK)
    R, K, V = zT[:, 0:4, :], zT[:, 4:8, :], zT[:, 8:12, :]
    th, sgx = small[:, 0:TOK], small[:, TOK:2 * TOK]
    lora, g_up = wide[:, 0:WIDTH], wide[:, WIDTH:2 * WIDTH]
    big = k.big
    four = lambda i: flat4(big[i])
    blk = lambda name, b: k.col[name][:, b:b + 1]

    diffed, shifted, lora_in = k.flag("token_diffs"), k.flag("shifted"), k.flag("lora_inputs")

    def differences(eng, lo, hi):
        eng.tensor_tensor(diff[:, lo:hi, 1:TOK], zT[:, lo:hi, 0:TOK - 1], zT[:, lo:hi, 1:TOK], ALU.subtract)
        return eng.tensor_scalar(diff[:, lo:hi, 0:1], zT[:, lo:hi, 0:1], -1.0, None, ALU.mult)

    def shift(b):
        return v.scalar_tensor_tensor(zT[:, b, :], diff[:, b, :], k.col["mu"][:, b:b + 1], zT[:, b, :], ALU.mult, ALU.add)

    @block.gpsimd
    def _(pool):
        differences(nc.gpsimd, 0, 5).then_inc(diffed.sem, 1)

    @block.vector
    def _(dve):
        steps.did(differences(v, 12, NZ))
        steps.settle(dve)
        for b in range(12, NZ):
            ins = shift(b)
        ins.then_inc(shifted.sem, 1)
        steps.did(differences(v, 5, 12))
        steps.settle(dve)
        for b in range(5, 12):
            shift(b)
        dve.wait_ge(diffed.sem, diffed.at(1))
        for b in range(5):
            shift(b)

    @block.scalar
    def _(act):
        act.wait_ge(shifted.sem, shifted.at(1))
        nc.scalar.activation(th[0:64, :], zT[0:64, 12, :], ACT.Tanh)
        nc.scalar.activation(sgx, zT[:, 13, :], ACT.Sigmoid).then_inc(lora_in.sem, 1)

    @block.tensor
    def _(pe):
        pe.wait_ge(lora_in.sem, lora_in.at(1))
        for t in range(NT):
            o = big[0][:, t * WIDTH:(t + 1) * WIDTH]
            nc_matmul(k, o, th[0:64, t * P:(t + 1) * P], lora[0:64, :], True, False)
            nc_matmul(k, o, k.c("ones")[0:1, :], k.w0[0:1, :], False, True)
        for b in range(NB):
            nc_matmul(k, big[1][:, b * TOK:(b + 1) * TOK], lora[64:P, b * P:(b + 1) * P], zT[64:P, 12, :], True, True)
            nc_matmul(k, big[2][:, b * TOK:(b + 1) * TOK], g_up[:, b * P:(b + 1) * P], sgx, True, True)
    for s in (diffed, shifted, lora_in):
        s.base += 1
    phase_end(block, k)

    @block.scalar
    def _(act):
        nc.scalar.activation(T0f, big[0], ACT.Sigmoid)
        for b in range(NB):
            nc.scalar.activation(T1[:, b, :], four(1)[:, b, :], ACT.Sigmoid, bias=blk("a0", b))

    @block.vector
    def _(dve):
        v.tensor_copy(g, big[2])
        for b in range(NB):
            steps.did(v.tensor_scalar(T5[:, b, :], K[:, b, :], blk("k_k", b), None, ALU.mult))
    phase_end(block, k)

    @block.tensor
    def _(pe):
        for n, m in ((0, "incl_up"), (1, "strict_up")):
            for b in range(NB):
                for t in range(NT):
                    nc_matmul(k, four(n)[:, b, t * P:(t + 1) * P], T0f[:, t * WIDTH + b * P:t * WIDTH + (b + 1) * P],
                              k.c(m), True, True)

    @block.vector
    def _(dve):
        v.tensor_tensor(diff[:, 0:4, :], T5, T5, ALU.mult)
        for b in range(NB):
            steps.did(v.tensor_scalar(diff[:, 4 + b, :], T1[:, b, :], -1.0, blk("k_a", b), ALU.add, ALU.mult))
        steps.settle(dve)
        v.scalar_tensor_tensor(K, diff[:, 4:8, :], 1.0, K, ALU.add, ALU.mult)
    phase_end(block, k)

    @block.tensor
    def _(pe):
        for half in range(2):
            nc_matmul(k, big[2][:, half * 512:(half + 1) * 512], k.c("blockones"),
                      diff[:, 2 * half:2 * half + 2, :].rearrange("p b t -> p (b t)"), True, True)

    @block.scalar
    def _(act):
        nc.scalar.activation(T2, four(0), ACT.Exp, scale=-DECAY)
        nc.scalar.activation(T3, four(0), ACT.Exp, scale=DECAY)
        nc.scalar.activation(T4, four(1), ACT.Exp, scale=-DECAY)

    @block.vector
    def _(dve):
        steps.did(v.tensor_tensor(T0, R, K, ALU.mult))
        steps.settle(dve)
        for b in range(NB):
            v.tensor_scalar(T0[:, b, :], T0[:, b, :], blk("r_k", b), None, ALU.mult)
    phase_end(block, k)

    @block.tensor
    def _(pe):
        for half in range(2):
            nc_matmul(k, big[3][:, half * 512:(half + 1) * 512], k.c("blockones"), T0f[:, half * 512:(half + 1) * 512],
                      True, True)

    @block.scalar
    def _(act):
        nc.scalar.activation(diff[:, 0:4, :], four(2), ACT.Sqrt)

    @block.gpsimd
    def _(pool):
        nc.gpsimd.tensor_copy(ends, T2[:, :, CHUNK - 1:TOK:CHUNK])
        nc.gpsimd.tensor_tensor(AR[:, :, 1, :], R, T2, ALU.mult)
        nc.gpsimd.tensor_tensor(KT, K, T3, ALU.mult)
    phase_end(block, k)

    b_ready = k.flag("b_ready")
    turn_back(block, k, V, Vtok, 4)
    turn_back(block, k, KT, Ktok, 0)

    @block.vector
    def _(dve):
        steps.did(v.tensor_scalar(diff[:, 0:4, :], diff[:, 0:4, :], 1e-12, None, ALU.max))
        steps.settle(dve)
        steps.did(v.reciprocal(diff[:, 0:4, :], diff[:, 0:4, :]))
        steps.settle(dve)
        steps.did(v.tensor_tensor(T5, T5, diff[:, 0:4, :], ALU.mult))
        steps.settle(dve)
        steps.did(v.tensor_tensor(T1, T5, T1, ALU.mult))
        steps.settle(dve)
        v.tensor_tensor(BT, T1, T3, ALU.mult).then_inc(b_ready.sem, 1)
        v.scalar_tensor_tensor(AR[:, :, 0, :], T5, -1.0, T4, ALU.mult, ALU.mult)
        v.tensor_tensor(flat4(bonus), four(3), V, ALU.mult)
        v.memset(S[:, 0], 0.0)

    @block.tensor
    def _(pe):
        pe.wait_ge(b_ready.sem, b_ready.at(1))
    turn_back(block, k, BT, Btok, 2)
    b_ready.base += 1
    phase_end(block, k)
    delta_rule(block, k, AR, BT, KT, Btok, Ktok, Vtok, S, W, U, ends, y)
    phase_end(block, k)

    half = lambda a, x: a[:, x * 512:(x + 1) * 512]
    summed, centred, varied, meaned, rooted = (k.flag(n) for n in ("head_sums", "centred", "head_squares", "meaned",
                                                                   "rooted"))

    @block.tensor
    def _(pe):
        for x in range(2):
            nc_matmul(k, half(big[0], x), k.c("blockones"), half(y, x), True, True).then_inc(summed.sem, 1)
        for x in range(2):
            pe.wait_ge(centred.sem, centred.at(x + 1))
            nc_matmul(k, half(big[1], x), k.c("blockones"), half(T0f, x), True, True).then_inc(varied.sem, 1)

    @block.vector
    def _(dve):
        for x in range(2):
            dve.wait_ge(summed.sem, summed.at(x + 1))
            steps.did(v.scalar_tensor_tensor(half(y, x), half(big[0], x), -1.0 / DH, half(y, x), ALU.mult, ALU.add))
            steps.settle(dve)
            v.tensor_tensor(half(T0f, x), half(y, x), half(y, x), ALU.mult).then_inc(centred.sem, 1)
        for x in range(2):
            dve.wait_ge(varied.sem, varied.at(x + 1))
            v.tensor_scalar(half(T0f, x), half(big[1], x), 1.0 / DH, GN_EPS, ALU.mult, ALU.add).then_inc(meaned.sem, 1)

    @block.scalar
    def _(act):
        for x in range(2):
            act.wait_ge(meaned.sem, meaned.at(x + 1))
            nc.scalar.activation(half(T0f, x), half(T0f, x), ACT.Sqrt).then_inc(rooted.sem, 1)

    @block.vector
    def _(dve):
        for x in range(2):
            dve.wait_ge(rooted.sem, rooted.at(x + 1))
            steps.did(v.reciprocal(half(T0f, x), half(T0f, x)))
            steps.settle(dve)
            steps.did(v.tensor_tensor(half(y, x), half(y, x), half(T0f, x), ALU.mult))
            steps.settle(dve)
            for b in (2 * x, 2 * x + 1):
                steps.did(v.tensor_scalar(flat4(y)[:, b, :], flat4(y)[:, b, :], blk("gn_w", b), blk("gn_b", b), ALU.mult,
                                          ALU.add))
            steps.settle(dve)
            steps.did(v.tensor_tensor(half(y, x), half(y, x), half(bonus, x), ALU.add))
            steps.settle(dve)
            v.tensor_tensor(yT[:, 2 * x:2 * x + 2, :].rearrange("p b t -> p (b t)"), half(y, x), half(g, x), ALU.mult)
    for s in (summed, centred, varied, meaned, rooted):
        s.base += 2


def flat4(x):
    return x.rearrange("p (b t) -> p b t", b=NB)


def gmlp(block, k, uv, w_s, yT, products):
    nc, v = k.nc, k.nc.vector
    steps = k.dve_steps
    ln_g, ln_b = k.ln[:, 0:WIDTH], k.ln[:, WIDTH:2 * WIDTH]
    vv = lambda t: uv[:, t, WIDTH:2 * WIDTH]
    varied, rooted, masked = k.flag("variance_ready"), k.flag("deviation_ready"), k.flag("w_s_masked")
    normed, spatial, gated = k.flag("v_normed"), k.flag("v_mixed"), k.flag("u_gated")

    @block.gpsimd
    def _(pool):
        nc.gpsimd.tensor_tensor(w_s.rearrange("p (g i) -> p g i", g=HEADS), w_s.rearrange("p (g i) -> p g i", g=HEADS),
                                k.c("upper").unsqueeze(1).to_broadcast([P, HEADS, P]), ALU.mult).then_inc(masked.sem, 1)

    @block.vector
    def _(dve):
        for t in range(NT):
            steps.did(v.tensor_reduce(k.stat[:, t:t + 1], vv(t), AX.X, ALU.add))
        steps.settle(dve)
        steps.did(v.tensor_scalar(k.stat[:, 2:4], k.stat[:, 0:2], -1.0 / WIDTH, None, ALU.mult))
        steps.settle(dve)
        for t in range(NT):
            steps.did(v.tensor_scalar(vv(t), vv(t), k.stat[:, 2 + t:3 + t], None, ALU.add))
        steps.settle(dve)
        for t in range(NT):
            steps.did(v.scalar_tensor_tensor(k.xn[:, t, 0:WIDTH], vv(t), 1.0, vv(t), ALU.mult, ALU.mult,
                                             accum_out=k.stat[:, t:t + 1]))
        steps.settle(dve)
        v.tensor_scalar(k.stat[:, 2:4], k.stat[:, 0:2], 1.0 / WIDTH, LN_EPS, ALU.mult, ALU.add).then_inc(varied.sem, 1)

    @block.scalar
    def _(act):
        act.wait_ge(varied.sem, varied.at(1))
        nc.scalar.activation(k.stat[:, 4:6], k.stat[:, 2:4], ACT.Sqrt).then_inc(rooted.sem, 1)

    @block.vector
    def _(dve):
        dve.wait_ge(rooted.sem, rooted.at(1))
        steps.did(v.reciprocal(k.stat[:, 6:8], k.stat[:, 4:6]))
        steps.settle(dve)
        for t in range(NT):
            steps.did(v.scalar_tensor_tensor(vv(t), vv(t), k.stat[:, 6 + t:7 + t], ln_g, ALU.mult, ALU.mult))
        steps.settle(dve)
        for t in range(NT):
            ins = v.tensor_tensor(vv(t), vv(t), ln_b, ALU.add)
        ins.then_inc(normed.sem, 1)
    products(0)

    @block.tensor
    def _(pe):
        pe.wait_ge(masked.sem, masked.at(1))
        pe.wait_ge(normed.sem, normed.at(1))
        for t in range(NT):
            for g in range(HEADS):
                ins = nc_matmul(k, k.bank[4 + t][:, g * 64:(g + 1) * 64], w_s[:, g * P:(g + 1) * P],
                                uv[:, t, WIDTH + g * 64:WIDTH + (g + 1) * 64], True, True)
        ins.then_inc(spatial.sem, 1)

    @block.vector
    def _(dve):
        dve.wait_ge(spatial.sem, spatial.at(1))
        for t in range(NT):
            for g in range(HEADS):
                u = uv[:, t, g * 64:(g + 1) * 64]
                ins = v.scalar_tensor_tensor(u, k.bank[4 + t][:, g * 64:(g + 1) * 64], k.col["b_s"][:, g:g + 1], u, ALU.add,
                                             ALU.mult)
        ins.then_inc(gated.sem, 1)
        take_over_low(dve, k)
    products(1)

    @block.tensor
    def _(pe):
        pe.wait_ge(gated.sem, gated.at(1))
    turn(block, k, uv, NB, yT)
    for s in (varied, rooted, masked, normed, spatial, gated):
        s.base += 1
    phase_end(block, k)


def chunk_arrays():
    def tiles(m):
        return m.reshape(-1, P, m.shape[1]).transpose(1, 0, 2).reshape(P, SLOT)

    def token(m, kt=4):
        n = SLOT // kt
        return [tiles(m[r:r + kt * P, c:c + n]) for c in range(0, m.shape[1], n) for r in range(0, m.shape[0], kt * P)]

    def channel(m):
        return token(m, 8)

    def ffn(a, g, d):
        return ffn_order(list(zip(channel(a), channel(g))), [tiles(d[r:r + 2 * P]) for r in range(0, D_FF, 2 * P)])
    return token, channel, ffn


def first_stream(v, l):
    token, channel, ffn = chunk_arrays()
    w = v["w_in"][l]
    out = token(w[:, :RWKV0]) + channel(w[:, RWKV0:UV0]) + token(w[:, UV0:])
    out += [c for n in range(3) for c in token(v["w_branch"][l, n])] + token(v["w_out"][l])
    out += ffn(v["ffn_w_up"][l][:, :D_FF], v["ffn_w_up"][l][:, D_FF:], v["ffn_w_down"][l])
    return np.stack(out)


FIRST_COLS = {"c": KD, "mu": NZ, "a0": NB, "k_k": NB, "k_a": NB, "r_k": NB, "gn_w": NB, "gn_b": NB,
              "conv_w": 3 * NF, "conv_b": NF, "b_s": HEADS}
FIRST_WIDE = {"lora": WIDTH, "g_up": WIDTH, "w_s": HEADS * P}


def first_small(v, l):
    col = lambda a: a.reshape(-1, P).T
    cols = [col(v["c"][0]), col(v["rwkv_mu"][l]), col(v["rwkv_a0"][l]), col(v["rwkv_k_k"][l]), col(v["rwkv_k_a"][l]),
            col(v["rwkv_r_k"][l].reshape(-1)), col(v["rwkv_gn_w"][l]), col(v["rwkv_gn_b"][l]),
            col(v["ffn_conv_w"][l].reshape(-1)), col(v["ffn_conv_b"][l]), v["gmlp_b_s"][l].T]
    wide = [np.concatenate([v["rwkv_w_up"][l], v["rwkv_a_up"][l]]), v["rwkv_g_up"][l],
            v["gmlp_w_s"][l].transpose(2, 0, 1).reshape(P, -1)]
    rows = [v["b_ada"][l], v["rwkv_w0"][l]]
    spread = [v["norm_mix"][l], v["norm_ffn"][l], v["gmlp_ln_g"][l], v["gmlp_ln_b"][l]]
    return [np.concatenate(cols, 1), np.concatenate(wide, 1), np.concatenate(rows), np.concatenate(spread)]


def columns(tile, sizes):
    out, at = {}, 0
    for name, n in sizes.items():
        out[name] = tile[:, at:at + n]
        at += n
    return out


def modulation(block, k, weights, cact, rowb, ring, sums):
    nc, v = k.nc, k.nc.vector
    landed = [k.flag(f"ada_landed{i}") for i in range(ADA_SLOTS)]
    used, summed, copied, c_ready = k.flag("ada_used"), k.flag("ada_summed"), k.flag("ada_copied"), k.flag("c_ready")
    groups = 3
    both = lambda g: [k.big[2 * (g % 2) + half] for half in range(2)]

    @block.sync
    def _(sp):
        for n in range(groups * KD):
            if n >= ADA_SLOTS:
                sp.wait_ge(used.sem, n + 1 - ADA_SLOTS)
            sp.dma_start(ring[n % ADA_SLOTS], weights[n]).then_inc(landed[n % ADA_SLOTS].sem, 16)

    @block.vector
    def _(dve):
        dve.wait_ge(c_ready.sem, c_ready.at(1))
        for n in range(groups * KD):
            g, kt = divmod(n, KD)
            w, total, scale = ring[n % ADA_SLOTS], sums[g % 2], cact[:, kt:kt + 1]
            dve.wait_ge(landed[n % ADA_SLOTS].sem, 16 * (n // ADA_SLOTS + 1))
            if kt == 0:
                if g >= 2:
                    dve.wait_ge(summed.sem, summed.at(g - 1))
                ins = v.tensor_scalar(total, w, scale, None, ALU.mult)
                if g == 0:
                    dve.wait_ge(k.flag("small_landed").sem, k.flag("small_landed").base)
                k.dve_steps.did(ins)
                k.dve_steps.settle(dve)
                ins = v.tensor_tensor(total[0:1, :], total[0:1, :], rowb[0:1, g * SLOT:(g + 1) * SLOT], ALU.add)
            else:
                dve.wait_ge(used.sem, used.at(n))
                ins = v.scalar_tensor_tensor(total, w, scale, total, ALU.mult, ALU.add)
            ins.then_inc(used.sem, 1)

    @block.tensor
    def _(pe):
        for g in range(groups):
            pe.wait_ge(used.sem, used.at(KD * (g + 1)))
            if g >= 2:
                pe.wait_ge(copied.sem, copied.at(g - 1))
            for q in range(4):
                o = both(g)[q // 2][:, (q % 2) * 512:(q % 2 + 1) * 512]
                ins = nc_matmul(k, o, k.c("ones"), sums[g % 2][:, q * 512:(q + 1) * 512], True, True)
            ins.then_inc(summed.sem, 1)

    first_sum = summed.base

    def copy_out(act, g):
        act.wait_ge(summed.sem, first_sum + g + 1)
        if g == 0:
            act.wait_ge(k.lines_stored, 16)
        for half in range(2):
            at = g * SLOT + half * D
            ins = nc.scalar.copy(mod_flat(k)[:, at:at + D], both(g)[half])
        ins.then_inc(copied.sem, 1)

    @block.scalar
    def _(act):
        for g in range(groups - 1):
            copy_out(act, g)

    @block.vector
    def _(dve):
        dve.wait_ge(copied.sem, copied.at(1))
        dve.wait_ge(summed.sem, summed.at(2))
    used.base += groups * KD
    summed.base += groups
    copied.base += groups
    c_ready.base += 1
    for s in landed:
        s.base += 16 * (groups * KD // ADA_SLOTS)
    return lambda act: copy_out(act, groups - 1)


def first_layer(block, k, A, l):
    nc = k.nc
    a = k.arena
    a.at = 0
    mod = a.take(6, D)
    yT = a.take(3 * NB, TOK)
    body = a.at
    small = k.flag("small_landed")
    rowb = a.take(6 * D)
    cact, spread = a.take(KD), a.take(2 * D)
    parts = lambda kt, t: (k.h_high[:, kt, t * P:(t + 1) * P], k.h_low[:, kt, t * P:(t + 1) * P])
    tok = lambda kt, t, i: parts(kt, t)
    row = lambda name: A[name][bass.ds(l, 1)]
    ring = [a.take(SLOT) for _ in range(ADA_SLOTS)]

    @block.scalar
    def _(act):
        act.dma_start(k.cols1[:], row("cols1").rearrange("a p n -> (a p) n")).then_inc(k.flag("cols_landed").sem, 16)
        for dst, src in ((rowb[0:1, :], row("rows1")[:, 0:6 * D]), (k.w0[0:1, :], row("rows1")[:, 6 * D:6 * D + WIDTH]),
                         (spread, row("spread1")[:, 0:2 * D].partition_broadcast(P).rearrange("p a n -> p (a n)"))):
            act.dma_start(dst, src).then_inc(small.sem, 16)
        act.wait_ge(k.flag("cols_landed").sem, 16)
        nc.scalar.activation(cact, k.col["c"], ACT.Silu).then_inc(k.flag("c_ready").sem, 1)

    small.base += 48
    last = modulation(block, k, row("ada").rearrange("a c p n -> (a c) p n"), cact, rowb, ring,
                      [yT.rearrange("p b t -> p (b t)")[:, 0:SLOT], k.xn[:, :, :].rearrange("p t n -> p (t n)")])
    stream(block, k, A["stream1"][bass.ds(l, 1)].rearrange("a c p n -> (a c) p n"), 72)

    def scale_gain(scale, n):
        @block.vector
        def _(dve):
            k.dve_steps.did(nc.vector.scalar_tensor_tensor(mod[:, scale, :], mod[:, scale, :], 1.0,
                                                           spread[:, n * D:(n + 1) * D], ALU.add, ALU.mult))
            k.dve_steps.settle(dve)
    scale_gain(1, 0)
    rms_norm(block, k, mod[:, 1, :], mod[:, 0, :], after=last)

    @block.scalar
    def _(act):
        split_high(act, k, 0, 0)
    turn(block, k, k.xn, KD, normed=True)

    @block.vector
    def _(dve):
        split_low(dve, k, 0, 0)
    phase_end(block, k)
    scale_gain(4, 1)
    a.at = body
    att = a.take(NT, 3 * WIDTH)
    product(block, k, "token", 512, 3, stationary=tok,
            act=lambda i, j, ps: nc.scalar.copy(att[:, 0, i * 512:(i + 1) * 512], ps[:, 0, :]),
            dve=lambda i, j, ps: nc.vector.tensor_copy(att[:, 1, i * 512:(i + 1) * 512], ps[:, 1, :]))
    phase_end(block, k)
    attention(block, k, att, yT)
    k.yT = yT
    a.at = body
    AR = mod[:, 0:2, :].rearrange("p m n -> p (m n)").rearrange("p (b x t) -> p b x t", b=NB, x=2)
    BT, KT = a.take(NB, TOK), a.take(NB, TOK)
    g, bonus = (yT[:, n * NB:(n + 1) * NB, :].rearrange("p b t -> p (b t)") for n in (2, 1))
    k.tok_at = a.at
    Btok, Ktok, Vtok = (a.take(NT, WIDTH) for _ in range(3))
    y = a.take(D)
    S, W, U, ends = a.take(2, NB, 64), a.take(WIDTH), a.take(WIDTH), a.take(NB, NCH)
    k.gram_at = a.at
    zT = a.take(NZ, TOK)
    lora = a.take(2 * WIDTH)
    scratch = [a.take(D), a.take(D), a.take(D), a.take(2 * TOK)]
    assert k.gram_at + 7 * D <= a.size

    @block.scalar
    def _(act):
        act.dma_start(lora, row("wide1")[:, :, 0:2 * WIDTH].rearrange("a p n -> (a p) n")).then_inc(small.sem, 16)
    small.base += 16
    zcopy = lambda f: lambda i, j, ps: f(zT[:, 2 * i:2 * i + 2, :].rearrange("p b t -> p (b t)"), ps[:, 0, :])
    product(block, k, "channel", 256, NZ // 2, moving=k.h_parts, unroll=8, act=zcopy(nc.scalar.copy))

    @block.tensor
    def _(pe):
        pe.wait_ge(small.sem, small.base)
    phase_end(block, k)
    rwkv(block, k, zT, lora, scratch, (AR, BT, KT, g, bonus, Btok, Ktok, Vtok, y, S, W, U, ends), yT[:, NB:2 * NB, :])
    a.at = body
    uv = a.take(NT, 2 * WIDTH)
    w_s, k.ln = a.take(HEADS * P), a.take(2 * WIDTH)

    @block.scalar
    def _(act):
        act.dma_start(k.ln, row("spread1")[:, 2 * D:2 * D + 2 * WIDTH].partition_broadcast(P).rearrange("p a n -> p (a n)")
                      ).then_inc(small.sem, 16)
        act.dma_start(w_s, row("wide1")[:, :, 2 * WIDTH:].rearrange("a p n -> (a p) n")).then_inc(small.sem, 16)
        act.wait_ge(small.sem, small.base + 32)
    small.base += 32

    both = token_out_dyn
    product(block, k, "token", 512, 2, stationary=tok, low="gpsimd",
            act=both(lambda o, i: nc.scalar.activation(o, i, ACT.Gelu_apprx_tanh), uv))
    phase_end(block, k)
    gates = a.take(NT, 3 * D)

    def gate_product(n):
        half = gates[:, :, n * 1536:(n + 1) * 1536]
        product(block, k, "token", 512, 3, stationary=tok, low=("gpsimd", "vector")[n],
                act=both(lambda o, i: nc.scalar.activation(o, i, ACT.Sigmoid), half))
    gmlp(block, k, uv, w_s, yT[:, 2 * NB:, :], gate_product)
    y4 = lambda n: yT[:, n * NB:(n + 1) * NB, :]
    done = k.chunk
    operand(block, k, y4(0), 0, done)
    operand(block, k, y4(1), 1, done)
    for n in range(3):
        product(block, k, "token", 512, 2, ktiles=4, stationary=lambda kt, t, i, n=n: parts(4 * (n % 2) + kt, t),
                dve=both(lambda o, i: nc.vector.tensor_tensor(o, o, i, ALU.mult), gates[:, :, n * D:(n + 1) * D]))
        if n == 0:
            operand(block, k, y4(2), 0, k.chunk)
    phase_end(block, k)

    merged = [k.flag("merged_dve"), k.flag("merged_pool")]

    def merge(op, steps, eng, t):
        steps.did(op(gates[:, t, 0:D], gates[:, t, 0:D], gates[:, t, D:2 * D], ALU.add))
        steps.settle(eng)
        op(gates[:, t, 0:D], gates[:, t, 0:D], gates[:, t, 2 * D:3 * D], ALU.add).then_inc(merged[t].sem, 1)

    @block.vector
    def _(dve):
        merge(nc.vector.tensor_tensor, k.dve_steps, dve, 0)

    @block.gpsimd
    def _(pool):
        merge(nc.gpsimd.tensor_tensor, k.pool_steps, pool, 1)
    turn(block, k, gates, KD, ready=merged)
    phase_end(block, k)
    product(block, k, "token", 512, 2, stationary=tok, dve=lambda i, j, ps: gated_add(k, i, ps, mod[:, 2, :]))
    phase_end(block, k)
    rms_norm(block, k, mod[:, 4, :], mod[:, 3, :])
    turn(block, k, k.xn, KD, normed=True)
    phase_end(block, k)
    a.at = body
    k.ffn_act, k.ffn_conv = a.take(2, 512), a.take(2, 512)
    ffn(block, k, lambda dve, half, ps: gated_add(k, half, ps, mod[:, 5, :]),
        conv=(k.col["conv_w"].rearrange("p (j b) -> p j b", j=3), k.col["conv_b"]))
    phase_end(block, k)


def gated_add(k, i, ps, gate):
    cols = slice(i * 512, (i + 1) * 512)
    for t in range(NT):
        k.dve_steps.did(k.nc.vector.tensor_tensor(k.xn[:, t, cols], ps[:, t, :], gate[:, cols], ALU.mult))
    k.dve_steps.settle(k.nc.vector)
    for t in range(NT):
        ins = k.nc.vector.tensor_tensor(k.x[:, t, cols], k.x[:, t, cols], k.xn[:, t, cols], ALU.add)
    return ins


def mod_flat(k):
    return k.arena.tile[:, 0:6 * D]


def second_stream(v, l):
    token, channel, ffn = chunk_arrays()
    w = v["w_in_2"][l]
    out = ffn(v["ffn1_w_gate_2"][l], v["ffn1_w_up_2"][l], v["ffn1_w_down_2"][l])
    out += channel(w[:, :S_GA]) + token(v["cmp_k_w1_2"][l], 8) + token(v["cmp_v_w1_2"][l], 8)
    out += channel(w[:, S_QB:S_VB]) + token(w[:, S_VB:S_AL]) + token(w[:, S_RB:])
    out += token(v["w_branch_nsa_2"][l]) + token(v["w_branch_gla_2"][l]) + token(v["w_out_2"][l])
    out += ffn(v["ffn2_w_gate_2"][l], v["ffn2_w_up_2"][l], v["ffn2_w_down_2"][l])
    return np.stack(out)


SECOND_COLS = {"pos_k": 16, "pos_v": 16, "w_small": KD * SMALL, "w2_k": 2 * DH, "w2_v": 2 * DH}


def second_small(v, l):
    pos = lambda p: p.reshape(16, 2, DH).transpose(1, 2, 0).reshape(P, 16)
    tiles = lambda m: m.reshape(-1, P, m.shape[1]).transpose(1, 0, 2).reshape(P, -1)
    w = v["w_in_2"][l]
    cols = [pos(v["cmp_pos_k_2"][l]), pos(v["cmp_pos_v_2"][l]),
            tiles(np.concatenate([w[:, S_AL:S_RB], np.zeros((D, GATE_AT - 16), np.float32), w[:, S_GA:S_QB]], 1)), tiles(v["cmp_k_w2_2"][l]),
            tiles(v["cmp_v_w2_2"][l])]
    rows = [v["gla_a_b_2"][l]]
    spread = [v["ffn1_norm_2"][l], v["mix_norm_2"][l], v["ffn2_norm_2"][l], v["gla_out_norm_2"][l]]
    return [np.concatenate(cols, 1), v["gla_a_w2_2"][l], np.concatenate(rows), np.concatenate(spread)]


def distance_lines(block, k, A, nc, load_constants):
    a = k.arena
    a.at = 0
    table, onehot, cols, line = a.take(HEADS), a.take(TOK), a.take(HEADS, P), a.take(HEADS, 512)
    loaded, v = k.flag("table_landed"), nc.vector

    @block.sync
    def _(sp):
        sp.dma_start(table[0:32, :], A["rel_table"]).then_inc(loaded.sem, 16)
        sp.dma_start(onehot[0:32, :], A["c_onehot"]).then_inc(loaded.sem, 16)
        load_constants(sp)

    @block.vector
    def _(dve):
        dve.wait_ge(loaded.sem, 32)
        dve.wait_ge(k.square_landed, 16)
        for h in range(HEADS):
            v.tensor_scalar(cols[0:32, h, :], k.c("ones")[0:32, :], table[0:32, h:h + 1], None, ALU.mult)
        v.memset(line[:, :, TOK:512], NEG)
    phase_end(block, k)

    @block.tensor
    def _(pe):
        for h in range(HEADS):
            nc_matmul(k, k.bank[h][:, 0:TOK], cols[0:32, h, :], onehot[0:32, :], True, True)
    phase_end(block, k)

    @block.vector
    def _(dve):
        for h in range(HEADS):
            v.tensor_copy(line[:, h, 0:TOK], k.bank[h][:, 0:TOK])
    phase_end(block, k)

    @block.sync
    def _(sp):
        flat = k.lines.rearrange("(p n) -> p n", n=HEADS * 512)
        sp.wait_ge(k.flag("phase_arrived").sem, 4 * k.phase)
        sp.dma_start(flat[0:P, :].rearrange("p (h n) -> p h n", h=HEADS), line).then_inc(k.lines_stored, 16)


def distance_bias(block, k):
    k.arena.at = 0
    k.bias = k.arena.take(HEADS, NT, TOK)
    pitch = HEADS * 512

    @block.sync
    def _(sp):
        sp.wait_ge(k.lines_stored, 16)
        for t in range(NT):
            c = TOK - 1 - t * P
            skewed = k.lines[c:c + P * (pitch - 1)].rearrange("(p n) -> p n", n=pitch - 1)
            for h in range(HEADS):
                sp.dma_start(k.bias[:, h, t, :], skewed[:, h * 512:h * 512 + TOK]).then_inc(k.bias_landed, 16)


def compress(block, k, pairs, keysT, values):
    nc, v = k.nc, k.nc.vector
    a = k.arena
    mark = a.at
    blocks = a.take(2, 16, 2, NC)
    hid, hid_tok = a.take(2, 2, 2 * NC), a.take(2, 2 * P)
    first = k.chunk
    used = k.flag("slot_used")

    @block.vector
    def _(dve):
        for n, name in enumerate(("pos_k", "pos_v")):
            for g in range(2):
                tokens = pairs[:, n, g, :].rearrange("p (c q) -> p q c", q=8)
                for late in range(2):
                    v.tensor_tensor(blocks[:, n, 8 * late:8 * late + 8, g, :], tokens[:, :, late:late + NC],
                                    k.col2[name][:, 8 * late:8 * late + 8].unsqueeze(2).to_broadcast([P, 8, NC]), ALU.add)
    phase_end(block, k)
    size = 2 * 16 * 2 * NC
    whole = blocks.rearrange("p n q g c -> p (n q g c)")
    parts = [x[:, :, :].rearrange("p a n -> p (a n)")[:, 0:size] for x in (k.hid_high, k.hid_low)]
    bh, bl = (x.rearrange("p (n q c) -> p n q c", n=2, q=16) for x in parts)

    @block.scalar
    def _(act):
        nc.scalar.copy(parts[0], whole)
    phase_end(block, k)

    @block.vector
    def _(dve):
        v.tensor_tensor(parts[1], whole, parts[0].bitcast(F32), ALU.subtract)
    phase_end(block, k)

    @block.tensor
    def _(pe):
        for n in range(2):
            for h in range(2):
                c = first + 2 * n + h
                wh, wl = slot_wait(pe, k, c, c, 8)
                for kt in range(8):
                    q = 8 * h + kt
                    ins = split_product(k, k.bank[4 + n][0:2 * NC, 0:2 * P], (bh[:, n, q, :], bl[:, n, q, :]),
                                        (wh[:, kt, :], wl[:, kt, :]), q == 0, q == 15)
                ins.then_inc(used.sem, 1)

    @block.scalar
    def _(act):
        for c in range(first + 1, first + 5):
            split_high(act, k, c, c)

    @block.vector
    def _(dve):
        for c in range(first + 1, first + 5):
            split_low(dve, k, c, c)
    k.chunk += 4
    phase_end(block, k)

    @block.scalar
    def _(act):
        for n in range(2):
            nc.scalar.activation(hid_tok[0:2 * NC, n, :], k.bank[4 + n][0:2 * NC, 0:2 * P], ACT.Silu)
    phase_end(block, k)

    @block.tensor
    def _(pe):
        for n in range(2):
            for hb in range(2):
                at = (2 * n + hb) * 2 * NC
                nc.tensor.transpose(k.bank[7][:, at:at + 2 * NC], hid_tok[0:2 * NC, n, hb * P:(hb + 1) * P],
                                    k.c("ident")[0:2 * NC, 0:2 * NC])
    phase_end(block, k)

    @block.vector
    def _(dve):
        v.tensor_copy(hid.rearrange("p n b c -> p (n b c)"), k.bank[7][:, 0:8 * NC])
    phase_end(block, k)

    @block.tensor
    def _(pe):
        for hb in range(2):
            nc_matmul(k, k.bank[4][0:64, 0:2 * NC], k.col2["w2_k"][:, hb * DH:(hb + 1) * DH], hid[:, 0, hb, :], hb == 0, hb == 1)
        for g in range(2):
            for hb in range(2):
                nc_matmul(k, k.bank[5][0:NC, g * DH:(g + 1) * DH], hid[:, 1, hb, g * NC:(g + 1) * NC],
                          k.col2["w2_v"][:, hb * DH:(hb + 1) * DH], hb == 0, hb == 1)
    phase_end(block, k)

    @block.vector
    def _(dve):
        for half in range(2):
            v.tensor_copy(keysT[half * 64:half * 64 + 64, 0:2 * NC], k.bank[4][0:64, 0:2 * NC])
        v.tensor_copy(values[0:NC, :], k.bank[5][0:NC, 0:2 * DH])
    phase_end(block, k)
    a.at = mark


def nsa(block, k, qT, keysT, valuesT, kc, vc, gates, oT):
    nc, v = k.nc, k.nc.vector
    a = k.arena
    mark = a.at
    S = a.take(HEADS, NT, 2 * TOK)
    C = a.take(HEADS, NT, 16)
    PT = a.take(2, 2, 384)
    CT = a.take(2, TOK)
    stat = lambda tile: tile[:, 0:48].rearrange("p (t h b) -> p t h b", t=NT, h=HEADS)
    mx, tot, rec = stat(k.mx), stat(k.tot), stat(k.rec)
    units = [(h, t) for h in range(HEADS) for t in range(NT)]
    scored, took, maxed = k.flag("scored"), k.flag("score_read"), k.flag("maxed")
    SS = lambda h, t: S[:, h, t, :].rearrange("p (b s) -> p b s", b=2)[:, :, 0:(t + 1) * P]

    @block.tensor
    def _(pe):
        for u, (h, t) in enumerate(units):
            if u >= 2:
                pe.wait_ge(took.sem, took.at(2 * (u - 1)))
            p0, n, g = 64 * (h % 2), (t + 1) * P, h // 4
            q = qT[p0:p0 + 64, h // 2, t * P:(t + 1) * P]
            for b in range(2):
                nc_matmul(k, k.bank[4 + u % 2][:, b * TOK:b * TOK + n], q, keysT[b][p0:p0 + 64, g, 0:n], True, True)
            nc_matmul(k, k.bank[6 + u % 2][:, 0:NC], q, kc[p0:p0 + 64, g * NC:(g + 1) * NC], True,
                      True).then_inc(scored.sem, 1)

    @block.vector
    def _(dve):
        dve.wait_ge(k.bias_landed, 16 * NT * HEADS)
        for u in range(len(units) + 1):
            if u < len(units):
                h, t = units[u]
                n = (t + 1) * P
                dve.wait_ge(scored.sem, scored.at(u + 1))
                v.tensor_tensor(SS(h, t), k.bank[4 + u % 2][:, :].rearrange("p (b s) -> p b s", b=2)[:, :, 0:n],
                                k.bias[:, h, t, 0:n].unsqueeze(1).to_broadcast([P, 2, n]), ALU.add).then_inc(took.sem, 1)
                v.tensor_tensor(C[:, h, t, 0:NC], k.bank[6 + u % 2][:, 0:NC], k.bias[:, h, t, 31:TOK:16],
                                ALU.add).then_inc(took.sem, 1)
            if u >= 1:
                h, t = units[u - 1]
                dve.wait_ge(took.sem, took.at(2 * u))
                v.tensor_reduce(mx[:, t, h, 1:3], SS(h, t), AX.X, ALU.max, negate=True)
                v.tensor_reduce(mx[:, t, h, 0:1], C[:, h, t, 0:NC], AX.X, ALU.max, negate=True).then_inc(maxed.sem, 1)

    @block.scalar
    def _(act):
        for u, (h, t) in enumerate(units):
            act.wait_ge(maxed.sem, maxed.at(u + 1))
            for b in range(3):
                x = C[:, h, t, 0:NC] if b == 0 else SS(h, t)[:, b - 1, :]
                nc.scalar.activation(x, x, ACT.Exp, bias=mx[:, t, h, b:b + 1], accum_out=tot[:, t, h, b:b + 1])
    scored.base += 16
    took.base += 32
    maxed.base += 16
    phase_end(block, k)

    @block.vector
    def _(dve):
        k.dve_steps.did(v.reciprocal(k.rec[:, 0:48], k.tot[:, 0:48]))
        k.dve_steps.settle(dve)
        v.tensor_tensor(k.rec[:, 0:48], k.rec[:, 0:48], gates, ALU.mult)
    phase_end(block, k)
    scaled = [k.flag("scaled_act"), k.flag("scaled_dve")]
    pturned, pread = k.flag("probs_turned"), [k.flag("probs_read_act"), k.flag("probs_read_dve")]
    mixed, yread = k.flag("mixed"), k.flag("mixed_read")
    base = lambda h: 4 * (h % 2)

    def mix(pe, h):
        for s in pread:
            pe.wait_ge(s.sem, s.at(h + 1))
        b = h // 2
        if h % 2 == 0 and b >= 2:
            pe.wait_ge(yread.sem, yread.at(b - 1))
        o = k.bank[3 + 4 * (b % 2)][64 * (h % 2):64 * (h % 2) + 64, 0:TOK]
        g = slice((h // 4) * DH, (h // 4 + 1) * DH)
        for n in range(2):
            nc_matmul(k, o, valuesT[n][:, 0, g], PT[:, h % 2, n, 0:TOK], n == 0, False)
            nc_matmul(k, o[:, P:TOK], valuesT[n][:, 1, g], PT[:, h % 2, n, TOK:384], False, False)
        nc_matmul(k, o, vc[0:NC, g], CT[0:NC, h % 2, :], False, True).then_inc(mixed.sem, 1)

    @block.tensor
    def _(pe):
        for h in range(HEADS):
            for s in scaled:
                pe.wait_ge(s.sem, s.at(h + 1))
            if h >= 2:
                for s in pread:
                    pe.wait_ge(s.sem, s.at(h - 1))
            for n in range(2):
                for i, (t, s) in enumerate(((0, 0), (1, 0), (1, 1))):
                    nc.tensor.transpose(k.bank[base(h) + n][:, i * P:(i + 1) * P],
                                        S[:, h, t, n * TOK + s * P:n * TOK + (s + 1) * P], k.c("ident"))
            for t in range(NT):
                ins = nc.tensor.transpose(k.bank[base(h) + 2][0:NC, t * P:(t + 1) * P], C[:, h, t, 0:NC], k.c("ident"))
            ins.then_inc(pturned.sem, 1)
            if h >= 1:
                mix(pe, h - 1)
        mix(pe, HEADS - 1)

    def out(act, b):
        act.wait_ge(mixed.sem, mixed.at(2 * b + 2))
        nc.scalar.copy(oT[:, b, :], k.bank[3 + 4 * (b % 2)][:, 0:TOK]).then_inc(yread.sem, 1)

    @block.scalar
    def _(act):
        def scale(h):
            for t in range(NT):
                ins = nc.scalar.activation(SS(h, t)[:, 0, :], SS(h, t)[:, 0, :], ACT.Copy, scale=rec[:, t, h, 1:2])
            ins.then_inc(scaled[0].sem, 1)
        scale(0)
        for h in range(HEADS):
            if h + 1 < HEADS:
                scale(h + 1)
            act.wait_ge(pturned.sem, pturned.at(h + 1))
            if h >= 2:
                act.wait_ge(mixed.sem, mixed.at(h - 1))
            nc.scalar.copy(PT[:, h % 2, 0, :], k.bank[base(h)][:, 0:384]).then_inc(pread[0].sem, 1)
            if h % 2 == 1 and h >= 3:
                out(act, h // 2 - 1)
        out(act, NB - 1)

    @block.vector
    def _(dve):
        def scale(h):
            for t in range(NT):
                v.tensor_scalar(SS(h, t)[:, 1, :], SS(h, t)[:, 1, :], rec[:, t, h, 2:3], None, ALU.mult)
                ins = v.scalar_tensor_tensor(C[:, h, t, 0:NC], C[:, h, t, 0:NC], rec[:, t, h, 0:1], k.seen[:, t, :],
                                             ALU.mult, ALU.mult)
            ins.then_inc(scaled[1].sem, 1)
        scale(0)
        for h in range(HEADS):
            if h + 1 < HEADS:
                scale(h + 1)
            dve.wait_ge(pturned.sem, pturned.at(h + 1))
            if h >= 2:
                dve.wait_ge(mixed.sem, mixed.at(h - 1))
            v.tensor_copy(PT[:, h % 2, 1, :], k.bank[base(h) + 1][:, 0:384])
            v.tensor_copy(CT[0:NC, h % 2, :], k.bank[base(h) + 2][0:NC, 0:TOK]).then_inc(pread[1].sem, 1)
    for s, n in ((scaled[0], 8), (scaled[1], 8), (pturned, 8), (pread[0], 8), (pread[1], 8), (mixed, 8), (yread, 4)):
        s.base += n
    phase_end(block, k)
    a.at = mark


def gla(block, k, tok, a, alT, gain, oT, products):
    nc, v = k.nc, k.nc.vector
    steps = k.dve_steps
    mark = a.at
    qT, kT, vb, rb = a.take(GH, TOK), a.take(GH, TOK), a.take(NT, GH * GV), a.take(NT, GH * GV)
    la, ex = k.xn[:, 0, :], k.xn[:, 1, :]
    o = a.take(NT, GH * GV)
    B, ki = (o[:, n, :].rearrange("p (h t) -> p h t", h=GH) for n in range(2))
    qd, ks = a.take(GH, TOK), a.take(GH, TOK)
    kst, AT = a.take(NT, WIDTH), a.take(NT * GH, P)
    S, ends = a.take(2, GH, GV), a.take(GH, NCH)
    big = k.big
    chunks = lambda x: x.rearrange("p h (c t) -> p h c t", c=NCH)
    flat = lambda x: x.rearrange("p b t -> p (b t)")
    decays, logs, log_a = k.flag("decay_done"), k.flag("decay_logs"), k.flag("log_a_ready")
    summed, sums_read, powers = k.flag("running_sums"), k.flag("sums_read"), k.flag("decay_powers")

    def by_channel(dst, scale):
        product(block, k, "channel", 256, 2, moving=k.h_parts, unroll=4,
                act=lambda i, j, ps: nc.scalar.activation(flat(dst[:, 2 * i:2 * i + 2, :]), ps[:, 0, :], ACT.Copy,
                                                          scale=scale))

    def by_token(op, dst):
        return lambda i, j, ps: [op(dst[:, t, i * 512:(i + 1) * 512], ps[:, t, :]) for t in range(NT)][-1]

    @block.tensor
    def _(pe):
        for t in range(NT):
            d = big[2][:, t * WIDTH:(t + 1) * WIDTH]
            nc_matmul(k, d, alT[0:16, t * P:(t + 1) * P], k.a_w2[0:16, :], True, False)
            ins = nc_matmul(k, d, k.c("ones")[0:1, :], k.w0[0:1, :], False, True)
        ins.then_inc(decays.sem, 1)

    @block.scalar
    def _(act):
        act.wait_ge(decays.sem, decays.at(1))
        k.act_steps.did(nc.scalar.activation(ex, big[2], ACT.Abs))
        k.act_steps.settle(act)
        k.act_steps.did(nc.scalar.activation(ex, ex, ACT.Exp, scale=-1.0))
        k.act_steps.settle(act)
        nc.scalar.activation(ex, ex, ACT.Ln, bias=1.0).then_inc(logs.sem, 1)
    by_channel(qT, P ** -0.5)

    @block.vector
    def _(dve):
        dve.wait_ge(logs.sem, logs.at(1))
        v.scalar_tensor_tensor(la, big[2], 0.0, ex, ALU.min, ALU.subtract).then_inc(log_a.sem, 1)
    by_channel(kT, 1.0)

    @block.tensor
    def _(pe):
        pe.wait_ge(log_a.sem, log_a.at(1))
        for h in range(GH):
            for t in range(NT):
                ins = nc_matmul(k, flat4(big[3])[:, h, t * P:(t + 1) * P],
                                la[:, t * WIDTH + h * P:t * WIDTH + (h + 1) * P], k.c("incl_up"), True, True)
        ins.then_inc(summed.sem, 1)
    product(block, k, "token", 512, 2, stationary=tok, dve=by_token(nc.vector.tensor_copy, vb))

    @block.vector
    def _(dve):
        dve.wait_ge(summed.sem, summed.at(1))
        steps.did(v.tensor_copy(B, flat4(big[3])))
        steps.settle(dve)
        last = chunks(B)[:, :, :, CHUNK - 1:CHUNK]
        for h in range(GH):
            ins = v.tensor_tensor(chunks(ks)[:, h], last[:, h].to_broadcast([P, NCH, CHUNK]), chunks(B)[:, h],
                                  ALU.subtract)
        ins.then_inc(sums_read.sem, 1)

    @block.scalar
    def _(act):
        act.wait_ge(sums_read.sem, sums_read.at(1))
        nc.scalar.activation(qd, B, ACT.Exp, scale=1.0 / 16)
        nc.scalar.activation(ki, B, ACT.Exp, scale=-1.0 / 16)
        nc.scalar.activation(ends, B[:, :, CHUNK - 1:TOK:CHUNK], ACT.Exp, scale=1.0 / 16)
        nc.scalar.activation(ks, ks, ACT.Exp, scale=1.0 / 16).then_inc(powers.sem, 1)
    product(block, k, "token", 512, 2, stationary=tok,
            act=by_token(lambda o, i: nc.scalar.activation(o, i, ACT.Silu), rb))

    @block.vector
    def _(dve):
        dve.wait_ge(powers.sem, powers.at(1))
        v.tensor_tensor(qd, qd, qT, ALU.mult)
        v.tensor_tensor(ki, ki, kT, ALU.mult)
        v.tensor_tensor(ks, ks, kT, ALU.mult)
        v.memset(S[:, 0], 0.0)
    for s in (decays, logs, log_a, summed, sums_read, powers):
        s.base += 1
    phase_end(block, k)

    @block.tensor
    def _(pe):
        for n in range(NT * GH):
            h, t = n % GH, slice((n // GH) * P, (n // GH + 1) * P)
            nc_matmul(k, big[1][:, n * P:(n + 1) * P], ki[:, h, t], qd[:, h, t], True, True)
    turn_back(block, k, ks, kst, 4)
    phase_end(block, k)

    @block.vector
    def _(dve):
        v.tensor_tensor(AT, big[1].rearrange("p (n t) -> p n t", t=P),
                        k.c("incl_up").unsqueeze(1).to_broadcast([P, NT * GH, P]), ALU.mult)
    phase_end(block, k)
    kv_done, s_ready, out_done, out_read = (k.flag(n) for n in ("gla_kv_done", "gla_s_ready", "gla_out_done",
                                                                "gla_out_read"))
    where = lambda c: (c // 2, slice(64 * (c % 2), 64 * (c % 2) + 64))
    kv_bank = lambda c: big[1 + 2 * (c % 2)]

    @block.tensor
    def _(pe):
        for c in range(NCH):
            t, rows = where(c)
            if c >= 2:
                pe.wait_ge(s_ready.sem, s_ready.at(c - 1))
            for h in range(GH if c < NCH - 1 else 0):
                ins = nc_matmul(k, kv_bank(c)[:, h * GV:(h + 1) * GV], kst[rows, t, h * P:(h + 1) * P],
                                vb[rows, t, h * GV:(h + 1) * GV], True, True)
            if c < NCH - 1:
                ins.then_inc(kv_done.sem, 1)
            if c >= 1:
                pe.wait_ge(s_ready.sem, s_ready.at(c))
            if c >= 2:
                pe.wait_ge(out_read.sem, out_read.at(c - 1))
            for h in range(GH):
                d = big[0][rows, h * GV:(h + 1) * GV]
                nc_matmul(k, d, qd[:, h, c * CHUNK:(c + 1) * CHUNK], S[:, c % 2, h, :], True, False)
                ins = nc_matmul(k, d, AT[:, t * GH + h, rows], vb[:, t, h * GV:(h + 1) * GV], False, True)
            ins.then_inc(out_done.sem, 1)

    @block.vector
    def _(dve):
        for c in range(NCH - 1):
            dve.wait_ge(kv_done.sem, kv_done.at(c + 1))
            if c >= 1:
                dve.wait_ge(out_done.sem, out_done.at(c))
            if c >= 1:
                dve.wait_ge(s_ready.sem, s_ready.at(c))
            for h in range(GH):
                ins = v.scalar_tensor_tensor(S[:, (c + 1) % 2, h, :], S[:, c % 2, h, :], ends[:, h, c:c + 1],
                                             kv_bank(c)[:, h * GV:(h + 1) * GV], ALU.mult, ALU.add)
            ins.then_inc(s_ready.sem, 1)

    @block.scalar
    def _(act):
        for c in range(NCH):
            t, rows = where(c)
            act.wait_ge(out_done.sem, out_done.at(c + 1))
            nc.scalar.copy(o[rows, t, :], big[0][rows, :]).then_inc(out_read.sem, 1)
    for s, n in ((kv_done, NCH - 1), (s_ready, NCH - 1), (out_done, NCH), (out_read, NCH)):
        s.base += n
    phase_end(block, k)
    ss = k.mx[:, 0:8]
    squared, meaned, rooted, ready = (k.flag(n) for n in ("squared", "meaned", "rooted", "gla_ready"))
    tile = lambda x, t, h: x[:, t, h * GV:(h + 1) * GV]
    sums = lambda t, h: ss[:, t * GH + h:t * GH + h + 1]

    @block.scalar
    def _(act):
        for h in range(GH):
            ins = nc.scalar.activation(tile(k.xn, 0, h), tile(o, 0, h), ACT.Square, accum_out=sums(0, h))
        ins.then_inc(squared.sem, 1)
        act.wait_ge(meaned.sem, meaned.at(1))
        nc.scalar.activation(k.rec[:, 0:8], k.tot[:, 0:8], ACT.Sqrt).then_inc(rooted.sem, 1)

    @block.vector
    def _(dve):
        for h in range(GH):
            steps.did(v.scalar_tensor_tensor(tile(k.xn, 1, h), tile(o, 1, h), 1.0, tile(o, 1, h), ALU.mult, ALU.mult,
                                             accum_out=sums(1, h)))
        steps.settle(dve)
        dve.wait_ge(squared.sem, squared.at(1))
        v.tensor_scalar(k.tot[:, 0:8], ss, 1.0 / GV, RMS_EPS, ALU.mult, ALU.add).then_inc(meaned.sem, 1)
        dve.wait_ge(rooted.sem, rooted.at(1))
        steps.did(v.reciprocal(ss, k.rec[:, 0:8]))
        steps.settle(dve)
        for t in range(NT):
            for h in range(GH):
                steps.did(v.scalar_tensor_tensor(tile(o, t, h), tile(o, t, h), sums(t, h), gain[:, h * GV:(h + 1) * GV],
                                                 ALU.mult, ALU.mult))
        steps.settle(dve)
        for t in range(NT):
            ins = v.tensor_tensor(o[:, t, :], o[:, t, :], rb[:, t, :], ALU.mult)
        ins.then_inc(ready.sem, 1)
    products()

    @block.tensor
    def _(pe):
        pe.wait_ge(ready.sem, ready.at(1))
    turn(block, k, o, NG, oT)
    for s in (squared, meaned, rooted, ready):
        s.base += 1
    phase_end(block, k)
    a.at = mark


def second_layer(block, k, A, l):
    nc = k.nc
    a = k.arena
    a.at = HEADS * NT * TOK
    small = k.flag("small_landed")
    row = lambda name: A[name][bass.ds(l, 1)]
    tok = lambda kt, t, i: parts(kt, t)
    cols = a.take(sum(SECOND_COLS.values()))
    k.col2 = columns(cols, SECOND_COLS)
    out_norm, k.a_w2 = a.take(D), a.take(WIDTH)
    body = a.at
    gain_landed = k.flag("gain_landed")
    parts = lambda kt, t: (k.h_high[:, kt, t * P:(t + 1) * P], k.h_low[:, kt, t * P:(t + 1) * P])

    @block.sync
    def _(sp):
        gain = row("spread2").partition_broadcast(P).rearrange("p a n -> p (a n)")[:, 0:D]
        sp.dma_start(k.spread[:], gain).then_inc(gain_landed.sem, 16)
    stream(block, k, A["stream2"][bass.ds(l, 1)].rearrange("a c p n -> (a c) p n"), 105)

    @block.scalar
    def _(act):
        spread = row("spread2").partition_broadcast(P).rearrange("p a n -> p (a n)")
        for dst, src in ((cols, row("cols2").rearrange("a p n -> (a p) n")),
                         (k.a_w2[0:16, :], row("a_w2").rearrange("a p n -> (a p) n")), (k.w0[0:1, :], row("rows2")),
                         (out_norm, spread[:, 3 * D:4 * D])):
            act.dma_start(dst, src).then_inc(small.sem, 16)
    small.base += 64

    def norm(n):
        @block.vector
        def _(dve):
            dve.wait_ge(gain_landed.sem, 16 * (n + 1))
        rms_norm(block, k, k.spread[:])
        if n < 2:
            @block.scalar
            def _(act):
                act.wait_ge(k.flag("normed").sem, k.flag("normed").base)
                act.dma_start(k.spread[:], row("spread2")[:, (n + 1) * D:(n + 2) * D].partition_broadcast(P).rearrange(
                    "p a n -> p (a n)")).then_inc(gain_landed.sem, 16)

    def feed_forward(n):
        a.at = body
        norm(n)
        if n == 0:
            @block.scalar
            def _(act):
                split_high(act, k, 0, 0)

            @block.vector
            def _(dve):
                split_low(dve, k, 0, 0)
        turn(block, k, k.xn, KD, normed=True)
        phase_end(block, k)
        k.ffn_act = a.take(2, 512)
        ffn(block, k, lambda dve, half, ps: scaled_add(k, half, ps, 0.5))
        phase_end(block, k)
    feed_forward(0)
    a.at = body
    oT, obT = a.take(NB, TOK), a.take(NG, TOK)
    alT = a.take(TOK)
    mixers = a.at
    small_high, small_low = (x[:, :, :].rearrange("p a n -> p (a n)")[:, 0:KD * SMALL].rearrange("p (k n) -> p k n", k=KD)
                             for x in (k.hid_high, k.hid_low))
    w_small = k.col2["w_small"].rearrange("p (k n) -> p k n", k=KD)

    @block.scalar
    def _(act):
        act.wait_ge(small.sem, small.at(0))
        nc.scalar.copy(small_high, w_small)
    norm(1)

    @block.vector
    def _(dve):
        nc.vector.tensor_tensor(small_low, w_small, small_high.bitcast(F32), ALU.subtract)
    turn(block, k, k.xn, KD, normed=True)
    phase_end(block, k)
    qT, pairs, keys, values = a.take(NB, TOK), a.take(2, 2, P), a.take(2, 2, TOK), a.take(2, NT, P)
    gates, kc, vc = a.take(NT * 24), a.take(32), a.take(2 * DH)
    valuesT, gatesT = a.take(2, TOK), a.take(TOK)
    flat = lambda x: x.rearrange("p b t -> p (b t)")
    product(block, k, "channel", 256, 2, moving=k.h_parts, unroll=4,
            act=lambda i, j, ps: nc.scalar.activation(flat(qT[:, 2 * i:2 * i + 2, :]), ps[:, 0, :], ACT.Copy,
                                                      scale=DH ** -0.5))

    def split_pairs(i, j, ps):
        for n in range(2):
            for g in range(2):
                for par in range(2):
                    ins = nc.scalar.copy(pairs[par * 64:par * 64 + 64, n, g, :],
                                         ps[g * 64:g * 64 + 64, 0, n * TOK + par:(n + 1) * TOK:2])
        return ins
    product(block, k, "channel", 256, 1, moving=k.h_parts, act=split_pairs)

    def both_halves(dst):
        def out(i, j, ps):
            for g in range(2):
                for half in range(2):
                    ins = nc.scalar.copy(dst[half * 64:half * 64 + 64, g, :], ps[g * 64:g * 64 + 64, 0, 0:TOK])
            return ins
        return out
    for n in range(2):
        product(block, k, "channel", 256, 1, moving=k.h_parts, act=both_halves(keys[:, n]),
                dve=lambda i, j, ps, n=n: nc.vector.tensor_copy(valuesT[:, n, :], ps[:, 1, 0:TOK]))

    @block.tensor
    def _(pe):
        for kt in range(KD):
            ins = split_product(k, k.bank[4][0:SMALL, 0:TOK], (small_high[:, kt, :], small_low[:, kt, :]), k.h_parts(kt),
                                kt == 0, kt == KD - 1)
    phase_end(block, k)

    @block.tensor
    def _(pe):
        for n in range(2):
            for t in range(NT):
                nc.tensor.transpose(k.bank[5][:, (2 * n + t) * P:(2 * n + t + 1) * P], valuesT[:, n, t * P:(t + 1) * P],
                                    k.c("ident"))

    @block.scalar
    def _(act):
        nc.scalar.activation(gatesT[GATE_AT:SMALL, :], k.bank[4][GATE_AT:SMALL, 0:TOK], ACT.Sigmoid)
        nc.scalar.copy(alT[0:16, :], k.bank[4][0:16, 0:TOK])
    phase_end(block, k)

    @block.tensor
    def _(pe):
        for t in range(NT):
            nc_matmul(k, k.bank[6][:, t * 24:(t + 1) * 24], gatesT[GATE_AT:SMALL, t * P:(t + 1) * P],
                      k.c("ident")[GATE_AT:SMALL, GATE_AT:SMALL], True, True)

    @block.scalar
    def _(act):
        nc.scalar.copy(values.rearrange("p n t d -> p (n t d)"), k.bank[5])
    phase_end(block, k)

    @block.scalar
    def _(act):
        nc.scalar.copy(gates, k.bank[6][:, 0:48])
    compress(block, k, pairs, kc, vc)
    nsa(block, k, qT, [keys[:, 0], keys[:, 1]], [values[:, 0], values[:, 1]], kc, vc, gates, oT)
    a.at = mixers
    token_out = lambda op, dst: (lambda i, j, ps: [op(dst[:, t, i * 512:(i + 1) * 512], ps[:, t, :]) for t in range(NT)][-1])
    gm = a.tile[:, mixers:mixers + NT * 2 * D].rearrange("p (t n) -> p t n", t=NT)

    def gate_products():
        product(block, k, "token", 512, 4, stationary=tok,
                act=token_out_dyn(lambda o, i: nc.scalar.activation(o, i, ACT.Sigmoid), gm))
    a.at = mixers
    gla(block, k, tok, a, alT, out_norm, obT, gate_products)
    merged = [k.flag("merged_dve"), k.flag("merged_pool")]
    mul = lambda o, i: nc.vector.tensor_tensor(o, o, i, ALU.mult)
    operand(block, k, oT, 0, k.chunk)
    operand(block, k, obT[:, 0:4, :], 1, k.chunk)
    product(block, k, "token", 512, 2, ktiles=4, stationary=tok, dve=token_out(mul, gm[:, :, 0:D]))
    operand(block, k, obT[:, 4:8, :], 0, k.chunk)
    product(block, k, "token", 512, 2, stationary=lambda kt, t, i: parts((kt + 4) % 8, t),
            dve=token_out(mul, gm[:, :, D:2 * D]))
    phase_end(block, k)

    @block.vector
    def _(dve):
        nc.vector.tensor_tensor(gm[:, 0, 0:D], gm[:, 0, 0:D], gm[:, 0, D:2 * D], ALU.add).then_inc(merged[0].sem, 1)

    @block.gpsimd
    def _(pool):
        nc.gpsimd.tensor_tensor(gm[:, 1, 0:D], gm[:, 1, 0:D], gm[:, 1, D:2 * D], ALU.add).then_inc(merged[1].sem, 1)
    turn(block, k, gm, KD, ready=merged)
    phase_end(block, k)
    product(block, k, "token", 512, 2, stationary=tok, dve=lambda i, j, ps: scaled_add(k, i, ps, 1.0))
    phase_end(block, k)
    feed_forward(2)
    assert k.chunk == 105, k.chunk


def token_out_dyn(op, dst):
    def out(i, j, ps):
        for t in range(NT):
            ins = op(dst[:, t, bass.ds(i * 512, 512)], ps[:, t, :])
        return ins
    return out


def scaled_add(k, i, ps, factor):
    cols = slice(i * 512, (i + 1) * 512)
    for t in range(NT):
        ins = k.nc.vector.scalar_tensor_tensor(k.x[:, t, cols], ps[:, t, :], factor, k.x[:, t, cols], ALU.mult, ALU.add)
    return ins


def build(nc, A, O, dump=None):
    with ExitStack() as ctx:
        k = Program(nc, ctx)
        square = k.sb("c_square", [P, len(CONSTS) * P])
        rows = k.sb("c_rows", [P, NT, 512 + 64 + NC])
        k.c = lambda name: square[:, CONSTS.index(name) * P:(CONSTS.index(name) + 1) * P]
        k.count, k.blocked = rows[:, :, 0:256], rows[:, :, 256:512]
        k.cos, k.sin, k.seen = rows[:, :, 512:544], rows[:, :, 544:576], rows[:, :, 576:576 + NC]
        k.x = k.sb("x", [P, NT, D])
        k.h_high, k.h_low = k.sb("h_high", [P, KD, TOK], F32R), k.sb("h_low", [P, KD, TOK], F32R)
        k.hid_high, k.hid_low = k.sb("hid_high", [P, 2, 512], F32R), k.sb("hid_low", [P, 2, 512], F32R)
        k.high = [k.sb(f"high{i}", [P, SLOT], F32R) for i in range(SLOTS)]
        k.low = [k.sb(f"low{i}", [P, SLOT], F32R) for i in range(SLOTS)]
        k.h_parts = lambda kt: (k.h_high[:, kt, :], k.h_low[:, kt, :])
        k.slots = [k.sb(f"slot{i}", [P, SLOT]) for i in range(SLOTS)]
        k.stat, k.mx, k.tot, k.rec = k.sb("stat", [P, 8]), k.sb("mx", [P, 64]), k.sb("tot", [P, 64]), k.sb("rec", [P, 64])
        k.cols1 = k.sb("cols1", [P, sum(FIRST_COLS.values())])
        k.col = columns(k.cols1, FIRST_COLS)
        k.w0, k.spread = k.sb("w0", [1, WIDTH]), k.sb("spread", [P, D])
        k.arena = Arena(k.sb("arena", [P, 25200]), 25200)
        k.xn = k.sb("xn", [P, NT, D])
        banks = [ctx.enter_context(nc.psum_tensor(f"pair{i}", [P, 2, 512], F32)) for i in range(4)]
        k.pair, k.acc = banks[0:2], banks[2:4]
        k.big = [b[:].rearrange("p a n -> p (a n)") for b in banks]
        k.bank = [banks[i // 2][:, i % 2, :] for i in range(8)]
        k.lines = nc.dram_tensor("bias_lines", [(P + 1) * HEADS * 512], F32, kind="Internal").ap()
        loaded = ctx.enter_context(nc.semaphore("consts_loaded"))
        k.square_landed = ctx.enter_context(nc.semaphore("square_landed"))
        k.lines_stored = ctx.enter_context(nc.semaphore("lines_stored"))
        k.bias_landed = ctx.enter_context(nc.semaphore("bias_landed"))
        with nc.Block() as block:
            def load_constants(sp):
                sp.dma_start(square[:], A["c_square"]).then_inc(k.square_landed, 16)
                sp.dma_start(rows[:], A["c_rows"]).then_inc(loaded, 16)
                sp.dma_start(k.spread[:], A["norm_final"].partition_broadcast(P).rearrange("p a n -> p (a n)")
                             ).then_inc(loaded, 16)
                sp.dma_start(k.x[:], A["x"].rearrange("a (t p) n -> p (a t) n", p=P)).then_inc(loaded, 16)
            distance_lines(block, k, A, nc, load_constants)

            @block.sync
            def _(sp):
                sp.wait_ge(loaded, 48)
        k.end_layer()
        with nc.Fori(0, DEPTH) as l:
            with nc.Block() as block:
                first_layer(block, k, A, l)
            k.end_layer()
        with nc.Block() as block:
            distance_bias(block, k)
            rms_norm(block, k, k.spread[:])

            @block.vector
            def _(dve):
                dve.wait_ge(k.flag("normed").sem, NT)
                nc.vector.tensor_copy(k.x[:], k.xn[:])
            phase_end(block, k)
        k.end_layer()
        with nc.Fori(0, DEPTH) as l:
            with nc.Block() as block:
                second_layer(block, k, A, l)
            k.end_layer()
        stored = ctx.enter_context(nc.semaphore("stored"))
        with nc.Block() as block:
            small = k.flag("final_norm_landed")

            @block.sync
            def _(sp):
                sp.dma_start(k.spread[:], A["final_norm_2"].partition_broadcast(P).rearrange("p a n -> p (a n)")
                             ).then_inc(small.sem, 16)

            @block.vector
            def _(dve):
                dve.wait_ge(small.sem, 16)
            rms_norm(block, k, k.spread[:])
            phase_end(block, k)

            @block.sync
            def _(sp):
                sp.wait_ge(k.flag("phase_arrived").sem, 4 * k.phase)
                sp.dma_start(O["out"].rearrange("a (t p) n -> p (a t) n", p=P), k.xn[:]).then_inc(stored, 16)
                sp.wait_ge(stored, 16)


def host_arrays(v):
    f = lambda a: np.ascontiguousarray(a)
    out = dict(shape_constants())
    out["x"] = v["x"]
    ada = [v["w_ada"][l].reshape(KD, P, 3, SLOT).transpose(2, 0, 1, 3).reshape(3 * KD, P, SLOT) for l in range(DEPTH)]
    out["ada"] = f(np.stack(ada))
    out["stream1"] = f(np.stack([first_stream(v, l) for l in range(DEPTH)]))
    for name, parts in zip(("cols1", "wide1", "rows1", "spread1"), zip(*[first_small(v, l) for l in range(DEPTH)])):
        out[name] = f(np.stack(parts))
    out["stream2"] = f(np.stack([second_stream(v, l) for l in range(DEPTH)]))
    for name, parts in zip(("cols2", "a_w2", "rows2", "spread2"), zip(*[second_small(v, l) for l in range(DEPTH)])):
        out[name] = f(np.stack(parts))
    out["rel_table"] = v["rel_table_2"]
    out["norm_final"] = v["norm_final"][None]
    out["final_norm_2"] = v["final_norm_2"][None]
    return out


def program(nc, A, out):
    build(nc, A, {"out": out})


def kernel(**inputs):
    import concourse.bacc as _bacc
    from concourse.bass_utils import run_bass_kernel_spmd as _run

    nc = _bacc.Bacc("TRN2", target_bir_lowering=False, num_devices=1)
    arrays = {f"in_{n}": a for n, a in host_arrays({n: np.asarray(a) for n, a in inputs.items()}).items()}
    A = {n[3:]: nc.dram_tensor(n, a.shape, mybir.dt.from_np(a.dtype), kind="ExternalInput").ap() for n, a in arrays.items()}
    out = nc.dram_tensor("out", [1, TOK, D], F32, kind="ExternalOutput").ap()
    program(nc, A, out)
    return _run(nc, [arrays], core_ids=[0]).results[0]["out"]
```
